# Optimizing a Trainium2 kernel written in Bass

```python
import math
import jax, jax.numpy as jnp
from jax import lax
import numpy as np

D_MODEL = 1024
BATCH = 1
SEQ = 2048
DEPTH = 1
DEC_BATCH = 8
DEC_SEQ = 1
PAST_LEN = 4096
PAGE_SIZE = 128

D_MIX = 2 * D_MODEL
D_ATTN = D_MIX // 2
D_SSD = D_MIX - D_ATTN
HEAD_DIM = 64
N_ATTN_HEADS = D_ATTN // HEAD_DIM
PATTERNS = ((128, 1), (512, 4), (2048, 16))
WINDOW_MAX = 2048
BLK = 128
N_BUCKETS = 32
MAX_DISTANCE = WINDOW_MAX
SSD_HEAD_DIM = 64
N_SSD_HEADS = D_SSD // SSD_HEAD_DIM
D_STATE = 128
N_GROUPS = 2
HEADS_PER_GROUP = N_SSD_HEADS // N_GROUPS
CONV_W = 4
CONV_DIM = D_SSD + 2 * N_GROUPS * D_STATE
CHUNK = 128
DT_MIN = 0.001
DT_MAX = 0.1
D_IN_PROJ = 4 * D_ATTN + D_SSD + CONV_DIM + N_SSD_HEADS
EPS = 1e-6

kernel_name = "hybrid_dilated_swa_ssd_step"

def _rmsnorm(x, w):
    xf = x.astype(jnp.float32)
    y = xf * lax.rsqrt(jnp.mean(xf * xf, axis=-1, keepdims=True) + EPS)
    return (y * w.astype(jnp.float32)).astype(x.dtype)

def _t5_bucket(dist):
    max_exact = N_BUCKETS // 2
    d_f = jnp.maximum(dist, 1).astype(jnp.float32)
    large = max_exact + (jnp.log(d_f / max_exact) / math.log(MAX_DISTANCE / max_exact)
                         * (N_BUCKETS - max_exact)).astype(jnp.int32)
    large = jnp.minimum(large, N_BUCKETS - 1)
    return jnp.where(dist < max_exact, dist, large)

def _mixer_inputs(x, norm_w, w_in, q_norm_w, k_norm_w):
    h = _rmsnorm(x, norm_w)
    proj = h @ w_in
    cuts = [D_ATTN, 2 * D_ATTN, 3 * D_ATTN, 4 * D_ATTN, 4 * D_ATTN + D_SSD,
            4 * D_ATTN + D_SSD + CONV_DIM]
    q, k, v, g, z, xbc, dt_raw = jnp.split(proj, cuts, axis=-1)
    heads = x.shape[:-1] + (N_ATTN_HEADS, HEAD_DIM)
    q = _rmsnorm(q.reshape(heads), q_norm_w)
    k = _rmsnorm(k.reshape(heads), k_norm_w)
    return q, k, v.reshape(heads), g, z, xbc, dt_raw

def _mixer_output(x, o_attn, g, y_ssd, z, ssd_norm_w, w_out):
    lead = x.shape[:-1]
    a = o_attn.reshape(lead + (D_ATTN,)).astype(jnp.float32) * jax.nn.silu(g.astype(jnp.float32))
    s = _rmsnorm(y_ssd.reshape(lead + (D_SSD,)).astype(jnp.float32)
                 * jax.nn.silu(z.astype(jnp.float32)), ssd_norm_w)
    mixed = jnp.concatenate([a, s], axis=-1).astype(x.dtype)
    return x + mixed @ w_out

def _merge(outs, lses):
    wts = jax.nn.softmax(jnp.stack(lses, axis=0), axis=0)
    o = jnp.sum(wts[..., None] * jnp.stack(outs, axis=0).astype(jnp.float32), axis=0)
    return o.astype(outs[0].dtype)

def _to_residue(a, d):
    b, s = a.shape[:2]
    L = s // d
    a = a.reshape((b, L, d) + a.shape[2:])
    a = jnp.moveaxis(a, 2, 1).reshape((b * d, L) + a.shape[3:])
    lp = -(-L // BLK) * BLK
    return jnp.pad(a, [(0, 0), (0, lp - L)] + [(0, 0)] * (a.ndim - 2))

def _from_residue(a, b, d, L):
    a = a[:, :L].reshape((b, d, L) + a.shape[2:])
    a = jnp.moveaxis(a, 1, 2)
    return a.reshape((b, L * d) + a.shape[3:])

def _band_attn(q, k, v, win_sub, dil, rel_bias):
    n, lp, h, dh = q.shape
    nb = lp // BLK
    qb = q.reshape(n, nb, BLK, h, dh)

    def ext(a):
        a = a.reshape(n, nb, BLK, h, dh)
        prev = jnp.concatenate([jnp.zeros_like(a[:, :1]), a[:, :-1]], axis=1)
        return jnp.concatenate([prev, a], axis=2)

    kx, vx = ext(k), ext(v)
    rel = jnp.arange(BLK)[:, None] + BLK - jnp.arange(2 * BLK)[None, :]
    band = (rel >= 0) & (rel <= win_sub)
    bias = jnp.moveaxis(rel_bias[_t5_bucket(jnp.maximum(rel, 0) * dil)], -1, 0).astype(jnp.float32)
    not_first = jnp.arange(2 * BLK) >= BLK
    scale = HEAD_DIM ** -0.5

    def one_block(args):
        qi, ki, vi, bi = args
        s = jnp.einsum('nqhd,nkhd->nhqk', qi, ki).astype(jnp.float32) * scale + bias
        valid = band & ((bi > 0) | not_first)[None, :]
        s = jnp.where(valid, s, -jnp.inf)
        lse = jax.nn.logsumexp(s, axis=-1)
        p = jnp.exp(s - lse[..., None]).astype(vi.dtype)
        o = jnp.einsum('nhqk,nkhd->nqhd', p, vi)
        return o, jnp.moveaxis(lse, 1, 2)

    o, lse = lax.map(one_block, (jnp.moveaxis(qb, 1, 0), jnp.moveaxis(kx, 1, 0),
                                 jnp.moveaxis(vx, 1, 0), jnp.arange(nb)))
    o = jnp.moveaxis(o, 0, 1).reshape(n, lp, h, dh)
    lse = jnp.moveaxis(lse, 0, 1).reshape(n, lp, h)
    return o, lse

def _dilated_attn_prompt(q, k, v, rel_bias):
    b, s = q.shape[:2]
    outs, lses = [], []
    for w, d in PATTERNS:
        L = s // d
        o, lse = _band_attn(_to_residue(q, d), _to_residue(k, d), _to_residue(v, d),
                            w // d, d, rel_bias)
        outs.append(_from_residue(o, b, d, L))
        lses.append(_from_residue(lse, b, d, L))
    return _merge(outs, lses)

def _dilated_attn_sample(q, k_all, v_all, n_past, rel_bias):
    t = q.shape[1]
    j = jnp.arange(t)
    scale = HEAD_DIM ** -0.5
    outs, lses = [], []
    for w, d in PATTERNS:
        kk = jnp.arange(w // d + 1)
        idx = n_past + j[:, None] - kk[None, :] * d
        valid = idx >= 0
        idx = jnp.maximum(idx, 0)
        kg, vg = k_all[:, idx], v_all[:, idx]
        bias = rel_bias[_t5_bucket(kk * d)].T.astype(jnp.float32)
        s = jnp.einsum('bthd,btkhd->bhtk', q, kg).astype(jnp.float32) * scale + bias[None, :, None, :]
        s = jnp.where(valid, s, -jnp.inf)
        lse = jax.nn.logsumexp(s, axis=-1)
        p = jnp.exp(s - lse[..., None]).astype(vg.dtype)
        outs.append(jnp.einsum('bhtk,btkhd->bthd', p, vg))
        lses.append(jnp.moveaxis(lse, 1, 2))
    return _merge(outs, lses)

def _conv_silu(xpad, conv_w, conv_b, t):
    y = conv_b + sum(xpad[:, i:i + t] * conv_w[i] for i in range(CONV_W))
    return jax.nn.silu(y)

def _ssd_split(xc, dt_raw, dt_bias, a_log):
    lead = xc.shape[:-1]
    gn = N_GROUPS * D_STATE
    xs = xc[..., :D_SSD].reshape(lead + (N_GROUPS, HEADS_PER_GROUP, SSD_HEAD_DIM))
    bm = xc[..., D_SSD:D_SSD + gn].reshape(lead + (N_GROUPS, D_STATE)).astype(jnp.float32)
    cm = xc[..., D_SSD + gn:].reshape(lead + (N_GROUPS, D_STATE)).astype(jnp.float32)
    dt = jax.nn.softplus(dt_raw.astype(jnp.float32) + dt_bias.astype(jnp.float32))
    dt = dt.reshape(lead + (N_GROUPS, HEADS_PER_GROUP))
    a = -jnp.exp(a_log.astype(jnp.float32)).reshape(N_GROUPS, HEADS_PER_GROUP)
    return xs, bm, cm, dt, a

def _ssd_chunked(xs, dt, a, bm, cm):
    b, s = xs.shape[:2]
    nc = s // CHUNK
    xdt = (xs.astype(jnp.float32) * dt[..., None]).reshape(b, nc, CHUNK, N_GROUPS, HEADS_PER_GROUP, SSD_HEAD_DIM)
    la = (dt * a).reshape(b, nc, CHUNK, N_GROUPS, HEADS_PER_GROUP)
    bc = bm.reshape(b, nc, CHUNK, N_GROUPS, D_STATE)
    cc = cm.reshape(b, nc, CHUNK, N_GROUPS, D_STATE)
    a_cs = jnp.cumsum(la, axis=2)
    causal = jnp.tril(jnp.ones((CHUNK, CHUNK), bool))[:, :, None, None]
    seg = a_cs[:, :, :, None] - a_cs[:, :, None, :]
    lmat = jnp.exp(jnp.where(causal, seg, -jnp.inf))
    cb = jnp.einsum('bclgn,bcsgn->bclsg', cc, bc)
    y_diag = jnp.einsum('bclsg,bclsgr,bcsgrp->bclgrp', cb, lmat, xdt)
    decay_to_end = jnp.exp(a_cs[:, :, -1:] - a_cs)
    states = jnp.einsum('bclgn,bclgr,bclgrp->bcgrpn', bc, decay_to_end, xdt)
    chunk_decay = jnp.exp(a_cs[:, :, -1])

    def step(h, inp):
        st, dec = inp
        return h * dec[..., None, None] + st, h

    h0 = jnp.zeros((b, N_GROUPS, HEADS_PER_GROUP, SSD_HEAD_DIM, D_STATE), jnp.float32)
    h_fin, h_prev = lax.scan(step, h0, (jnp.moveaxis(states, 1, 0), jnp.moveaxis(chunk_decay, 1, 0)))
    h_prev = jnp.moveaxis(h_prev, 0, 1)
    y_off = jnp.einsum('bclgn,bcgrpn,bclgr->bclgrp', cc, h_prev, jnp.exp(a_cs))
    y = (y_diag + y_off).reshape(b, s, N_GROUPS, HEADS_PER_GROUP, SSD_HEAD_DIM)
    return y, h_fin

def _ssd_recurrent(xs, dt, a, bm, cm, h0):
    def step(h, inp):
        xt, dtt, bt, ct = inp
        h = h * jnp.exp(dtt * a)[..., None, None] + jnp.einsum(
            'bgrp,bgn->bgrpn', xt.astype(jnp.float32) * dtt[..., None], bt)
        return h, jnp.einsum('bgrpn,bgn->bgrp', h, ct)

    h, ys = lax.scan(step, h0, (jnp.moveaxis(xs, 1, 0), jnp.moveaxis(dt, 1, 0),
                                jnp.moveaxis(bm, 1, 0), jnp.moveaxis(cm, 1, 0)))
    return jnp.moveaxis(ys, 0, 1), h

def _prompt_layer(x, norm_w, w_in, q_norm_w, k_norm_w, rel_bias, conv_w, conv_b,
                  dt_bias, a_log, d_skip, ssd_norm_w, w_out):
    b, s = x.shape[:2]
    q, k, v, g, z, xbc, dt_raw = _mixer_inputs(x, norm_w, w_in, q_norm_w, k_norm_w)
    o = _dilated_attn_prompt(q, k, v, rel_bias)
    xc = _conv_silu(jnp.pad(xbc, ((0, 0), (CONV_W - 1, 0), (0, 0))), conv_w, conv_b, s)
    xs, bm, cm, dt, a = _ssd_split(xc, dt_raw, dt_bias, a_log)
    y, h = _ssd_chunked(xs, dt, a, bm, cm)
    y = y + d_skip.astype(jnp.float32).reshape(N_GROUPS, HEADS_PER_GROUP)[..., None] * xs.astype(jnp.float32)
    out = _mixer_output(x, o, g, y, z, ssd_norm_w, w_out)
    nw = min(WINDOW_MAX, s)
    new = (k[:, s - nw:], v[:, s - nw:], xbc[:, s - (CONV_W - 1):],
           h.reshape(b, N_SSD_HEADS, SSD_HEAD_DIM, D_STATE).astype(x.dtype))
    return out, new

def _sample_layer(x, win_k, win_v, conv_state, ssm_state, norm_w, w_in, q_norm_w, k_norm_w,
                  rel_bias, conv_w, conv_b, dt_bias, a_log, d_skip, ssd_norm_w, w_out):
    b, t = x.shape[:2]
    q, k, v, g, z, xbc, dt_raw = _mixer_inputs(x, norm_w, w_in, q_norm_w, k_norm_w)
    k_all = jnp.concatenate([win_k.astype(k.dtype), k], axis=1)
    v_all = jnp.concatenate([win_v.astype(v.dtype), v], axis=1)
    o = _dilated_attn_sample(q, k_all, v_all, win_k.shape[1], rel_bias)
    xcat = jnp.concatenate([conv_state.astype(xbc.dtype), xbc], axis=1)
    xc = _conv_silu(xcat, conv_w, conv_b, t)
    xs, bm, cm, dt, a = _ssd_split(xc, dt_raw, dt_bias, a_log)
    h0 = ssm_state.reshape(b, N_GROUPS, HEADS_PER_GROUP, SSD_HEAD_DIM, D_STATE).astype(jnp.float32)
    y, h = _ssd_recurrent(xs, dt, a, bm, cm, h0)
    y = y + d_skip.astype(jnp.float32).reshape(N_GROUPS, HEADS_PER_GROUP)[..., None] * xs.astype(jnp.float32)
    out = _mixer_output(x, o, g, y, z, ssd_norm_w, w_out)
    new = (k, v, xcat[:, -(CONV_W - 1):],
           h.reshape(b, N_SSD_HEADS, SSD_HEAD_DIM, D_STATE).astype(x.dtype))
    return out, new

def setup_inputs(seed: int = 0) -> dict:
    key = jax.random.key(seed)
    ks = jax.random.split(key, 18)
    f32 = jnp.float32
    win_buf = min(WINDOW_MAX, PAST_LEN)

    def gain(k, n):
        return 1.0 + 0.02 * jax.random.normal(k, (DEPTH, n), f32)

    u = jax.random.uniform(ks[10], (DEPTH, N_SSD_HEADS), f32)
    dt0 = jnp.exp(u * (math.log(DT_MAX) - math.log(DT_MIN)) + math.log(DT_MIN))
    dt_bias = dt0 + jnp.log(-jnp.expm1(-dt0))
    return {
        "x_prompt": jax.random.normal(ks[0], (BATCH, SEQ, D_MODEL), f32),
        "x_sample": jax.random.normal(ks[1], (DEC_BATCH, DEC_SEQ, D_MODEL), f32),
        "cache_win_k": jax.random.normal(ks[2], (DEPTH, DEC_BATCH, win_buf, N_ATTN_HEADS, HEAD_DIM), f32),
        "cache_win_v": jax.random.normal(ks[3], (DEPTH, DEC_BATCH, win_buf, N_ATTN_HEADS, HEAD_DIM), f32),
        "state_conv": jax.random.normal(ks[4], (DEPTH, DEC_BATCH, CONV_W - 1, CONV_DIM), f32),
        "state_ssm": 0.5 * jax.random.normal(ks[5], (DEPTH, DEC_BATCH, N_SSD_HEADS, SSD_HEAD_DIM, D_STATE), f32),
        "norm_w": gain(ks[6], D_MODEL),
        "w_in": jax.random.normal(ks[7], (DEPTH, D_MODEL, D_IN_PROJ), f32) * D_MODEL ** -0.5,
        "q_norm_w": gain(ks[8], HEAD_DIM),
        "k_norm_w": gain(ks[9], HEAD_DIM),
        "rel_bias": 0.5 * jax.random.normal(ks[11], (N_BUCKETS, N_ATTN_HEADS), f32),
        "conv_w": jax.random.normal(ks[12], (DEPTH, CONV_W, CONV_DIM), f32) * CONV_W ** -0.5,
        "conv_b": 0.01 * jax.random.normal(ks[13], (DEPTH, CONV_DIM), f32),
        "dt_bias": dt_bias,
        "a_log": jnp.log(jax.random.uniform(ks[14], (DEPTH, N_SSD_HEADS), f32, 1.0, 16.0)),
        "d_skip": gain(ks[15], N_SSD_HEADS),
        "ssd_norm_w": gain(ks[16], D_SSD),
        "w_out": jax.random.normal(ks[17], (DEPTH, D_MIX, D_MODEL), f32) * D_MIX ** -0.5,
    }

def reference(x_prompt, x_sample, cache_win_k, cache_win_v, state_conv, state_ssm,
              norm_w, w_in, q_norm_w, k_norm_w, rel_bias, conv_w, conv_b, dt_bias,
              a_log, d_skip, ssd_norm_w, w_out):
    y_p, y_s = x_prompt, x_sample
    new_p, new_s = [], []
    for l in range(DEPTH):
        lw = (norm_w[l], w_in[l], q_norm_w[l], k_norm_w[l], rel_bias, conv_w[l], conv_b[l],
              dt_bias[l], a_log[l], d_skip[l], ssd_norm_w[l], w_out[l])
        y_p, st_p = _prompt_layer(y_p, *lw)
        y_s, st_s = _sample_layer(y_s, cache_win_k[l], cache_win_v[l], state_conv[l], state_ssm[l], *lw)
        new_p.append(st_p)
        new_s.append(st_s)
    kp, vp, cp, hp = (jnp.stack(a) for a in zip(*new_p))
    k_s, v_s, c_s, h_s = (jnp.stack(a) for a in zip(*new_s))
    return (y_p, y_s, kp, vp, cp, hp, k_s, v_s, c_s, h_s)


_drawn_inputs = setup_inputs


def setup_inputs(seed=0):
    import zlib

    import numpy as np

    out = dict(_drawn_inputs(seed))
    spreads = {}
    factors = {'q_norm_w': 8.0, 'rel_bias': 2.922, 'conv_b': 3.1, 'd_skip': 8.0, 'ssd_norm_w': 4.983}
    for name, (base, spread) in spreads.items():
        noise = np.random.default_rng([zlib.crc32(name.encode()), seed]).standard_normal(out[name].shape)
        drawn = base * np.exp(spread * noise) if base else spread * noise
        out[name] = __import__('jax').numpy.asarray(drawn.astype(out[name].dtype))
    for name, factor in factors.items():
        out[name] = (out[name] * factor).astype(out[name].dtype)
    return out
```

```python
import math
from contextlib import ExitStack

import numpy as np
import concourse.bass as bass
from concourse import mybir

F32 = mybir.dt.float32
F32R = mybir.dt.float32r
ALU = mybir.AluOpType
ACTF = mybir.ActivationFunctionType
AX = mybir.AxisListType

P = 128
D = 1024
SEQ = 2048
NB = 8
TOK = SEQ + NB
TILES = SEQ // P
KT = D // P
H = 16
HD = 64
NST = 128
CONV = 1536
TAPS = 4
WIN = 2048
EPS = 1e-6
BUCKETS = 32
DILATIONS = (1, 4, 16)
MASKED = -1e30
Q0, K0, V0, Z0, G0, C0, DT0 = 0, D, 2 * D, 3 * D, 4 * D, 5 * D, 5 * D + CONV
NPROJ = DT0 + H
SLAB = 256
SHIFTS = 3 * P
BIAS_AT = ((0, 2 * P), (2 * P, 2 * P), (4 * P, P))
BIAS_W = 5 * P
RING = 4


def with_axes(ap, axes, offset=0):
    return bass.AP(tensor=ap.tensor, offset=ap.offset + offset, ap=[list(ap.ap[0])] + [list(a) for a in axes])


def spread(ap, n):
    return bass.AP(tensor=ap.tensor, offset=ap.offset, ap=[list(a) for a in ap.ap] + [[0, n]])


def repeat(ap, n):
    return bass.AP(tensor=ap.tensor, offset=ap.offset, ap=[list(ap.ap[0]), [0, n]] + [list(a) for a in ap.ap[1:]])


def rows_of(ap, n):
    return bass.AP(tensor=ap.tensor, offset=ap.offset, ap=[[0, n]] + [list(a) for a in ap.ap])


class Chain:

    def __init__(self, engine, done):
        self.engine, self.done, self.base, self.count = engine, done, 0, 0

    def __call__(self, instruction):
        self.count += 1
        instruction.then_inc(self.done, 1)
        self.engine.wait_ge(self.done, self.base + self.count)


def project(nc, io, scr):
    with ExitStack() as outer:
        def sb(ctx, name, shape, dt=F32):
            return ctx.enter_context(nc.sbuf_tensor(name, shape, dt))

        hT_hi = sb(outer, "hT_hi", [P, KT, TOK], F32R)
        hT_lo = sb(outer, "hT_lo", [P, KT, TOK], F32R)

        with ExitStack() as ctx:
            xin = sb(ctx, "xin", [P, 2, D])
            hn = sb(ctx, "hn", [P, 2, D])
            norm_b = sb(ctx, "norm_b", [P, D])
            ident = sb(ctx, "ident_p", [P, P])
            ss = sb(ctx, "ss", [P, 2])
            ms = sb(ctx, "ms", [P, 2])
            rstd = sb(ctx, "rstd", [P, 2])
            mhalf = sb(ctx, "mhalf", [P, 1])
            hp = [ctx.enter_context(nc.psum_tensor(f"hp{b}", [P, KT, P], F32)) for b in range(2)]
            sem = lambda n: nc.alloc_semaphore(n)
            x_loaded = [sem(f"x_loaded{b}") for b in range(2)]
            const_loaded = sem("const_loaded")
            mhalf_set = sem("mhalf_set")
            squared, meaned, rooted, normed = sem("squared"), sem("meaned"), sem("rooted"), sem("normed")
            transposed, hi_done, lo_done = sem("transposed"), sem("hi_done"), sem("lo_done")
            block = ctx.enter_context(nc.Block())
            n_tiles = TILES + 1

            @block.sync
            def _(sp):
                sp.dma_start(norm_b[:, :], rows_of(io["norm_w"], P)).then_inc(const_loaded, 16)
                sp.dma_start(ident[:, :], io["ident"]).then_inc(const_loaded, 16)
                for t in range(2):
                    sp.dma_start(xin[:, t, :], io["x_all"][t * P:(t + 1) * P, :]).then_inc(x_loaded[t], 16)
                with sp.Fori(1, TILES // 2) as j:
                    for b in range(2):
                        sp.wait_ge(normed, 2 * j + b - 1)
                        sp.dma_start(xin[:, b, :], io["x_all"][bass.ds((2 * j + b) * P, P), :]).then_inc(x_loaded[b], 16)
                sp.wait_ge(normed, TILES - 1)
                sp.dma_start(xin[0:NB, 0, :], io["x_all"][SEQ:TOK, :]).then_inc(x_loaded[0], 16)

            @block.scalar
            def _(act):
                def tile(j, b, rows, first):
                    act.wait_ge(x_loaded[b], 16 * (j + 1))
                    if not first:
                        act.wait_ge(transposed, 2 * j + b - 1)
                    act.activation(hn[0:rows, b, :], xin[0:rows, b, :], ACTF.Square,
                                   accum_out=ss[0:rows, b:b + 1]).then_inc(squared, 1)

                def take_hi(j, b, rows):
                    act.wait_ge(transposed, 2 * j + b + 1)
                    act.copy(hT_hi[:, :, bass.ds((2 * j + b) * P, rows)], hp[b][:, :, 0:rows]).then_inc(hi_done, 1)

                for b in range(2):
                    tile(0, b, P, True)
                for b in range(2):
                    take_hi(0, b, P)
                with act.Fori(1, TILES // 2) as j:
                    for b in range(2):
                        tile(j, b, P, False)
                        take_hi(j, b, P)
                tile(TILES // 2, 0, NB, False)
                take_hi(TILES // 2, 0, NB)

            @block.gpsimd
            def _(pool):
                pool.memset(mhalf[:, :], -0.5).then_inc(mhalf_set, 1)
                pool.wait_ge(mhalf_set, 1)

                def root(n, b, rows):
                    pool.wait_ge(meaned, n + 1)
                    pool.tensor_tensor(rstd[0:rows, b:b + 1], ms[0:rows, b:b + 1], mhalf[0:rows, :], ALU.pow).then_inc(rooted, 1)

                with pool.Fori(0, TILES // 2) as j:
                    for b in range(2):
                        root(2 * j + b, b, P)
                root(TILES, 0, NB)

            @block.vector
            def _(dve):
                def scale(n, b, rows):
                    dve.wait_ge(squared, n + 1)
                    dve.tensor_scalar(ms[0:rows, b:b + 1], ss[0:rows, b:b + 1], 1.0 / D, EPS, ALU.mult, ALU.add).then_inc(meaned, 1)
                    dve.wait_ge(rooted, n + 1)
                    dve.scalar_tensor_tensor(out=hn[0:rows, b, :], in0=xin[0:rows, b, :], scalar=rstd[0:rows, b:b + 1],
                                             in1=norm_b[0:rows, :], op0=ALU.mult, op1=ALU.mult).then_inc(normed, 1)

                def take_lo(n, b, rows):
                    dve.wait_ge(hi_done, n + 1)
                    part = hT_hi[:, :, bass.ds(n * P, rows)]
                    dve.tensor_tensor(hT_lo[:, :, bass.ds(n * P, rows)], hp[b][:, :, 0:rows], part.bitcast(F32),
                                      ALU.subtract).then_inc(lo_done, 1)

                dve.wait_ge(const_loaded, 32)
                for b in range(2):
                    scale(b, b, P)
                for b in range(2):
                    take_lo(b, b, P)
                with dve.Fori(1, TILES // 2) as j:
                    for b in range(2):
                        scale(2 * j + b, b, P)
                        take_lo(2 * j + b, b, P)
                scale(TILES, 0, NB)
                take_lo(TILES, 0, NB)

            @block.tensor
            def _(pe):
                def turn(n, b, rows, first):
                    pe.wait_ge(normed, n + 1)
                    if not first:
                        pe.wait_ge(lo_done, n - 1)
                    for k in range(KT):
                        last = pe.transpose(hp[b][:, k, 0:rows], hn[0:rows, b, k * P:(k + 1) * P], ident[0:rows, 0:rows])
                    last.then_inc(transposed, 1)

                pe.wait_ge(const_loaded, 32)
                for b in range(2):
                    turn(b, b, P, True)
                with pe.Fori(1, TILES // 2) as j:
                    for b in range(2):
                        turn(2 * j + b, b, P, False)
                turn(TILES, 0, NB, False)

        with ExitStack() as ctx:
            w_raw = sb(ctx, "w_raw", [P, 2, KT, SLAB])
            w_hi = sb(ctx, "w_hi", [P, 2, KT, SLAB], F32R)
            w_lo = sb(ctx, "w_lo", [P, 2, KT, SLAB], F32R)
            stage = sb(ctx, "stage", [P, RING, SLAB])
            stage_s = sb(ctx, "stage_s", [P, SLAB])
            squares = sb(ctx, "squares", [P, SLAB])
            scaled = sb(ctx, "scaled", [P, SLAB])
            ssq = sb(ctx, "ssq", [P, 4])
            msq = sb(ctx, "msq", [P, 4])
            rsq = sb(ctx, "rsq", [P, 4])
            mhalf = sb(ctx, "mhalf4", [P, 4])
            zero = sb(ctx, "zero", [P, 1])
            qkw = sb(ctx, "qkw", [P, 2, HD])
            banks = [ctx.enter_context(nc.psum_tensor(f"bank{r}", [P, 512], F32)) for r in range(RING)]
            bank_s = ctx.enter_context(nc.psum_tensor("bank_s", [P, SLAB], F32))
            xc_in = sb(ctx, "xc_in", [P, TAPS - 1 + SEQ])
            xc = sb(ctx, "xc", [P, SEQ])
            cw = sb(ctx, "cw", [P, CONV // P, TAPS])
            cb = sb(ctx, "cb", [P, CONV // P])
            sem = lambda n: nc.alloc_semaphore(n)
            w_loaded = [sem(f"w_loaded{b}") for b in range(2)]
            small_loaded = sem("small_loaded")
            w_high = sem("w_high")
            w_split = sem("w_split")
            mm_done = sem("mm_done")
            norm_free = sem("norm_free")
            bank_free = sem("bank_free")
            s_done = sem("s_done")
            s_free = sem("s_free")
            s_staged = sem("s_staged")
            s_stored = sem("s_stored")
            q_sq, q_sum, q_root = sem("q_sq"), sem("q_sum"), sem("q_root")
            q_own = sem("q_own")
            staged = sem("staged")
            stored = [sem(f"stored{r}") for r in range(RING)]
            mhalf_set = sem("mhalf4_set")
            conv_step = sem("conv_step")
            conv_sum = sem("conv_sum")
            conv_act = sem("conv_act")
            raw_stored = sem("raw_stored")
            xc_stored = sem("xc_stored")
            pad_set = sem("pad_set")
            block = ctx.enter_context(nc.Block())

            TOK_SLABS = G0 // SLAB
            CH_SLABS = (DT0 - G0) // SLAB
            PER = TILES
            GROUPS = SEQ // 512
            CPER = 2 * GROUPS
            ALL_TOK = TOK_SLABS * PER
            NORM = 2 * D // SLAB * PER
            G_TILES = D // P
            ALL = ALL_TOK + CH_SLABS * CPER
            N_SLABS = TOK_SLABS + CH_SLABS
            w_cols = io["w_in"].rearrange("(k p) n -> p k n", p=P)

            @block.gpsimd
            def _(pool):
                def load(s, b, width=SLAB):
                    pool.dma_start(w_raw[:, b, :, 0:width], w_cols[:, :, bass.ds(s * SLAB, width)]).then_inc(w_loaded[b], 16)

                def split(s, b, width=SLAB):
                    pool.tensor_tensor(w_hi[:, b, :, 0:width], w_raw[:, b, :, 0:width], with_axes(zero[:, :], [[0, KT], [0, width]]),
                                       ALU.add).then_inc(w_high, 1)
                    pool.wait_ge(w_high, s + 1)
                    pool.tensor_tensor(w_lo[:, b, :, 0:width], w_raw[:, b, :, 0:width], w_hi[:, b, :, 0:width].bitcast(F32),
                                       ALU.subtract).then_inc(w_split, 1)
                    pool.wait_ge(w_split, s + 1)

                pool.memset(mhalf[:, :], -0.5).then_inc(mhalf_set, 1)
                pool.memset(zero[:, :], 0.0).then_inc(mhalf_set, 1)
                pool.wait_ge(mhalf_set, 2)
                load(0, 0)
                load(1, 1)
                for b in range(2):
                    pool.wait_ge(w_loaded[b], 16)
                    split(b, b)
                    load(2 + b, b)

                def norm_split(first_slab):
                    with pool.Fori(0, 2) as j:
                        for b in range(2):
                            s = first_slab + 2 * j + b
                            with pool.Fori(0, PER) as t:
                                pool.wait_ge(q_sum, s * PER + t + 1)
                                pool.tensor_tensor(rsq[:, :], msq[:, :], mhalf[:, :], ALU.pow).then_inc(q_root, 1)
                            pool.wait_ge(s_done, s + 1)
                            pool.wait_ge(w_loaded[b], 16 * (first_slab // 2 + j + 2))
                            split(s + 2, b)
                            load(s + 4, b)

                norm_split(0)
                norm_split(4)
                last = N_SLABS // 2 - 2
                with pool.Fori(4, last) as j:
                    for b in range(2):
                        pool.wait_ge(s_done, 2 * j + b + 1)
                        pool.wait_ge(w_loaded[b], 16 * (j + 2))
                        split(2 * j + b + 2, b)
                        load(2 * j + b + 4, b)
                for b in range(2):
                    s = 2 * last + b
                    pool.wait_ge(s_done, s + 1)
                    pool.wait_ge(w_loaded[b], 16 * (last + 2))
                    split(s + 2, b)
                    if b == 0:
                        load(N_SLABS, 0, H)
                pool.wait_ge(s_done, N_SLABS - 1)
                pool.wait_ge(w_loaded[0], 16 * (N_SLABS // 2 + 1))
                split(N_SLABS, 0, H)

            @block.tensor
            def _(pe):
                def product(out, lhs_hi, lhs_lo, rhs_hi, rhs_lo):
                    for k in range(KT):
                        pe.matmul(out, lhs_hi(k), rhs_hi(k), start=k == 0, stop=False)
                        pe.matmul(out, lhs_hi(k), rhs_lo(k), start=False, stop=False)
                        last = pe.matmul(out, lhs_lo(k), rhs_hi(k), start=False, stop=k == KT - 1)
                    return last

                def sample_rows(s, b, width=SLAB):
                    pe.wait_ge(s_free, s + 1)
                    return product(bank_s[0:NB, 0:width],
                                   lambda k: hT_hi[:, k, SEQ:TOK], lambda k: hT_lo[:, k, SEQ:TOK],
                                   lambda k: w_hi[:, b, k, 0:width], lambda k: w_lo[:, b, k, 0:width])

                def token_slab(s, b, free, before):
                    pe.wait_ge(w_split, s + 1)
                    for t in range(TILES):
                        pe.wait_ge(free, s * PER + t + 1 - before)
                        product(banks[t % RING][:, 0:SLAB],
                                lambda k: hT_hi[:, k, t * P:(t + 1) * P], lambda k: hT_lo[:, k, t * P:(t + 1) * P],
                                lambda k: w_hi[:, b, k, :], lambda k: w_lo[:, b, k, :]).then_inc(mm_done, 1)
                    sample_rows(s, b).then_inc(s_done, 1)

                with pe.Fori(0, NORM // PER // 2) as j:
                    for b in range(2):
                        token_slab(2 * j + b, b, norm_free, 0)
                pe.wait_ge(norm_free, RING + NORM)
                with pe.Fori(NORM // PER // 2, TOK_SLABS // 2) as j:
                    for b in range(2):
                        token_slab(2 * j + b, b, bank_free, NORM)
                with pe.Fori(0, CH_SLABS // 2) as j:
                    for b in range(2):
                        s = TOK_SLABS + 2 * j + b
                        pe.wait_ge(w_split, s + 1)
                        for m in range(CPER):
                            c, g = m // GROUPS, m % GROUPS
                            pe.wait_ge(bank_free, ALL_TOK - NORM + (2 * j + b) * CPER + m + 1)
                            product(banks[m % RING][:, :],
                                    lambda k: w_hi[:, b, k, c * P:(c + 1) * P], lambda k: w_lo[:, b, k, c * P:(c + 1) * P],
                                    lambda k: hT_hi[:, k, g * 512:(g + 1) * 512],
                                    lambda k: hT_lo[:, k, g * 512:(g + 1) * 512]).then_inc(mm_done, 1)
                        sample_rows(s, b).then_inc(s_done, 1)
                pe.wait_ge(w_split, N_SLABS + 1)
                for g in range(GROUPS):
                    pe.wait_ge(bank_free, ALL - NORM + g + 1)
                    product(banks[g % RING][0:H, :], lambda k: w_hi[:, 0, k, 0:H], lambda k: w_lo[:, 0, k, 0:H],
                            lambda k: hT_hi[:, k, g * 512:(g + 1) * 512],
                            lambda k: hT_lo[:, k, g * 512:(g + 1) * 512]).then_inc(mm_done, 1)
                sample_rows(N_SLABS, 0, H).then_inc(s_done, 1)

            @block.scalar
            def _(act):
                act.sem_inc(bank_free, RING)
                act.sem_inc(s_free, 1)

                def sample_out(s, width=SLAB):
                    act.wait_ge(s_done, s + 1)
                    act.wait_ge(s_stored, 16 * (s + 1))
                    act.copy(stage_s[0:NB, 0:width], bank_s[0:NB, 0:width]).then_inc(s_free, 1)

                with act.Fori(0, 8) as s:
                    with act.Fori(0, PER // RING) as u:
                        for r in range(RING):
                            n = s * PER + RING * u + r
                            act.wait_ge(mm_done, n + 1)
                            act.wait_ge(q_own, n + 1)
                            act.activation(squares[:, :], banks[r][:, 0:SLAB], ACTF.Square).then_inc(q_sq, 1)
                    sample_out(s)
                with act.Fori(8, 12) as s:
                    with act.Fori(0, PER // RING) as u:
                        for r in range(RING):
                            n = s * PER + RING * u + r
                            act.wait_ge(mm_done, n + 1)
                            act.wait_ge(stored[r], 16 * (s * (PER // RING) + u + 1))
                            act.copy(stage[:, r, :], banks[r][:, 0:SLAB]).then_inc(bank_free, 1)
                    sample_out(s)
                with act.Fori(12, 16) as s:
                    with act.Fori(0, PER // RING) as u:
                        for r in range(RING):
                            n = s * PER + RING * u + r
                            act.wait_ge(mm_done, n + 1)
                            act.wait_ge(stored[r], 16 * (s * (PER // RING) + u + 1))
                            act.activation(stage[:, r, :], banks[r][:, 0:SLAB], ACTF.Silu).then_inc(bank_free, 1)
                    sample_out(s)
                with act.Fori(0, D // SLAB) as s:
                    for c in range(2):
                        act.wait_ge(xc_stored, 16 * (2 * s + c + 1))
                        for g in range(GROUPS):
                            n = ALL_TOK + s * CPER + c * GROUPS + g
                            act.wait_ge(mm_done, n + 1)
                            act.activation(xc[:, g * 512:(g + 1) * 512], banks[g][:, :], ACTF.Silu).then_inc(bank_free, 1)
                    sample_out(TOK_SLABS + s)
                with act.Fori(0, CONV // SLAB) as s:
                    for c in range(2):
                        m = 2 * s + c
                        act.wait_ge(raw_stored, 16 * (m + 1))
                        act.wait_ge(conv_sum, m + 1)
                        for g in range(GROUPS):
                            n = ALL_TOK + G_TILES * GROUPS + m * GROUPS + g
                            act.wait_ge(mm_done, n + 1)
                            act.copy(xc_in[:, TAPS - 1 + g * 512:TAPS - 1 + (g + 1) * 512], banks[g][:, :]).then_inc(bank_free, 1)
                        act.wait_ge(conv_sum, m + 2)
                        act.activation(xc[:, :], xc[:, :], ACTF.Silu).then_inc(conv_act, 1)
                    sample_out(TOK_SLABS + D // SLAB + s)
                act.wait_ge(xc_stored, 16 * (G_TILES + CONV // P + 1))
                for g in range(GROUPS):
                    act.wait_ge(mm_done, ALL + g + 1)
                    act.copy(xc[0:H, g * 512:(g + 1) * 512], banks[g][0:H, :]).then_inc(bank_free, 1)
                sample_out(N_SLABS, H)

            @block.vector
            def _(dve):
                dve.sem_inc(norm_free, RING)
                dve.sem_inc(q_own, 1)
                dve.memset(xc_in[:, 0:TAPS - 1], 0.0).then_inc(pad_set, 1)
                dve.wait_ge(pad_set, 1)
                dve.sem_inc(conv_sum, 1)
                dve.wait_ge(small_loaded, 64)
                dve.tensor_scalar(qkw[:, 0, :], qkw[:, 0, :], HD ** -0.5, None, ALU.mult).then_inc(pad_set, 1)
                dve.wait_ge(pad_set, 2)
                for kind in range(2):
                    with dve.Fori(4 * kind, 4 * kind + 4) as s:
                        with dve.Fori(0, PER // RING) as u:
                            for r in range(RING):
                                n = s * PER + RING * u + r
                                dve.wait_ge(q_sq, n + 1)
                                dve.tensor_reduce(ssq[:, :], squares[:, :].rearrange("p (h e) -> p h e", e=HD), AX.X,
                                                  ALU.add).then_inc(q_own, 1)
                                dve.wait_ge(q_own, n + 2)
                                dve.tensor_scalar(msq[:, :], ssq[:, :], 1.0 / HD, EPS, ALU.mult, ALU.add).then_inc(q_sum, 1)
                                dve.wait_ge(q_root, n + 1)
                                dve.tensor_tensor(scaled[:, :].rearrange("p (h e) -> p h e", e=HD),
                                                  banks[r][:, 0:SLAB].rearrange("p (h e) -> p h e", e=HD),
                                                  spread(rsq[:, :], HD), ALU.mult).then_inc(norm_free, 1)
                                dve.wait_ge(norm_free, RING + n + 1)
                                dve.wait_ge(stored[r], 16 * (s * (PER // RING) + u + 1))
                                dve.tensor_tensor(stage[:, r, :].rearrange("p (h e) -> p h e", e=HD),
                                                  scaled[:, :].rearrange("p (h e) -> p h e", e=HD),
                                                  repeat(qkw[:, kind, :], 4), ALU.mult).then_inc(staged, 1)
                with dve.Fori(0, CONV // P) as m:
                    dve.wait_ge(xc_stored, 16 * (G_TILES + m + 1))
                    dve.wait_ge(bank_free, RING + ALL_TOK - NORM + (G_TILES + m + 1) * GROUPS)
                    w = cw[:, bass.ds(m, 1), :].rearrange("p a t -> p (a t)")
                    dve.tensor_scalar(xc[:, :], xc_in[:, 0:SEQ], w[:, 0:1], cb[:, bass.ds(m, 1)], ALU.mult, ALU.add).then_inc(conv_step, 1)
                    for i in range(1, TAPS):
                        dve.wait_ge(conv_step, (TAPS - 1) * m + i)
                        dve.scalar_tensor_tensor(out=xc[:, :], in0=xc_in[:, i:i + SEQ], scalar=w[:, i:i + 1], in1=xc[:, :],
                                                 op0=ALU.mult, op1=ALU.add).then_inc(conv_step if i < TAPS - 1 else conv_sum, 1)

            @block.sync
            def _(sp):
                for r in range(RING):
                    sp.sem_inc(stored[r], 16)
                sp.sem_inc(s_stored, 16)
                sp.sem_inc(xc_stored, 16)
                sp.sem_inc(raw_stored, 16)
                sp.dma_start(qkw[:, 0, :], rows_of(io["q_norm_w"], P)).then_inc(small_loaded, 16)
                sp.dma_start(qkw[:, 1, :], rows_of(io["k_norm_w"], P)).then_inc(small_loaded, 16)
                sp.dma_start(cw[:, :, :], io["conv_w_t"].rearrange("(m p) t -> p m t", p=P)).then_inc(small_loaded, 16)
                sp.dma_start(cb[:, :], io["conv_b"].rearrange("(m p) -> p m", p=P),
                             allow_slow_non_contiguous=True).then_inc(small_loaded, 16)

                def sample_store(s, width=SLAB):
                    sp.wait_ge(s_free, s + 2)
                    sp.dma_start(scr["proj_s"][:, bass.ds(s * SLAB, width)], stage_s[0:NB, 0:width]).then_inc(s_stored, 16)

                for kind, dst in enumerate((scr["q"], io["k_out"], io["v_out"], scr["z"])):
                    with sp.Fori(0, 4) as s:
                        with sp.Fori(0, PER // RING) as u:
                            for r in range(RING):
                                n = (4 * kind + s) * PER + RING * u + r
                                if kind < 2:
                                    sp.wait_ge(staged, n + 1)
                                else:
                                    sp.wait_ge(bank_free, RING + n + 1 - NORM)
                                sp.dma_start(dst[bass.ds((RING * u + r) * P, P), bass.ds(s * SLAB, SLAB)],
                                             stage[:, r, :]).then_inc(stored[r], 16)
                        sample_store(4 * kind + s)
                with sp.Fori(0, D // SLAB) as s:
                    for c in range(2):
                        sp.wait_ge(bank_free, RING + ALL_TOK - NORM + (2 * s + c + 1) * GROUPS)
                        sp.dma_start(scr["gT"][bass.ds((2 * s + c) * P, P), :], xc[:, :]).then_inc(xc_stored, 16)
                    sample_store(TOK_SLABS + s)
                with sp.Fori(0, CONV // SLAB) as s:
                    for c in range(2):
                        m = 2 * s + c
                        sp.wait_ge(bank_free, RING + ALL_TOK - NORM + (G_TILES + m + 1) * GROUPS)
                        sp.dma_start(io["conv_p"][bass.ds(m * P, P), :], xc_in[:, SEQ:SEQ + TAPS - 1],
                                     allow_slow_non_contiguous=True).then_inc(raw_stored, 16)
                        sp.wait_ge(conv_act, m + 1)
                        sp.dma_start(scr["xcT"][bass.ds(m * P, P), :], xc[:, :]).then_inc(xc_stored, 16)
                    sample_store(TOK_SLABS + D // SLAB + s)
                sp.wait_ge(bank_free, RING + ALL - NORM + GROUPS)
                sp.dma_start(scr["dtT"], xc[0:H, :]).then_inc(xc_stored, 16)
                sample_store(N_SLABS, H)
                for r in range(RING):
                    sp.wait_ge(stored[r], 16 * (TOK_SLABS * PER // RING + 1))
                sp.wait_ge(xc_stored, 16 * (G_TILES + CONV // P + 2))
                sp.wait_ge(raw_stored, 16 * (CONV // P + 1))
                sp.wait_ge(s_stored, 16 * (N_SLABS + 2))


def bias_tables(nc, io, scr):
    with ExitStack() as ctx:
        relb = ctx.enter_context(nc.sbuf_tensor("relb", [BUCKETS + 1, H], F32))
        onehot = ctx.enter_context(nc.sbuf_tensor("onehot_sb", [BUCKETS + 1, 3, SHIFTS], F32))
        rows = ctx.enter_context(nc.sbuf_tensor("rows_sb", [H, 3, SHIFTS], F32))
        banks = [ctx.enter_context(nc.psum_tensor(f"tab{p}", [P, 512], F32)) for p in range(3)]
        sem = lambda n: nc.alloc_semaphore(n)
        loaded, ones_set, made, copied, stored, spread_out = (
            sem("tab_loaded"), sem("tab_ones"), sem("tab_made"), sem("tab_copied"), sem("tab_stored"), sem("tab_spread"))
        block = ctx.enter_context(nc.Block())

        @block.sync
        def _(sp):
            sp.dma_start(relb[0:BUCKETS, :], io["rel_bias"]).then_inc(loaded, 16)
            sp.dma_start(onehot[:, :, :], io["onehot"].rearrange("b (d u) -> b d u", d=3)).then_inc(loaded, 16)
            sp.wait_ge(copied, 3)
            sp.dma_start(scr["rows"], rows[:, :, :].rearrange("h d u -> h (d u)")).then_inc(stored, 16)
            sp.wait_ge(stored, 16)
            for p, (at, wide) in enumerate(BIAS_AT):
                first = p * SHIFTS + P - 1 + 2 * P - wide
                src = bass.AP(tensor=scr["rows"].tensor, offset=first, ap=[[3 * SHIFTS, H], [-1, P], [1, wide]])
                sp.dma_start(scr["bias"].rearrange("(h q) n -> h q n", q=P)[:, :, at:at + wide], src).then_inc(spread_out, 16)
            sp.wait_ge(spread_out, 48)

        @block.vector
        def _(dve):
            dve.memset(relb[BUCKETS:BUCKETS + 1, :], 1.0).then_inc(ones_set, 1)
            for p in range(3):
                dve.wait_ge(made, p + 1)
                dve.tensor_copy(rows[:, p, :], banks[p][0:H, 0:SHIFTS]).then_inc(copied, 1)

        @block.tensor
        def _(pe):
            pe.wait_ge(loaded, 32)
            pe.wait_ge(ones_set, 1)
            for p in range(3):
                pe.matmul(banks[p][0:H, 0:SHIFTS], relb[:, :], onehot[:, p, :], start=True, stop=True).then_inc(made, 1)


def attention_plan():
    tiles, at = [], 0
    block = {}
    order = [(2, r, 0) for r in range(16)] + [(1, r, b) for b in range(4) for r in range(4)] + [(0, 0, t) for t in range(16)]
    for p, r, b in order:
        prev = p < 2 and b > 0
        tiles.append((p, r, b, at, prev))
        if prev:
            block[p, r, b, "prev"] = at
            at += P
        block[p, r, b, "own"] = at
        at += P
    tile_at = {(p, r, b): n for n, (p, r, b, _, _) in enumerate(tiles)}
    groups = []
    for g in range(4):
        rs = range(4 * g, 4 * g + 4)
        groups.append(dict(
            blocks=[block[2, r, 0, "own"] for r in rs], needs=tile_at[2, rs[-1], 0],
            products=[dict(v=(2, r), at=P * (r % 4), n=P, bank=g, col=P * (r % 4), start=r % 4 == 0) for r in rs]))
    for half in range(2):
        for r in range(4):
            blocks, products = [], []
            for kb in (2 * half, 2 * half + 1):
                n = 2 * P if kb < 3 else P
                products.append(dict(v=(1, 4 * kb + r), at=P * len(blocks), n=n, bank=r, col=P * kb, start=kb == 0))
                blocks.append(block[1, r, kb, "own"])
                if kb < 3:
                    blocks.append(block[1, r, kb + 1, "prev"])
            groups.append(dict(blocks=blocks, needs=tile_at[1, r, min(3, 2 * half + 2)], products=products))
    for u in range(8):
        blocks, products = [], []
        for kb in (2 * u, 2 * u + 1):
            at_own = P * len(blocks)
            blocks.append(block[0, 0, kb, "own"])
            if kb < 15:
                blocks.append(block[0, 0, kb + 1, "prev"])
            if kb % 4 < 3:
                products.append(dict(v=(0, kb), at=at_own, n=2 * P, bank=kb // 4, col=P * (kb % 4), start=kb == 0))
            else:
                products.append(dict(v=(0, kb), at=at_own, n=P, bank=kb // 4, col=3 * P, start=False))
                if kb < 15:
                    products.append(dict(v=(0, kb), at=at_own + P, n=P, bank=kb // 4 + 1, col=0, start=True))
        groups.append(dict(blocks=blocks, needs=tile_at[0, 0, min(15, 2 * u + 2)], products=products))
    return tiles, groups, at


def attend(nc, io, scr):
    tiles, groups, width = attention_plan()
    NG = len(groups)
    NT = len(tiles)
    FRONT = 8 + NT // 2
    with ExitStack() as ctx:
        def sb(name, shape, dt=F32):
            return ctx.enter_context(nc.sbuf_tensor(name, shape, dt))

        ident = sb("ident_a", [P, P])
        q_in = sb("q_in", [P, TILES, P])
        k_in = sb("k_in", [P, TILES, P])
        q_st = sb("q_st", [P, SEQ], F32R)
        k_hi = sb("k_hi", [P, SEQ], F32R)
        k_lo = sb("k_lo", [P, SEQ], F32R)
        v_in = sb("v_in", [P, 3, TILES, 3 * HD])
        bias = sb("bias_sb", [P, 2, BIAS_W])
        score = sb("score", [P, 2, width])
        top = sb("top", [P, 2, NT])
        tick = sb("tick", [P, 2, NT // 2])
        tops = sb("tops_sb", [P, 3, TILES])
        top2 = sb("top2", [P, TILES])
        ntop = sb("ntop_sb", [P, 2, NT])
        turned_p = sb("turned_p", [P, 4, 512])
        acc = sb("acc", [P, 2, SEQ])
        recip = sb("recip", [P, SEQ])
        gate = sb("gate", [P, SEQ])
        den_in = sb("den_in", [P, 16])
        minus_one = sb("minus_one", [P, 16])
        front = [ctx.enter_context(nc.psum_tensor(f"front{b}", [P, 512], F32)) for b in range(2)]
        back = [ctx.enter_context(nc.psum_tensor(f"back{b}", [P, 512], F32)) for b in range(2)]
        obank = [ctx.enter_context(nc.psum_tensor(f"obank{b}", [P, 512], F32)) for b in range(4)]
        sem = lambda n: nc.alloc_semaphore(n)
        const_in = sem("const_in")
        qk_loaded = sem("qk_loaded")
        v_loaded = [sem(f"v_loaded{p}") for p in range(3)]
        ones_set = sem("ones_set")
        bias_loaded = [sem(f"bias_loaded{b}") for b in range(2)]
        gate_loaded = sem("gate_loaded")
        front_ready = sem("front_ready")
        front_free = sem("front_free")
        hi_taken = sem("hi_taken")
        top_written, top_read, top_maxed, ntop_made, ntop_written, ntop_loaded = (
            sem("top_written"), sem("top_read"), sem("top_maxed"), sem("ntop_made"), sem("ntop_written"), sem("ntop_loaded"))
        exp_done = sem("exp_done")
        back_ready = sem("back_ready")
        even_out, odd_out = sem("even_out"), sem("odd_out")
        mixed = sem("mixed")
        o_out = [sem("o1_out"), sem("o4_out"), sem("o16_out")]
        den_moved = sem("den_moved")
        recip_done = sem("recip_done")
        scaled = sem("scaled")
        finished = sem("finished")
        stored = sem("mix_stored")
        block = ctx.enter_context(nc.Block())

        def v_src(p, j):
            d = DILATIONS[p]
            cols = io["v_out"][:, bass.ds(j * P, P)]
            if p == 0:
                return cols.rearrange("(t i) c -> i t c", i=P)
            if p == 1:
                return cols.rearrange("(b i r) c -> i b r c", b=4, r=4)
            return cols.rearrange("(i r) c -> i r c", r=16)

        def load_v(eng, p, j):
            src = v_src(p, j)
            for side in range(2):
                at = 2 * HD * side
                dst = v_in[:, p, :, at:at + HD]
                if p == 1:
                    for b in range(4):
                        eng.dma_start(dst[:, 4 * b:4 * b + 4, :], src[:, b, :, side * HD:(side + 1) * HD]).then_inc(v_loaded[p], 16)
                else:
                    eng.dma_start(dst, src[:, :, side * HD:(side + 1) * HD]).then_inc(v_loaded[p], 16)

        V_LOADS = (2, 8, 2)

        def token_order(ap_of_row, p):
            t, o = ap_of_row.tensor, ap_of_row.offset
            if p == 0:
                return bass.AP(tensor=t, offset=o, ap=[[1, P], [P, TILES]])
            if p == 1:
                return bass.AP(tensor=t, offset=o, ap=[[4, P], [512, 4], [1, 4]])
            return bass.AP(tensor=t, offset=o, ap=[[16, P], [1, 16]])

        col_at = {0: 32, 1: 16, 2: 0}

        @block.sync
        def _(sp):
            def load_qk(h):
                for dst, src in ((q_in, scr["q"]), (k_in, io["k_out"])):
                    for twice in range(2):
                        sp.dma_start(dst[:, :, twice * HD:(twice + 1) * HD],
                                     src[:, bass.ds(h * HD, HD)].rearrange("(t i) c -> i t c", i=P)).then_inc(qk_loaded, 16)

            def load_bias(h, b):
                sp.dma_start(bias[:, b, :], scr["bias"][bass.ds(h * P, P), :]).then_inc(bias_loaded[b], 16)

            def load_gate(j):
                sp.dma_start(gate[:, :], scr["gT"][bass.ds(j * P, P), :]).then_inc(gate_loaded, 16)

            def meet(h, b):
                sp.wait_ge(front_free, 2 + FRONT * (h + 1))
                for p in range(3):
                    at = col_at[p]
                    sp.dma_start(token_order(scr["tops"][p:p + 1, :], p), top[:, b, at:at + 16],
                                 allow_slow_non_contiguous=True).then_inc(top_written, 16)
                sp.wait_ge(top_written, 48 * (h + 1))
                sp.dma_start(tops[:, :, :], scr["tops"].rearrange("d (i r) -> i d r", r=16)).then_inc(top_read, 16)

            def part(h, b):
                sp.wait_ge(ntop_made, h + 1)
                sp.dma_start(token_order(scr["ntop"], 2), ntop[:, b, 0:16]).then_inc(ntop_written, 16)
                sp.wait_ge(ntop_written, 16 * (h + 1))
                for p in range(2):
                    at = col_at[p]
                    sp.dma_start(ntop[:, b, at:at + 16], token_order(scr["ntop"], p),
                                 allow_slow_non_contiguous=True).then_inc(ntop_loaded, 16)
                sp.wait_ge(ntop_loaded, 32 * (h + 1))

            def denominators(h, b):
                den = HD * (1 - b)
                sp.wait_ge(o_out[0], 4 * h + 8)
                sp.dma_start(scr["den"][0:1, :], acc[den:den + 1, b, :]).then_inc(den_moved, 16)
                sp.wait_ge(den_moved, 64 * h + 16)
                sp.dma_start(den_in[:, :], scr["den"][0, :].rearrange("(i r) -> i r", r=16)).then_inc(den_moved, 16)
                sp.wait_ge(recip_done, h + 1)
                sp.dma_start(scr["den"][1, :].rearrange("(i r) -> i r", r=16), den_in[:, :]).then_inc(den_moved, 16)
                sp.wait_ge(den_moved, 64 * h + 48)
                sp.dma_start(recip[HD * b:HD * b + HD, :], rows_of(scr["den"][1, :], HD)).then_inc(den_moved, 16)

            def store(h, b):
                sp.wait_ge(finished, h + 1)
                sp.dma_start(scr["mT"][bass.ds(h * HD, HD), :], acc[HD * b:HD * b + HD, b, :]).then_inc(stored, 16)

            def step(h, b, pair, den=True, qk=True, v=True, bias_on=True):
                if bias_on:
                    load_bias(h + 1, 1 - b)
                if b == 1 and v:
                    for p, lots in ((1, 12), (0, 20)):
                        sp.wait_ge(mixed, NG * (h - 2) + lots)
                        load_v(sp, p, pair)
                if den:
                    denominators(h - 2, b)
                meet(h, b)
                if qk:
                    sp.wait_ge(front_ready, FRONT * (h + 1) + 8)
                    load_qk(h + 2)
                part(h, b)
                if den:
                    store(h - 2, b)
                if b == 1 and v:
                    load_gate(pair)
                if b == 0:
                    sp.wait_ge(mixed, NG * (h - 1) + 4)
                    load_v(sp, 2, pair + 1)

            sp.sem_inc(stored, 32)
            sp.dma_start(ident[:, :], io["ident"]).then_inc(const_in, 16)
            load_qk(0)
            load_bias(0, 0)
            sp.wait_ge(ones_set, 2)
            sp.wait_ge(front_ready, 8)
            load_qk(1)
            load_bias(1, 1)
            for p in (2, 1, 0):
                load_v(sp, p, 0)
            load_gate(0)
            meet(0, 0)
            sp.wait_ge(front_ready, FRONT + 8)
            load_qk(2)
            part(0, 0)
            sp.wait_ge(front_free, 2 + FRONT)
            step(1, 1, 0, den=False, v=False)
            step(2, 0, 0)
            with sp.Fori(1, H // 2 - 2) as i:
                step(2 * i + 1, 1, i)
                step(2 * i + 2, 0, i)
            step(H - 3, 1, H // 2 - 2)
            step(H - 2, 0, H // 2 - 2, qk=False)
            step(H - 1, 1, H // 2 - 1, qk=False, bias_on=False)
            for h in (H - 2, H - 1):
                denominators(h, h % 2)
                store(h, h % 2)
            sp.wait_ge(stored, 16 * (H + 2))

        @block.gpsimd
        def _(pool):
            pool.memset(v_in[:, :, :, HD:2 * HD], 1.0).then_inc(ones_set, 1)
            pool.memset(minus_one[:, :], -1.0).then_inc(ones_set, 1)
            pool.wait_ge(ones_set, 2)

            def finish(h, b, pair):
                rows = slice(HD * b, HD * b + HD)
                pool.wait_ge(den_moved, 64 * h + 32)
                pool.tensor_tensor(den_in[:, :], den_in[:, :], minus_one[:, :], ALU.pow).then_inc(recip_done, 1)
                pool.wait_ge(den_moved, 64 * h + 64)
                pool.tensor_tensor(acc[rows, b, :], acc[rows, b, :], recip[rows, :], ALU.mult).then_inc(scaled, 1)
                pool.wait_ge(scaled, h + 1)
                pool.wait_ge(gate_loaded, 16 * (pair + 1))
                pool.tensor_tensor(acc[rows, b, :], acc[rows, b, :], gate[rows, :], ALU.mult).then_inc(finished, 1)
                pool.wait_ge(finished, h + 1)

            with pool.Fori(0, H // 2) as i:
                finish(2 * i, 0, i)
                finish(2 * i + 1, 1, i)

        @block.tensor
        def _(pe):
            def front_bank(n_before, b):
                pe.wait_ge(front_free, n_before + 1)
                return front[b]

            def turn(h):
                pe.wait_ge(qk_loaded, 64 * (h + 1))
                for u in range(8):
                    c, src = u // 2, (q_in, k_in)[u % 2]
                    bank = front_bank(FRONT * h + u, u % 2)
                    for t in range(4):
                        last = pe.transpose(bank[:, t * P:(t + 1) * P],
                                            src[:, 4 * c + t, :], ident[:, :])
                    last.then_inc(front_ready, 1)

            def scores(h, b):
                pe.wait_ge(front_free, 2 + FRONT * h + 8)
                for u in range(NT // 2):
                    bank = front_bank(FRONT * h + 8 + u, u % 2)
                    for s in range(2):
                        p, r, blk, _, prev = tiles[2 * u + s]
                        d = DILATIONS[p]
                        lhs = with_axes(q_st[:, 0:1], [[d, P]], P * d * blk + r)
                        if p == 2:
                            axes, at = [[1, 2], [16, P]], r - r % 2
                        else:
                            axes, at = [[d, 2 * P]], P * d * max(blk - 1, 0) + r
                        out = bank[:, 2 * P * s:2 * P * (s + 1)]
                        pe.matmul(out, lhs, with_axes(k_hi[:, 0:1], axes, at), start=True, stop=False)
                        last = pe.matmul(out, lhs, with_axes(k_lo[:, 0:1], axes, at), start=False, stop=True)
                    last.then_inc(front_ready, 1)

            def mix(h, b, pair):
                vcols = slice(HD * b, HD * b + P)

                def turn_lot(g):
                    lot = groups[g]
                    pe.wait_ge(exp_done, NT * h + lot["needs"] + 1)
                    if g >= 2:
                        pe.wait_ge((even_out, odd_out)[g % 2], NG // 2 * h + g // 2)
                    for n, at in enumerate(lot["blocks"]):
                        last = pe.transpose(back[g % 2][:, n * P:(n + 1) * P], score[:, b, at:at + P], ident[:, :])
                    last.then_inc(back_ready, 1)

                def multiply(g):
                    pe.wait_ge((even_out, odd_out)[g % 2], NG // 2 * h + g // 2 + 1)
                    lot = groups[g]
                    if g in (0, 4, 12):
                        pe.wait_ge(v_loaded[{0: 2, 4: 1, 12: 0}[g]], 16 * V_LOADS[{0: 2, 4: 1, 12: 0}[g]] * (pair + 1))
                    for m in lot["products"]:
                        p = m["v"][0]
                        if m["start"]:
                            if p < 2:
                                pe.wait_ge(o_out[p + 1], 4 * h + m["bank"] + 1)
                            else:
                                pe.wait_ge(o_out[0], 4 * h + m["bank"] + 1)
                        last = pe.matmul(obank[m["bank"]][:, m["col"]:m["col"] + m["n"]], v_in[:, p, m["v"][1], vcols],
                                         turned_p[:, g % 4, m["at"]:m["at"] + m["n"]], start=m["start"], stop=True,
                                         skip_group_check=True)
                    last.then_inc(mixed, 1)

                for g in range(NG + 1):
                    if g < NG:
                        turn_lot(g)
                    if g >= 1:
                        multiply(g - 1)

            pe.wait_ge(const_in, 16)
            turn(0)
            scores(0, 0)
            turn(1)
            with pe.Fori(0, H // 2 - 1) as i:
                scores(2 * i + 1, 1)
                turn(2 * i + 2)
                mix(2 * i, 0, i)
                scores(2 * i + 2, 0)
                turn(2 * i + 3)
                mix(2 * i + 1, 1, i)
            scores(H - 1, 1)
            mix(H - 2, 0, H // 2 - 1)
            mix(H - 1, 1, H // 2 - 1)

        @block.vector
        def _(dve):
            dve.sem_inc(front_free, 2)
            dve.sem_inc(o_out[0], 4)

            def turn(h):
                for u in range(8):
                    c, bank = u // 2, front[u % 2]
                    cols = slice(512 * c, 512 * (c + 1))
                    dve.wait_ge(hi_taken, 8 * h + u + 1)
                    if u % 2 == 0:
                        dve.tensor_tensor(q_st[HD:P, cols], bank[HD:P, :], q_st[HD:P, cols].bitcast(F32),
                                          ALU.subtract).then_inc(front_free, 1)
                    else:
                        dve.tensor_tensor(k_lo[:, cols], bank[:, :], k_hi[:, cols].bitcast(F32), ALU.subtract).then_inc(front_free, 1)

            def scores(h, b, pair_use):
                dve.wait_ge(bias_loaded[b], 16 * (pair_use + 1))
                for u in range(NT // 2):
                    dve.wait_ge(front_ready, FRONT * h + 8 + u + 1)
                    dve.memset(tick[:, b, u:u + 1], 0.0)
                    for s in range(2):
                        n = 2 * u + s
                        p, r, blk, at, prev = tiles[n]
                        b_at, b_w = BIAS_AT[p]
                        w = 2 * P if prev else P
                        skip = P if p == 2 and r % 2 else 0
                        last = dve.tensor_tensor_reduce(
                            out=score[:, b, at:at + w], in0=front[u % 2][:, 2 * P * s + skip:2 * P * s + skip + w],
                            in1=bias[:, b, b_at + b_w - w:b_at + b_w], scale=1.0, scalar=-3e38, op0=ALU.add, op1=ALU.max,
                            accum_out=top[:, b, n:n + 1])
                    last.then_inc(front_free, 1)

            def meet(h, b):
                dve.wait_ge(top_read, 16 * (h + 1))
                dve.tensor_reduce(top2[:, :], tops[:, :, :].rearrange("p d r -> p r d"), AX.X, ALU.max).then_inc(top_maxed, 1)
                dve.wait_ge(top_maxed, h + 1)
                dve.tensor_scalar(ntop[:, b, 0:16], top2[:, :], -1.0, None, ALU.mult).then_inc(ntop_made, 1)

            def mix(h, b, more=True):
                for g in range(NG + 1):
                    if g == 4 and more:
                        meet(h + 1, 1 - b)
                    if g < NG and g % 2 == 0:
                        dve.wait_ge(back_ready, NG * h + g + 1)
                        if g >= 4:
                            dve.wait_ge(mixed, NG * h + g - 3)
                        n = P * len(groups[g]["blocks"])
                        dve.tensor_copy(turned_p[:, g % 4, 0:n], back[0][:, 0:n]).then_inc(even_out, 1)
                    if 10 <= g <= 13:
                        r = g - 10
                        dve.wait_ge(mixed, NG * h + 8 + r + 1)
                        dve.wait_ge(o_out[2], 4 * h + 4)
                        sl = acc[:, b, :].rearrange("p (i r) -> p i r", r=4)[:, :, r]
                        dve.tensor_tensor(sl, sl, obank[r][:, :], ALU.add).then_inc(o_out[1], 1)
                    if g in (15, 17, 19, 20):
                        r = {15: 0, 17: 1, 19: 2, 20: 3}[g]
                        dve.wait_ge(mixed, NG * h + 12 + 2 * r + 2)
                        if r == 0:
                            dve.wait_ge(o_out[1], 4 * h + 4)
                        cols = slice(512 * r, 512 * (r + 1))
                        dve.tensor_tensor(acc[:, b, cols], acc[:, b, cols], obank[r][:, :], ALU.add).then_inc(o_out[0], 1)

            turn(0)
            scores(0, 0, 0)
            turn(1)
            meet(0, 0)
            with dve.Fori(0, H // 2 - 1) as i:
                scores(2 * i + 1, 1, i)
                turn(2 * i + 2)
                mix(2 * i, 0)
                scores(2 * i + 2, 0, i + 1)
                turn(2 * i + 3)
                mix(2 * i + 1, 1)
            scores(H - 1, 1, H // 2 - 1)
            mix(H - 2, 0)
            mix(H - 1, 1, False)

        @block.scalar
        def _(act):
            def turn(h):
                for u in range(8):
                    c, bank = u // 2, front[u % 2]
                    cols = slice(512 * c, 512 * (c + 1))
                    act.wait_ge(front_ready, FRONT * h + u + 1)
                    act.copy((q_st, k_hi)[u % 2][:, cols], bank[:, :]).then_inc(hi_taken, 1)

            def exps(h, b):
                act.wait_ge(ntop_loaded, 32 * (h + 1))
                act.wait_ge(ntop_made, h + 1)
                for n, (p, r, blk, at, prev) in enumerate(tiles):
                    w = 2 * P if prev else P
                    act.activation(score[:, b, at:at + w], score[:, b, at:at + w], ACTF.Exp,
                                   bias=ntop[:, b, n:n + 1]).then_inc(exp_done, 1)

            def mix(h, b):
                for g in range(NG):
                    if g % 2 == 1:
                        act.wait_ge(back_ready, NG * h + g + 1)
                        if g >= 4:
                            act.wait_ge(mixed, NG * h + g - 3)
                        n = P * len(groups[g]["blocks"])
                        act.copy(turned_p[:, g % 4, 0:n], back[1][:, 0:n]).then_inc(odd_out, 1)
                    if 2 <= g <= 5:
                        r = g - 2
                        act.wait_ge(mixed, NG * h + r + 1)
                        if r == 0:
                            act.wait_ge(stored, 16 * (h + 1))
                        dst = acc[:, b, :].rearrange("p (i r) -> p r i", r=16)[:, 4 * r:4 * r + 4, :]
                        act.copy(dst, obank[r][:, :].rearrange("p (r i) -> p r i", r=4)).then_inc(o_out[2], 1)

            turn(0)
            turn(1)
            with act.Fori(0, H // 2 - 1) as i:
                exps(2 * i, 0)
                turn(2 * i + 2)
                mix(2 * i, 0)
                exps(2 * i + 1, 1)
                turn(2 * i + 3)
                mix(2 * i + 1, 1)
            exps(H - 2, 0)
            mix(H - 2, 0)
            exps(H - 1, 1)
            mix(H - 1, 1)


def scan(nc, io, scr):
    NC = SEQ // P
    G = 2
    HG = H // G
    with ExitStack() as ctx:
        def sb(name, shape, dt=F32):
            return ctx.enter_context(nc.sbuf_tensor(name, shape, dt))

        ident = sb("ident_s", [P, P])
        tri = sb("tri_sb", [P, P])
        dt_raw = sb("dt_raw", [H, SEQ])
        step_h = sb("step_h", [H, SEQ])
        cum_h = sb("cum_h", [H, SEQ])
        work_a = sb("work_a", [H, SEQ])
        work_b = sb("work_b", [H, SEQ])
        h_small = sb("h_small", [H, 4])
        d_row = sb("d_row", [P, H])
        norm_b = sb("norm_b_s", [P, D])
        tok = sb("tok", [P, 2, NC, H])
        xc = sb("xc_chunk", [P, 2, CONV // P, P])
        zt = sb("zt", [P, 2, D])
        cum_all = sb("cum_all", [P, 2, H, P])
        x_tok = sb("x_tok", [P, 2, D])
        b_tok = sb("b_tok", [P, 2, G * P])
        masked = sb("masked", [P, G, P])
        decay = sb("decay", [P, 2, H, P])
        pre = sb("pre", [P, 2, 3, H])
        fac = sb("fac", [P, 2, 3, H])
        xdt = sb("xdt", [P, 2, D])
        xend = sb("xend", [P, 2, D])
        xskip = sb("xskip", [P, 2, D])
        part = sb("part", [P, D])
        state = sb("state", [P, D])
        sq = sb("sq_s", [P, D])
        small = sb("small_s", [P, 3])
        mhalf = sb("mhalf_s", [P, 1])
        out_t = sb("out_t", [P, 2, KT, P])
        XA = ctx.enter_context(nc.psum_tensor("XA", [P, D], F32))
        MX = ctx.enter_context(nc.psum_tensor("MX", [P, 512], F32))
        OFF = ctx.enter_context(nc.psum_tensor("OFF", [P, D], F32))
        DG = ctx.enter_context(nc.psum_tensor("DG", [P, D], F32))
        sem = lambda n: nc.alloc_semaphore(n)
        small_in, mhalf_set = sem("small_in_s"), sem("mhalf_set_s")
        pro_act, pro_dve, pro_pe, pro_ok, cum_out = (
            sem("pro_act"), sem("pro_dve"), sem("pro_pe"), sem("pro_ok"), sem("cum_out"))
        xc_in, z_in, cum_in = ([sem(f"{n}{b}") for b in range(2)] for n in ("xc_in_s", "z_in_s", "cum_in_s"))
        x_turned = sem("x_turned")
        mx_ready = sem("mx_ready")
        x_taken = sem("x_taken")
        b_taken = sem("b_taken")
        cb_masked = sem("cb_masked")
        seg_ready = sem("seg_ready")
        seg_exp = sem("seg_exp")
        fac_ready, pre_ready = sem("fac_ready"), sem("pre_ready")
        dve_a, dve_b = sem("dve_a"), sem("dve_b")
        decay_ready = sem("decay_ready")
        xdt_ready, xend_ready, xskip_ready = sem("xdt_ready"), sem("xend_ready"), sem("xskip_ready")
        off_ready, diag_ready, new_ready = sem("off_ready"), sem("diag_ready"), sem("new_ready")
        off_out = sem("off_out")
        diag_out = sem("diag_out")
        state_ready = sem("state_ready")
        skip_added, gated, squared, meaned, rooted, normed = (
            sem("skip_added"), sem("gated_s"), sem("squared_s"), sem("meaned_s"), sem("rooted_s"), sem("normed_s"))
        u_turned, u_taken = sem("u_turned"), sem("u_taken")
        stored = [sem(f"stored_s{b}") for b in range(2)]
        ssm_stored = sem("ssm_stored")
        block = ctx.enter_context(nc.Block())

        heads = lambda ap: ap.rearrange("p (h e) -> p h e", e=HD)

        @block.sync
        def _(sp):
            def load(c, b):
                sp.dma_start(xc[:, b, :, :], scr["xcT"].rearrange("(m p) t -> p m t", p=P)[:, :, bass.ds(c * P, P)]).then_inc(xc_in[b], 16)
                sp.dma_start(zt[:, b, :], scr["z"][bass.ds(c * P, P), :]).then_inc(z_in[b], 16)
                row = scr["cum"][:, bass.ds(c * P, P)]
                sp.dma_start(cum_all[:, b, :, :], bass.AP(tensor=row.tensor, offset=row.offset, ap=[[0, P], [SEQ, H], [1, P]],
                                                          )).then_inc(cum_in[b], 16)

            def store(c, b):
                sp.wait_ge(u_taken, c + 1)
                sp.dma_start(scr["mT"][D:2 * D, :].rearrange("(m p) t -> p m t", p=P)[:, :, bass.ds(c * P, P)],
                             out_t[:, b, :, :]).then_inc(stored[b], 16)

            for b in range(2):
                sp.sem_inc(stored[b], 16)
            sp.dma_start(dt_raw[:, :], scr["dtT"]).then_inc(small_in, 16)
            sp.dma_start(h_small[:, 0:1], io["dt_bias"].rearrange("(h o) -> h o", o=1)).then_inc(small_in, 16)
            sp.dma_start(h_small[:, 1:2], io["a_log"].rearrange("(h o) -> h o", o=1)).then_inc(small_in, 16)
            sp.dma_start(ident[:, :], io["ident"]).then_inc(small_in, 16)
            sp.dma_start(tri[:, :], io["tri"]).then_inc(small_in, 16)
            sp.dma_start(d_row[:, :], rows_of(io["d_skip"], P)).then_inc(small_in, 16)
            sp.dma_start(norm_b[:, :], rows_of(io["ssd_norm_w"], P)).then_inc(small_in, 16)
            sp.wait_ge(pro_ok, 1)
            sp.dma_start(scr["cum"], cum_h[:, :]).then_inc(cum_out, 16)
            sp.wait_ge(cum_out, 16)
            load(0, 0)
            load(1, 1)

            def step(c, b):
                store(c, b)
                load(c + 2, b)

            with sp.Fori(0, NC // 2 - 1) as i:
                for b in range(2):
                    step(2 * i + b, b)
            store(NC - 2, 0)
            store(NC - 1, 1)
            sp.wait_ge(state_ready, NC + 1)
            sp.dma_start(io["ssm_p"], state[:, :]).then_inc(ssm_stored, 16)
            sp.wait_ge(ssm_stored, 16)
            for b in range(2):
                sp.wait_ge(stored[b], 16 * (NC // 2 + 1))

        @block.scalar
        def _(act):
            act.wait_ge(small_in, 16 * 7)
            act.activation(h_small[:, 2:3], h_small[:, 1:2], ACTF.Exp).then_inc(pro_act, 1)
            act.wait_ge(pro_dve, 2)
            act.activation(work_b[:, :], work_b[:, :], ACTF.Exp, scale=-1.0).then_inc(pro_act, 1)
            act.wait_ge(pro_dve, 3)
            act.activation(step_h[:, :], work_a[:, :], ACTF.Ln).then_inc(pro_act, 1)

            def prepare(c, b):
                act.wait_ge(x_turned, c + 1)
                act.copy(x_tok[:, b, :], XA[:, :]).then_inc(x_taken, 1)
                act.wait_ge(mx_ready, c + 1)
                act.copy(b_tok[:, b, :], MX[:, 0:G * P]).then_inc(b_taken, 1)
                act.wait_ge(pre_ready, c + 1)
                act.activation(fac[:, b, :, :], pre[:, b, :, :], ACTF.Exp).then_inc(fac_ready, 1)
                act.wait_ge(seg_ready, c + 1)
                act.activation(cum_all[:, b, :, :], cum_all[:, b, :, :], ACTF.Exp).then_inc(seg_exp, 1)

            def apply(c, b, i):
                act.wait_ge(gated, c + 1)
                act.activation(sq[:, :], xskip[:, b, :], ACTF.Square, accum_out=small[:, 0:1]).then_inc(squared, 1)
                act.wait_ge(u_turned, c + 1)
                act.wait_ge(stored[b], 16 * (i + 1))
                act.copy(out_t[:, b, :, :], OFF[:, :].rearrange("p (m t) -> p m t", t=P)).then_inc(u_taken, 1)

            prepare(0, 0)
            with act.Fori(0, NC // 2 - 1) as i:
                prepare(2 * i + 1, 1)
                apply(2 * i, 0, i)
                prepare(2 * i + 2, 0)
                apply(2 * i + 1, 1, i)
            prepare(NC - 1, 1)
            apply(NC - 2, 0, NC // 2 - 1)
            apply(NC - 1, 1, NC // 2 - 1)

        @block.gpsimd
        def _(pool):
            pool.memset(mhalf[:, :], -0.5).then_inc(mhalf_set, 1)
            pool.memset(state[:, :], 0.0).then_inc(mhalf_set, 1)
            pool.wait_ge(mhalf_set, 2)

            def prepare(c, b):
                pool.wait_ge(x_taken, c + 1)
                pool.tensor_tensor(heads(xskip[:, b, :]), heads(x_tok[:, b, :]), spread(d_row[:, :], HD), ALU.mult).then_inc(xskip_ready, 1)
                pool.wait_ge(xskip_ready, c + 1)
                pool.wait_ge(xdt_ready, c + 1)
                pool.wait_ge(fac_ready, c + 1)
                pool.tensor_tensor(heads(xend[:, b, :]), heads(xdt[:, b, :]), spread(fac[:, b, 0, :], HD), ALU.mult).then_inc(xend_ready, 1)
                pool.wait_ge(xend_ready, c + 1)

            def apply(c, b, i):
                pool.wait_ge(diag_out, c + 1)
                pool.tensor_tensor(xskip[:, b, :], xskip[:, b, :], part[:, :], ALU.add).then_inc(skip_added, 1)
                pool.wait_ge(skip_added, c + 1)
                pool.wait_ge(z_in[b], 16 * (i + 1))
                pool.tensor_tensor(xskip[:, b, :], xskip[:, b, :], zt[:, b, :], ALU.mult).then_inc(gated, 1)
                pool.wait_ge(gated, c + 1)
                pool.wait_ge(meaned, c + 1)
                pool.tensor_tensor(small[:, 2:3], small[:, 1:2], mhalf[:, :], ALU.pow).then_inc(rooted, 1)
                pool.wait_ge(rooted, c + 1)

            pool.wait_ge(small_in, 16 * 7)
            prepare(0, 0)
            with pool.Fori(0, NC // 2 - 1) as i:
                prepare(2 * i + 1, 1)
                apply(2 * i, 0, i)
                prepare(2 * i + 2, 0)
                apply(2 * i + 1, 1, i)
            prepare(NC - 1, 1)
            apply(NC - 2, 0, NC // 2 - 1)
            apply(NC - 1, 1, NC // 2 - 1)

        @block.vector
        def _(dve):
            chain = Chain(dve, pro_dve)
            dve.wait_ge(small_in, 16 * 7)
            chain(dve.tensor_scalar(dt_raw[:, :], dt_raw[:, :], h_small[:, 0:1], None, ALU.add))
            chain(dve.scalar_tensor_tensor(out=work_b[:, :], in0=dt_raw[:, :], scalar=-1.0, in1=dt_raw[:, :],
                                           op0=ALU.mult, op1=ALU.max))
            dve.wait_ge(pro_act, 2)
            chain(dve.tensor_scalar(work_a[:, :], work_b[:, :], 1.0, None, ALU.add))
            dve.wait_ge(pro_act, 3)
            chain(dve.tensor_tensor(step_h[:, :], step_h[:, :], work_b[:, :], ALU.mult))
            chain(dve.tensor_scalar(work_a[:, :], work_a[:, :], -1.0, None, ALU.add))
            chain(dve.scalar_tensor_tensor(out=cum_h[:, :], in0=work_a[:, :], scalar=0.0, in1=work_b[:, :],
                                           op0=ALU.is_equal, op1=ALU.mult))
            chain(dve.tensor_scalar(work_a[:, :], work_a[:, :], 1e-30, None, ALU.max))
            chain(dve.reciprocal(work_a[:, :], work_a[:, :]))
            chain(dve.tensor_tensor(step_h[:, :], step_h[:, :], work_a[:, :], ALU.mult))
            chain(dve.tensor_tensor(step_h[:, :], step_h[:, :], cum_h[:, :], ALU.add))
            chain(dve.scalar_tensor_tensor(out=step_h[:, :], in0=dt_raw[:, :], scalar=0.0, in1=step_h[:, :],
                                           op0=ALU.max, op1=ALU.add))
            chain(dve.tensor_scalar(h_small[:, 2:3], h_small[:, 2:3], -1.0, None, ALU.mult))
            chain(dve.tensor_scalar(work_b[:, :], step_h[:, :], h_small[:, 2:3], None, ALU.mult))
            chain(dve.memset(work_a[:, :], 1.0))
            chain(dve.memset(work_a[:, :].rearrange("h (c l) -> h c l", l=P)[:, :, 0:1], 0.0))
            dve.tensor_tensor_scan(cum_h[:, :], work_a[:, :], work_b[:, :], 0.0, ALU.mult, ALU.add).then_inc(pro_ok, 1)
            dve.wait_ge(pro_pe, 1)
            dve.tensor_copy(tok[:, :, :, :], MX[:, :].rearrange("p (a c h) -> p a c h", a=2, h=H)).then_inc(pro_ok, 1)
            dve.wait_ge(pro_ok, 2)
            dve.wait_ge(mhalf_set, 2)
            dve.sem_inc(state_ready, 1)

            def prepare(c, b, i):
                step = tok[:, 0, bass.ds(c, 1), :].rearrange("p o h -> p (o h)")
                cum = tok[:, 1, bass.ds(c, 1), :].rearrange("p o h -> p (o h)")
                dve.wait_ge(cum_in[b], 16 * (i + 1))
                last = cum_all[:, b, :, P - 1:P].rearrange("p h o -> p (h o)")
                a = Chain(dve, dve_a)
                a.base = 4 * c
                a(dve.tensor_tensor(pre[:, b, 0, :], last, cum, ALU.subtract))
                a(dve.tensor_scalar(pre[:, b, 1, :], cum, 1.0, None, ALU.mult))
                dve.tensor_copy(pre[:, b, 2, :], last).then_inc(pre_ready, 1)
                dve.wait_ge(pre_ready, c + 1)
                a(dve.tensor_tensor(cum_all[:, b, :, :], cum_all[:, b, :, :], spread(cum, P), ALU.subtract))
                dve.tensor_scalar(cum_all[:, b, :, :], cum_all[:, b, :, :], 0.0, None, ALU.min).then_inc(seg_ready, 1)
                dve.wait_ge(x_taken, c + 1)
                dve.tensor_tensor(heads(xdt[:, b, :]), heads(x_tok[:, b, :]), spread(step, HD), ALU.mult).then_inc(xdt_ready, 1)
                dve.wait_ge(b_taken, c + 1)
                dve.tensor_tensor(masked[:, :, :], MX[:, G * P:].rearrange("p (g l) -> p g l", g=G), repeat(tri[:, :], G),
                                  ALU.mult).then_inc(cb_masked, 1)
                dve.wait_ge(cb_masked, c + 1)
                dve.wait_ge(seg_exp, c + 1)
                for g in range(G):
                    hs = slice(HG * g, HG * (g + 1))
                    ins = dve.tensor_tensor(decay[:, b, hs, :], cum_all[:, b, hs, :], repeat(masked[:, g, :], HG), ALU.mult)
                    if g == 0:
                        a(ins)
                    else:
                        ins.then_inc(decay_ready, 1)
                dve.wait_ge(decay_ready, c + 1)
                assert a.count == 4

            def apply(c, b, first=False):
                dve.wait_ge(fac_ready, c + 1)
                dve.wait_ge(off_ready, c + 1)
                if not first:
                    dve.wait_ge(skip_added, c)
                dve.tensor_tensor(heads(part[:, :]), heads(OFF[:, :]), spread(fac[:, b, 1, :], HD), ALU.mult).then_inc(off_out, 1)
                dve.wait_ge(off_out, c + 1)
                dve.wait_ge(diag_ready, c + 1)
                dve.tensor_tensor(part[:, :], DG[:, :], part[:, :], ALU.add).then_inc(diag_out, 1)
                dve.tensor_tensor(heads(state[:, :]), heads(state[:, :]), spread(fac[:, b, 2, :], HD), ALU.mult).then_inc(dve_b, 1)
                dve.wait_ge(dve_b, c + 1)
                dve.wait_ge(new_ready, c + 1)
                dve.tensor_tensor(state[:, :], XA[:, :], state[:, :], ALU.add).then_inc(state_ready, 1)
                dve.wait_ge(squared, c + 1)
                dve.tensor_scalar(small[:, 1:2], small[:, 0:1], 1.0 / D, EPS, ALU.mult, ALU.add).then_inc(meaned, 1)
                dve.wait_ge(rooted, c + 1)
                dve.scalar_tensor_tensor(out=xskip[:, b, :], in0=xskip[:, b, :], scalar=small[:, 2:3], in1=norm_b[:, :],
                                         op0=ALU.mult, op1=ALU.mult).then_inc(normed, 1)

            prepare(0, 0, 0)
            prepare(1, 1, 0)
            apply(0, 0, True)
            prepare(2, 0, 1)
            apply(1, 1)
            with dve.Fori(1, NC // 2 - 1) as i:
                prepare(2 * i + 1, 1, i)
                apply(2 * i, 0)
                prepare(2 * i + 2, 0, i + 1)
                apply(2 * i + 1, 1)
            prepare(NC - 1, 1, NC // 2 - 1)
            apply(NC - 2, 0)
            apply(NC - 1, 1)

        @block.tensor
        def _(pe):
            pe.wait_ge(small_in, 16 * 7)
            pe.wait_ge(pro_ok, 1)
            for a, src in enumerate((step_h, cum_h)):
                for c in range(NC):
                    at = (a * NC + c) * H
                    last = pe.transpose(MX[:, at:at + H], src[:, c * P:(c + 1) * P], ident[0:H, 0:H])
            last.then_inc(pro_pe, 1)
            pe.wait_ge(pro_ok, 2)

            def prepare(c, b, i, first=False):
                pe.wait_ge(xc_in[b], 16 * (i + 1))
                if not first:
                    pe.wait_ge(x_taken, c)
                    pe.wait_ge(state_ready, c)
                for m in range(KT):
                    last = pe.transpose(XA[:, m * P:(m + 1) * P], xc[:, b, m, :], ident[:, :])
                last.then_inc(x_turned, 1)
                if not first:
                    pe.wait_ge(cb_masked, c)
                for g in range(G):
                    pe.transpose(MX[:, g * P:(g + 1) * P], xc[:, b, KT + g, :], ident[:, :])
                for g in range(G):
                    last = pe.matmul(MX[:, (G + g) * P:(G + g + 1) * P], xc[:, b, KT + g, :], xc[:, b, KT + G + g, :],
                                     start=True, stop=True)
                last.then_inc(mx_ready, 1)

            def apply(c, b, first=False):
                pe.wait_ge(state_ready, c + 1)
                if not first:
                    pe.wait_ge(u_taken, c)
                for g in range(G):
                    last = pe.matmul(OFF[:, g * 512:(g + 1) * 512], xc[:, b, KT + G + g, :], state[:, g * 512:(g + 1) * 512],
                                     start=True, stop=True)
                last.then_inc(off_ready, 1)
                pe.wait_ge(x_taken, (c + 2) if not last_one[0] else NC)
                pe.wait_ge(b_taken, c + 1)
                pe.wait_ge(xend_ready, c + 1)
                for g in range(G):
                    last = pe.matmul(XA[:, g * 512:(g + 1) * 512], b_tok[:, b, g * P:(g + 1) * P], xend[:, b, g * 512:(g + 1) * 512],
                                     start=True, stop=True)
                last.then_inc(new_ready, 1)
                pe.wait_ge(decay_ready, c + 1)
                if not first:
                    pe.wait_ge(diag_out, c)
                for h in range(H):
                    last = pe.matmul(DG[:, h * HD:(h + 1) * HD], decay[:, b, h, :], xdt[:, b, h * HD:(h + 1) * HD],
                                     start=True, stop=True)
                last.then_inc(diag_ready, 1)
                pe.wait_ge(off_out, c + 1)
                pe.wait_ge(normed, c + 1)
                for m in range(KT):
                    last = pe.transpose(OFF[:, m * P:(m + 1) * P], xskip[:, b, m * P:(m + 1) * P], ident[:, :])
                last.then_inc(u_turned, 1)

            last_one = [False]
            prepare(0, 0, 0, True)
            prepare(1, 1, 0)
            apply(0, 0, True)
            prepare(2, 0, 1)
            apply(1, 1)
            with pe.Fori(1, NC // 2 - 1) as i:
                prepare(2 * i + 1, 1, i)
                apply(2 * i, 0)
                prepare(2 * i + 2, 0, i + 1)
                apply(2 * i + 1, 1)
            prepare(NC - 1, 1, NC // 2 - 1)
            apply(NC - 2, 0)
            last_one[0] = True
            apply(NC - 1, 1)


def decode(nc, io, scr):
    BH = NB * H
    NP = len(DILATIONS)
    with ExitStack() as ctx:
        def sb(name, shape, dt=F32):
            return ctx.enter_context(nc.sbuf_tensor(name, shape, dt))

        qk = sb("qk_d", [BH, 2, HD])
        qk_w = sb("qk_w_d", [BH, 2, HD])
        v_new = sb("v_new", [BH, HD])
        g_t = sb("g_d", [BH, HD])
        z_t = sb("z_d", [BH, HD])
        norm_h = sb("norm_h", [BH, HD])
        col = sb("col_d", [BH, 4])
        window = sb("window", [BH, TAPS, CONV // H])
        taps = sb("taps", [BH, TAPS, CONV // H])
        conv_bias = sb("conv_bias_d", [BH, CONV // H])
        ident = sb("ident_d", [P, P])
        pick_sb = sb("pick_sb", [BH, 4])
        same_sb = sb("same_sb", [BH, BH])
        seq_sb = sb("seq_sb", [NB, BH])
        near_sb = sb("near_sb", [BUCKETS, NP * P + 1])
        rel_rep = sb("rel_rep", [BUCKETS, NB, H])
        sums = sb("sums_d", [BH, 2])
        rs = sb("rs_d", [BH, 2])
        half = sb("half_d", [BH, 2])
        prod = sb("prod_d", [BH, HD])
        s0 = sb("s0", [BH, 1])
        q_all = sb("q_all", [P, 2, D])
        kt = sb("kt_d", [P, 2, NP, D])
        vt = sb("vt_d", [P, 2, NP, D])
        S = sb("S_d", [P, NP, BH])
        biased = sb("biased", [BH, NP * P + 1])
        prob = sb("prob_d", [BH, NP, P])
        probT = sb("probT", [P, NP, BH])
        top = sb("top_d", [BH, 4])
        p0 = sb("p0_d", [BH, 1])
        den = sb("den_d", [BH, 2])
        pv = sb("pv_d", [P, BH])
        att = sb("att_d", [BH, HD])
        half_a = sb("half_a", [BH, HD])
        raw_d, abs_d, one_d, ln_d, tiny_d, rate_d = (sb(f"soft{i}", [BH, 1]) for i in range(6))
        scal = sb("scal_d", [BH, 3])
        state = sb("state_d", [BH, HD, NST])
        outer = sb("outer_d", [BH, HD, NST])
        bc4 = sb("bc4", [NB, 4 * NST])
        bc = sb("bc_d", [BH, 2, NST])
        bc_half = sb("bc_half", [BH, 2, NST])
        x_h = sb("x_h", [BH, HD])
        xdt = sb("xdt_d", [BH, HD])
        y_h = sb("y_h", [BH, HD])
        us = sb("us_d", [BH, 3])
        ps = lambda name, shape: ctx.enter_context(nc.psum_tensor(name, shape, F32))
        near_ps = ps("near_ps", [BH, 512])
        turn_ps = ps("turn_ps", [P, 512])
        back_ps = ps("back_ps", [P, 512])
        pv_ps = ps("pv_ps", [P, 512])
        bc_ps = ps("bc_ps", [BH, 512])
        pvT_ps = ps("pvT_ps", [BH, 512])
        rms_ps = ps("rms_ps", [BH, 512])
        sem = lambda n: nc.alloc_semaphore("d_" + n)
        loaded, xc_in, state_in = sem("loaded"), sem("xc_in"), sem("state_in")
        half_set, squared, meaned, rooted, qk_ready = sem("half_set"), sem("squared"), sem("meaned"), sem("rooted"), sem("qk_ready")
        q_stored, xc_stored, stored = sem("q_stored"), sem("xc_stored"), sem("stored")
        conv_sum, conv_act = sem("conv_sum"), sem("conv_act")
        silu = sem("silu")
        dv = sem("vector_order")
        k_in, v_in, q_in = ([sem(f"{n}{b}") for b in range(2)] for n in ("k_in", "v_in", "q_in"))
        k_used = sem("k_used")
        v_used = sem("v_used")
        near_ready, turned, bc_ready = sem("near_ready"), sem("turned"), sem("bc_ready")
        near_out = sem("near_out")
        top_ready, exped, p0_ready, backed, prob_out, pv_ready, pv_out, pvT_ready = (
            sem("top_ready"), sem("exped"), sem("p0_ready"), sem("backed"), sem("prob_out"), sem("pv_ready"), sem("pv_out"), sem("pvT_ready"))
        a_exp, abs_ready, e_ready, w_ready, ln_ready, rate_ready, decay_ready = (
            sem("a_exp"), sem("abs_ready"), sem("e_ready"), sem("w_ready"), sem("ln_ready"), sem("rate_ready"), sem("decay_ready"))
        state_ready, u_ready, u_sq, u_sum, u_mean, u_root, u_norm, att_ready = (
            sem("state_ready"), sem("u_ready"), sem("u_sq"), sem("u_sum"), sem("u_mean"), sem("u_root"), sem("u_norm"), sem("att_ready"))
        block = ctx.enter_context(nc.Block())

        proj = scr["proj_s"]
        CW = CONV // H
        N_LOADS = 5 + 2 + 1 + 4 + 4 + 4 + 1 + 4 + 2

        def pairs(vector, width):
            return bass.AP(tensor=vector.tensor, offset=vector.offset, ap=[[0, NB], [width, H], [1, width]])

        @block.sync
        def _(sp):
            def part_of(first, width=HD):
                return bass.AP(tensor=proj.tensor, offset=first, ap=[[NPROJ, NB], [width, H], [1, width]])

            def load(out, src):
                sp.dma_start(out, src).then_inc(loaded, 16)

            def load_cache(out, src, j, b, signal):
                for p, d in enumerate(DILATIONS):
                    row = src[bass.ds(2 * j + b, 1), WIN - P * d, :]
                    sp.dma_start(out[:, b, p, :], bass.AP(tensor=row.tensor, offset=row.offset, ap=[[d * D, P], [1, D]])).then_inc(signal[b], 16)

            def load_q(j, b):
                row = scr["q_s"][bass.ds((2 * j + b) * H, H), :]
                sp.dma_start(q_all[:, b, :], bass.AP(tensor=row.tensor, offset=row.offset, ap=[[0, P], [1, D]])).then_inc(q_in[b], 16)

            load(qk[:, 0, :], part_of(Q0))
            load(qk[:, 1, :], part_of(K0))
            load(v_new[:, :], part_of(V0))
            load(g_t[:, :], part_of(G0))
            load(z_t[:, :], part_of(Z0))
            load(qk_w[:, 0, :], rows_of(io["q_norm_w"], BH))
            load(qk_w[:, 1, :], rows_of(io["k_norm_w"], BH))
            load(norm_h[:, :], pairs(io["ssd_norm_w"], HD))
            load(col[:, 0:1], part_of(DT0, 1))
            for i, name in enumerate(("dt_bias", "a_log", "d_skip")):
                load(col[:, 1 + i:2 + i], pairs(io[name], 1))
            for i in range(TAPS):
                if i < TAPS - 1:
                    src = bass.AP(tensor=io["state_conv"].tensor, offset=i * CONV, ap=[[(TAPS - 1) * CONV, NB], [CW, H], [1, CW]])
                else:
                    src = part_of(C0, CW)
                load(window[:, i, :], src)
                load(taps[:, i, :], pairs(io["conv_w"][i, :], CW))
            load(conv_bias[:, :], pairs(io["conv_b"], CW))
            load(ident[:, :], io["ident"])
            load(pick_sb[:, :], io["pick"])
            load(same_sb[:, :], io["same_seq"])
            load(seq_sb[:, :], io["of_seq"])
            load(near_sb[:, :], io["near"])
            load(rel_rep[:, :, :], bass.AP(tensor=io["rel_bias"].tensor, offset=0, ap=[[H, BUCKETS], [0, NB], [1, H]]))
            sp.dma_start(state[:, :, :], io["state_ssm"].rearrange("a (p n) -> a p n", n=NST)).then_inc(state_in, 16)
            for b in range(2):
                load_cache(kt, io["cache_k"], 0, b, k_in)
            sp.dma_start(io["conv_s"][:, 0:TAPS - 2, :], io["state_conv"][:, 1:TAPS - 1, :]).then_inc(stored, 16)
            sp.dma_start(io["conv_s"][:, TAPS - 2, :], proj[:, C0:DT0]).then_inc(stored, 16)
            sp.wait_ge(qk_ready, 2)
            sp.dma_start(scr["q_s"], qk[:, 0, :]).then_inc(q_stored, 16)
            sp.dma_start(io["ks_out"], qk[:, 1, :]).then_inc(stored, 16)
            sp.dma_start(io["vs_out"], v_new[:, :]).then_inc(stored, 16)
            sp.wait_ge(q_stored, 16)
            for b in range(2):
                load_q(0, b)
            sp.wait_ge(conv_act, 1)
            sp.dma_start(bass.AP(tensor=scr["xc_s"].tensor, offset=0, ap=[[CONV, NB], [CW, H], [1, CW]]), taps[:, 0, :]).then_inc(xc_stored, 16)
            sp.wait_ge(xc_stored, 16)
            sp.dma_start(x_h[:, :], bass.AP(tensor=scr["xc_s"].tensor, offset=0, ap=[[CONV, NB], [HD, H], [1, HD]])).then_inc(xc_in, 16)
            sp.dma_start(bc4[:, :], scr["xc_s"][:, D:CONV]).then_inc(xc_in, 16)
            for b in range(2):
                load_cache(vt, io["cache_v"], 0, b, v_in)
            with sp.Fori(1, NB // 2) as j:
                for b in range(2):
                    sp.wait_ge(k_used, 2 * j + b - 1)
                    load_cache(kt, io["cache_k"], j, b, k_in)
                    load_q(j, b)
            with sp.Fori(1, NB // 2) as j:
                for b in range(2):
                    sp.wait_ge(v_used, 2 * j + b - 1)
                    load_cache(vt, io["cache_v"], j, b, v_in)
            sp.wait_ge(state_ready, 1)
            sp.dma_start(io["ssm_s"].rearrange("a (p n) -> a p n", n=NST), state[:, :, :]).then_inc(stored, 16)
            mixed = scr["mixed_s"]
            sp.wait_ge(u_norm, 1)
            sp.dma_start(bass.AP(tensor=mixed.tensor, offset=D, ap=[[2 * D, NB], [HD, H], [1, HD]]), y_h[:, :]).then_inc(stored, 16)
            sp.wait_ge(att_ready, 1)
            sp.dma_start(bass.AP(tensor=mixed.tensor, offset=0, ap=[[2 * D, NB], [HD, H], [1, HD]]), att[:, :]).then_inc(stored, 16)
            sp.wait_ge(stored, 16 * 7)

        @block.scalar
        def _(act):
            act.wait_ge(loaded, 16 * N_LOADS)
            for i in range(2):
                act.activation(outer[:, i, 0:HD], qk[:, i, :], ACTF.Square, accum_out=sums[:, i:i + 1]).then_inc(squared, 1)
            act.activation(rate_d[:, :], col[:, 2:3], ACTF.Exp).then_inc(a_exp, 1)
            act.wait_ge(abs_ready, 1)
            act.activation(abs_d[:, :], abs_d[:, :], ACTF.Exp, scale=-1.0).then_inc(e_ready, 1)
            act.wait_ge(w_ready, 1)
            act.activation(ln_d[:, :], one_d[:, :], ACTF.Ln).then_inc(ln_ready, 1)
            act.wait_ge(rate_ready, 1)
            act.activation(scal[:, 2:3], scal[:, 1:2], ACTF.Exp).then_inc(decay_ready, 1)
            act.wait_ge(conv_sum, 1)
            act.activation(taps[:, 0, :], window[:, 0, :], ACTF.Silu).then_inc(conv_act, 1)
            act.activation(g_t[:, :], g_t[:, :], ACTF.Silu).then_inc(silu, 1)
            act.activation(z_t[:, :], z_t[:, :], ACTF.Silu).then_inc(silu, 1)
            act.wait_ge(near_ready, 1)
            act.copy(biased[:, :], near_ps[:, 0:NP * P + 1]).then_inc(near_out, 1)
            act.wait_ge(top_ready, 1)
            act.activation(prob[:, :, :], biased[:, 0:NP * P].rearrange("a (d j) -> a d j", j=P), ACTF.Exp, bias=top[:, 2:3],
                           accum_out=den[:, 0:1]).then_inc(exped, 1)
            act.activation(p0[:, :], s0[:, :], ACTF.Exp, bias=top[:, 2:3]).then_inc(p0_ready, 1)
            act.wait_ge(u_ready, 1)
            act.activation(xdt[:, :], y_h[:, :], ACTF.Square, accum_out=us[:, 0:1]).then_inc(u_sq, 1)
            act.wait_ge(backed, 1)
            act.copy(probT[:, :, :], back_ps[:, 0:NP * P].rearrange("j (d a) -> j d a", a=BH)).then_inc(prob_out, 1)
            act.wait_ge(pv_ready, 1)
            act.copy(pv[:, :], pv_ps[:, 0:BH]).then_inc(pv_out, 1)

        @block.gpsimd
        def _(pool):
            pool.memset(half[:, :], -0.5).then_inc(half_set, 1)
            pool.wait_ge(half_set, 1)
            pool.wait_ge(meaned, 1)
            pool.tensor_tensor(rs[:, :], sums[:, :], half[:, :], ALU.pow).then_inc(rooted, 1)
            pool.wait_ge(rooted, 1)
            pool.wait_ge(u_mean, 1)
            pool.tensor_tensor(us[:, 2:3], us[:, 1:2], half[:, 0:1], ALU.pow).then_inc(u_root, 1)

        @block.vector
        def _(dve):
            own = Chain(dve, dv)
            dve.wait_ge(loaded, 16 * N_LOADS)
            dve.wait_ge(squared, 2)
            dve.tensor_scalar(sums[:, :], sums[:, :], 1.0 / HD, EPS, ALU.mult, ALU.add).then_inc(meaned, 1)
            dve.wait_ge(rooted, 1)
            own(dve.tensor_scalar(rs[:, 0:1], rs[:, 0:1], HD ** -0.5, None, ALU.mult))
            for i in range(2):
                dve.scalar_tensor_tensor(out=qk[:, i, :], in0=qk[:, i, :], scalar=rs[:, i:i + 1], in1=qk_w[:, i, :],
                                         op0=ALU.mult, op1=ALU.mult).then_inc(qk_ready, 1)
            own(dve.tensor_tensor(window[:, :, :], window[:, :, :], taps[:, :, :], ALU.mult))
            own(dve.tensor_tensor(window[:, 0:2, :], window[:, 0:2, :], window[:, 2:4, :], ALU.add))
            own(dve.tensor_tensor(window[:, 0, :], window[:, 0, :], window[:, 1, :], ALU.add))
            dve.tensor_tensor(window[:, 0, :], window[:, 0, :], conv_bias[:, :], ALU.add).then_inc(conv_sum, 1)
            own(dve.tensor_tensor(raw_d[:, :], col[:, 0:1], col[:, 1:2], ALU.add))
            dve.scalar_tensor_tensor(out=abs_d[:, :], in0=raw_d[:, :], scalar=-1.0, in1=raw_d[:, :],
                                     op0=ALU.mult, op1=ALU.max).then_inc(abs_ready, 1)
            dve.wait_ge(e_ready, 1)
            dve.tensor_scalar(one_d[:, :], abs_d[:, :], 1.0, None, ALU.add).then_inc(w_ready, 1)
            dve.wait_ge(ln_ready, 1)
            own(dve.tensor_tensor(ln_d[:, :], ln_d[:, :], abs_d[:, :], ALU.mult))
            own(dve.tensor_scalar(one_d[:, :], one_d[:, :], -1.0, None, ALU.add))
            own(dve.scalar_tensor_tensor(out=tiny_d[:, :], in0=one_d[:, :], scalar=0.0, in1=abs_d[:, :],
                                         op0=ALU.is_equal, op1=ALU.mult))
            own(dve.tensor_scalar(one_d[:, :], one_d[:, :], 1e-30, None, ALU.max))
            own(dve.reciprocal(one_d[:, :], one_d[:, :]))
            own(dve.tensor_tensor(ln_d[:, :], ln_d[:, :], one_d[:, :], ALU.mult))
            own(dve.tensor_tensor(ln_d[:, :], ln_d[:, :], tiny_d[:, :], ALU.add))
            own(dve.scalar_tensor_tensor(out=scal[:, 0:1], in0=raw_d[:, :], scalar=0.0, in1=ln_d[:, :],
                                         op0=ALU.max, op1=ALU.add))
            dve.wait_ge(a_exp, 1)
            dve.scalar_tensor_tensor(out=scal[:, 1:2], in0=rate_d[:, :], scalar=-1.0, in1=scal[:, 0:1],
                                     op0=ALU.mult, op1=ALU.mult).then_inc(rate_ready, 1)
            dve.wait_ge(qk_ready, 2)
            own(dve.tensor_tensor(prod[:, :], qk[:, 0, :], qk[:, 1, :], ALU.mult))
            own(dve.tensor_reduce(s0[:, :], prod[:, :], axis=AX.X, op=ALU.add))

            used = Chain(dve, k_used)
            before = own.count
            with dve.Fori(0, NB // 2) as j:
                for b in range(2):
                    dve.wait_ge(k_in[b], 16 * NP * (j + 1))
                    dve.wait_ge(q_in[b], 16 * (j + 1))
                    dve.tensor_tensor(kt[:, b, :, :], kt[:, b, :, :], repeat(q_all[:, b, :], NP), ALU.mult).then_inc(dv, 1)
                    dve.wait_ge(dv, before + 2 * j + b + 1)
                    dve.tensor_reduce(S[:, :, bass.ds((2 * j + b) * H, H)], kt[:, b, :, :].rearrange("p d (h e) -> p d h e", e=HD),
                                      axis=AX.X, op=ALU.add).then_inc(k_used, 1)
            own.count += NB

            dve.wait_ge(bc_ready, 1)
            bcg = bc_ps[:, :].rearrange("a (i g n) -> a i g n", i=2, g=2)
            own(dve.tensor_scalar(bc_half[:, :, :], bcg[:, :, 1, :], pick_sb[:, 3:4], None, ALU.mult))
            own(dve.scalar_tensor_tensor(out=bc[:, :, :], in0=bcg[:, :, 0, :], scalar=pick_sb[:, 2:3], in1=bc_half[:, :, :],
                                         op0=ALU.mult, op1=ALU.add))
            dve.wait_ge(xc_in, 32)
            own(dve.tensor_scalar(xdt[:, :], x_h[:, :], scal[:, 0:1], None, ALU.mult))
            own(dve.tensor_tensor(outer[:, :, :], spread(xdt[:, :], NST), repeat(bc[:, 0, :], HD), ALU.mult))
            dve.wait_ge(decay_ready, 1)
            dve.wait_ge(state_in, 16)
            dve.scalar_tensor_tensor(out=state[:, :, :], in0=state[:, :, :], scalar=scal[:, 2:3], in1=outer[:, :, :],
                                     op0=ALU.mult, op1=ALU.add).then_inc(state_ready, 1)
            dve.wait_ge(state_ready, 1)

            dve.wait_ge(turned, 1)
            dve.wait_ge(near_out, 1)
            own(dve.tensor_tensor(biased[:, 0:NP * P], turn_ps[:, 0:NP * P], biased[:, 0:NP * P], ALU.add))
            own(dve.tensor_tensor(s0[:, :], s0[:, :], biased[:, NP * P:], ALU.add))
            own(dve.tensor_reduce(top[:, 0:1], biased[:, 0:NP * P], axis=AX.X, op=ALU.max))
            own(dve.tensor_tensor(top[:, 1:2], top[:, 0:1], s0[:, :], ALU.max))
            dve.tensor_scalar(top[:, 2:3], top[:, 1:2], -1.0, None, ALU.mult).then_inc(top_ready, 1)

            own(dve.tensor_tensor(outer[:, :, :], state[:, :, :], repeat(bc[:, 1, :], HD), ALU.mult))
            own(dve.tensor_reduce(y_h[:, :], outer[:, :, :], axis=AX.X, op=ALU.add))
            own(dve.scalar_tensor_tensor(out=y_h[:, :], in0=x_h[:, :], scalar=col[:, 3:4], in1=y_h[:, :],
                                         op0=ALU.mult, op1=ALU.add))
            dve.wait_ge(silu, 2)
            dve.tensor_tensor(y_h[:, :], y_h[:, :], z_t[:, :], ALU.mult).then_inc(u_ready, 1)
            dve.wait_ge(u_sum, 1)
            dve.tensor_scalar(us[:, 1:2], rms_ps[:, 0:1], 1.0 / D, EPS, ALU.mult, ALU.add).then_inc(u_mean, 1)
            dve.wait_ge(u_root, 1)
            dve.scalar_tensor_tensor(out=y_h[:, :], in0=y_h[:, :], scalar=us[:, 2:3], in1=norm_h[:, :],
                                     op0=ALU.mult, op1=ALU.mult).then_inc(u_norm, 1)

            dve.wait_ge(p0_ready, 1)
            dve.wait_ge(exped, 1)
            own(dve.tensor_scalar(p0[:, :], p0[:, :], float(NP), None, ALU.mult))
            own(dve.tensor_tensor(den[:, 0:1], den[:, 0:1], p0[:, :], ALU.add))
            own(dve.reciprocal(den[:, 1:2], den[:, 0:1]))
            own(dve.tensor_scalar(half_a[:, :], v_new[:, :], p0[:, 0:1], None, ALU.mult))
            dve.wait_ge(pvT_ready, 1)
            for i in range(2):
                own(dve.scalar_tensor_tensor(out=half_a[:, :], in0=pvT_ps[:, i * HD:(i + 1) * HD], scalar=pick_sb[:, i:i + 1],
                                             in1=half_a[:, :], op0=ALU.mult, op1=ALU.add))
            dve.scalar_tensor_tensor(out=att[:, :], in0=half_a[:, :], scalar=den[:, 1:2], in1=g_t[:, :],
                                     op0=ALU.mult, op1=ALU.mult).then_inc(att_ready, 1)

        @block.tensor
        def _(pe):
            pe.wait_ge(loaded, 16 * N_LOADS)
            pe.matmul(near_ps[:, 0:NP * P + 1], rel_rep[:, :, :].rearrange("b s h -> b (s h)"), near_sb[:, :], start=True, stop=True).then_inc(near_ready, 1)
            pe.wait_ge(xc_in, 32)
            pe.matmul(bc_ps[:, :], seq_sb[:, :], bc4[:, :], start=True, stop=True).then_inc(bc_ready, 1)
            pe.wait_ge(k_used, NB)
            for p in range(NP):
                last = pe.transpose(turn_ps[:, p * P:(p + 1) * P], S[:, p, :], ident[:, :])
            last.then_inc(turned, 1)
            pe.wait_ge(exped, 1)
            for p in range(NP):
                last = pe.transpose(back_ps[:, p * P:(p + 1) * P], prob[:, p, :], ident[:, :])
            last.then_inc(backed, 1)
            pe.wait_ge(prob_out, 1)
            with pe.Fori(0, NB // 2) as j:
                for b in range(2):
                    pe.wait_ge(v_in[b], 16 * NP * (j + 1))
                    for h in range(0, H, 2):
                        at = (2 * j + b) * H + h
                        for p in range(NP):
                            last = pe.matmul(pv_ps[:, bass.ds(at, 2)], vt[:, b, p, h * HD:(h + 2) * HD],
                                             probT[:, p, bass.ds(at, 2)], start=p == 0, stop=p == NP - 1)
                    last.then_inc(v_used, 1)
            pe.wait_ge(v_used, NB)
            pe.sem_inc(pv_ready, 1)
            pe.wait_ge(u_sq, 1)
            pe.matmul(rms_ps[:, 0:1], same_sb[:, :], us[:, 0:1], start=True, stop=True).then_inc(u_sum, 1)
            pe.wait_ge(pv_out, 1)
            pe.transpose(pvT_ps[:, 0:P], pv[:, :], ident[:, :]).then_inc(pvT_ready, 1)


def output(nc, io, scr):
    MK = 2 * D // P
    with ExitStack() as ctx:
        def sb(name, shape, dt=F32):
            return ctx.enter_context(nc.sbuf_tensor(name, shape, dt))

        w_hi = sb("wo_hi", [P, MK, D], F32R)
        w_lo = sb("wo_lo", [P, MK, D], F32R)
        m_raw = sb("m_raw", [P, 2, MK, P])
        m_hi = sb("m_hi", [P, 2, MK, P], F32R)
        m_lo = sb("m_lo", [P, 2, MK, P], F32R)
        x_t = sb("x_o", [P, 2, D])
        ident = sb("ident_o", [P, P])
        acc = [ctx.enter_context(nc.psum_tensor(f"acc{b}", [P, D], F32)) for b in range(2)]
        ms_ps = ctx.enter_context(nc.psum_tensor("ms_ps", [P, MK, NB], F32))
        sem = lambda n: nc.alloc_semaphore("o_" + n)
        w_in_ = [sem(f"w_in{b}") for b in range(2)]
        w_high, w_split = sem("w_high"), sem("w_split")
        m_in, x_in, y_stored = ([sem(f"{n}{b}") for b in range(2)] for n in ("m_in", "x_in", "y_stored"))
        m_high, m_split, done, added = sem("m_high"), sem("m_split"), sem("done"), sem("added")
        s_in, s_turned, ident_in = sem("s_in"), sem("s_turned"), sem("ident_in")
        block = ctx.enter_context(nc.Block())
        slab = lambda b: m_raw[:, b, 0:D // P, :].rearrange("p a t -> p (a t)")
        mixed_s = x_t[0:NB, :, :].rearrange("p a n -> p (a n)")

        @block.sync
        def _(sp):
            sp.dma_start(ident[:, :], io["ident"]).then_inc(ident_in, 16)
            for k in range(MK):
                if k >= 2:
                    sp.wait_ge(w_split, k - 1)
                sp.dma_start(slab(k % 2), io["w_out"][k * P:(k + 1) * P, :]).then_inc(w_in_[k % 2], 16)

            def load_m(t, b):
                sp.dma_start(m_raw[:, b, :, :], scr["mT"].rearrange("(m p) t -> p m t", p=P)[:, :, bass.ds(t * P, P)]).then_inc(m_in[b], 16)

            def load_x(t, b, rows=P):
                sp.dma_start(x_t[0:rows, b, :], io["x_all"][bass.ds(t * P, rows), :]).then_inc(x_in[b], 16)

            def store(t, b, rows=P):
                sp.wait_ge(added, t + 1)
                sp.dma_start(io["y_out"][bass.ds(t * P, rows), :], x_t[0:rows, b, :]).then_inc(y_stored[b], 16)

            for b in range(2):
                sp.wait_ge(w_split, MK - 1 + b)
                load_m(b, b)
                load_x(b, b)
            with sp.Fori(0, TILES // 2 - 1) as j:
                for b in range(2):
                    sp.wait_ge(m_split, 2 * j + b + 1)
                    load_m(2 * j + b + 2, b)
                    store(2 * j + b, b)
                    sp.wait_ge(y_stored[b], 16 * (j + 1))
                    load_x(2 * j + b + 2, b)
            store(TILES - 2, 0)
            store(TILES - 1, 1)
            for b in range(2):
                sp.wait_ge(y_stored[b], 16 * (TILES // 2))
            sp.dma_start(mixed_s, scr["mixed_s"]).then_inc(s_in, 16)
            sp.wait_ge(s_turned, 1)
            load_x(TILES, 0, NB)
            store(TILES, 0, NB)
            sp.wait_ge(y_stored[0], 16 * (TILES // 2 + 1))

        @block.scalar
        def _(act):
            for k in range(MK):
                act.wait_ge(w_in_[k % 2], 16 * (k // 2 + 1))
                act.copy(w_hi[:, k, :], slab(k % 2)).then_inc(w_high, 1)

            def high(t, b, j):
                act.wait_ge(m_in[b], 16 * (j + 1))
                if not isinstance(t, int) or t >= 2:
                    act.wait_ge(done, t - 1)
                act.copy(m_hi[:, b, :, :], m_raw[:, b, :, :]).then_inc(m_high, 1)

            for b in range(2):
                high(b, b, 0)
            with act.Fori(1, TILES // 2) as j:
                for b in range(2):
                    high(2 * j + b, b, j)
            act.wait_ge(done, TILES - 1)
            act.wait_ge(s_turned, 1)
            act.copy(m_hi[:, 0, :, 0:NB], ms_ps[:, :, :]).then_inc(m_high, 1)

        @block.vector
        def _(dve):
            for k in range(MK):
                dve.wait_ge(w_high, k + 1)
                dve.tensor_tensor(w_lo[:, k, :], slab(k % 2), w_hi[:, k, :].bitcast(F32), ALU.subtract).then_inc(w_split, 1)

            def low(t, b):
                dve.wait_ge(m_high, t + 1)
                dve.tensor_tensor(m_lo[:, b, :, :], m_raw[:, b, :, :], m_hi[:, b, :, :].bitcast(F32), ALU.subtract).then_inc(m_split, 1)

            def add(t, b, j, rows=P):
                dve.wait_ge(done, t + 1)
                dve.wait_ge(x_in[b], 16 * (j + 1))
                dve.tensor_tensor(x_t[0:rows, b, :], acc[b][0:rows, :], x_t[0:rows, b, :], ALU.add).then_inc(added, 1)

            for b in range(2):
                low(b, b)
            with dve.Fori(0, TILES // 2 - 1) as j:
                for b in range(2):
                    add(2 * j + b, b, j)
                    low(2 * j + b + 2, b)
            for b in range(2):
                add(TILES - 2 + b, b, TILES // 2 - 1)
            dve.wait_ge(m_high, TILES + 1)
            dve.tensor_tensor(m_lo[:, 0, :, 0:NB], ms_ps[:, :, :], m_hi[:, 0, :, 0:NB].bitcast(F32), ALU.subtract).then_inc(m_split, 1)
            add(TILES, 0, TILES // 2, NB)

        @block.tensor
        def _(pe):
            def tile(t, b, rows=P):
                pe.wait_ge(m_split, t + 1)
                if not isinstance(t, int) or t >= 2:
                    pe.wait_ge(added, t - 1)
                for n in range(D // 512):
                    out = acc[b][0:rows, n * 512:(n + 1) * 512]
                    cols = slice(n * 512, (n + 1) * 512)
                    for k in range(MK):
                        pe.matmul(out, m_hi[:, b, k, 0:rows], w_hi[:, k, cols], start=k == 0, stop=False)
                        pe.matmul(out, m_hi[:, b, k, 0:rows], w_lo[:, k, cols], start=False, stop=False)
                        last = pe.matmul(out, m_lo[:, b, k, 0:rows], w_hi[:, k, cols], start=False, stop=k == MK - 1)
                last.then_inc(done, 1)

            pe.wait_ge(w_split, MK)
            for b in range(2):
                tile(b, b)
            with pe.Fori(1, TILES // 2) as j:
                for b in range(2):
                    tile(2 * j + b, b)
            pe.wait_ge(ident_in, 16)
            pe.wait_ge(s_in, 16)
            for k in range(MK):
                last = pe.transpose(ms_ps[:, k, :], mixed_s[:, k * P:(k + 1) * P], ident[0:NB, 0:NB])
            last.then_inc(s_turned, 1)
            tile(TILES, 0, NB)


def build(nc, io):
    scr = {name: nc.dram_tensor(name, shape, F32).ap() for name, shape in SCRATCH.items()}
    for stage in STAGES:
        with nc.cleanup_on_exit():
            stage(nc, io, scr)
            nc.all_engine_barrier()
    return scr


SCRATCH = {
    "q": (SEQ, D),
    "z": (SEQ, D),
    "gT": (D, SEQ),
    "xcT": (CONV, SEQ),
    "dtT": (H, SEQ),
    "proj_s": (NB, NPROJ),
    "rows": (H, 3 * SHIFTS),
    "bias": (H * P, BIAS_W),
    "tops": (3, SEQ),
    "ntop": (1, SEQ),
    "den": (2, SEQ),
    "cum": (H, SEQ),
    "q_s": (NB * H, HD),
    "xc_s": (NB, CONV),
    "mixed_s": (NB, 2 * D),
    "mT": (2 * D, SEQ),
}
STAGES = [project, bias_tables, attend, scan, decode, output]
OUTPUTS = {
    "y_out": (TOK, D),
    "k_out": (SEQ, D),
    "v_out": (SEQ, D),
    "conv_p": (CONV, TAPS - 1),
    "ssm_p": (P, D),
    "ks_out": (NB * H, HD),
    "vs_out": (NB * H, HD),
    "conv_s": (NB, TAPS - 1, CONV),
    "ssm_s": (NB * H, HD * NST),
}


def t5_bucket(dist):
    exact = BUCKETS // 2
    far = np.maximum(dist, 1).astype(np.float32)
    large = exact + (np.log(far / np.float32(exact)) / np.float32(math.log(WIN / exact))
                     * np.float32(BUCKETS - exact)).astype(np.int32)
    return np.where(dist < exact, dist, np.minimum(large, BUCKETS - 1))


def constants():
    dist = 2 * P - 1 - np.arange(SHIFTS)
    inside = (dist >= 0) & (dist <= P)
    onehot = np.zeros((BUCKETS + 1, 3, SHIFTS), np.float32)
    for p, d in enumerate(DILATIONS):
        for u in np.flatnonzero(inside):
            onehot[t5_bucket(dist[u] * d), p, u] = 1.0
    onehot[BUCKETS, :, ~inside] = MASKED
    tri = np.triu(np.ones((P, P), np.float32))
    pair = np.arange(NB * H)
    pick = np.stack([pair % 2 == 0, pair % 2 == 1, pair % H < H // 2, pair % H >= H // 2], axis=1).astype(np.float32)
    same = (pair[:, None] // H == pair[None, :] // H).astype(np.float32)
    of_seq = (np.arange(NB)[:, None] == pair[None, :] // H).astype(np.float32)
    near = np.zeros((BUCKETS, len(DILATIONS) * P + 1), np.float32)
    for p, d in enumerate(DILATIONS):
        for j in range(P):
            near[t5_bucket((P - j) * d), p * P + j] = 1.0
    near[t5_bucket(0), -1] = 1.0
    return {"pick": pick, "same_seq": same, "of_seq": of_seq, "near": near, "tri": tri, "ident": np.eye(P, dtype=np.float32), "onehot": onehot.reshape(BUCKETS + 1, 3 * SHIFTS)}


def laid_out(inputs):
    a = {k: np.asarray(v) for k, v in inputs.items()}
    w = a["w_in"][0]
    cuts = np.split(w, [D, 2 * D, 3 * D, 4 * D, 5 * D, 5 * D + CONV], axis=1)
    q, k, v, g, z, xbc, dt = cuts
    out = {
        "x_all": np.concatenate([a["x_prompt"][0], a["x_sample"][:, 0]], axis=0),
        "w_in": np.concatenate([q, k, v, z, g, xbc, dt], axis=1),
        "norm_w": a["norm_w"][0], "q_norm_w": a["q_norm_w"][0], "k_norm_w": a["k_norm_w"][0],
        "conv_w_t": a["conv_w"][0].T, "conv_b": a["conv_b"][0],
        "conv_w": a["conv_w"][0],
        "cache_k": a["cache_win_k"][0].reshape(NB, WIN, D), "cache_v": a["cache_win_v"][0].reshape(NB, WIN, D),
        "state_conv": a["state_conv"][0], "state_ssm": a["state_ssm"][0].reshape(NB * H, HD * NST),
        "rel_bias": a["rel_bias"], "dt_bias": a["dt_bias"][0], "a_log": a["a_log"][0], "d_skip": a["d_skip"][0],
        "ssd_norm_w": a["ssd_norm_w"][0], "w_out": a["w_out"][0],
    }
    return {k: np.ascontiguousarray(v) for k, v in {**out, **constants()}.items()}


def kernel(**inputs):
    import concourse.bacc as bacc
    from concourse.bass_utils import run_bass_kernel_spmd

    nc = bacc.Bacc("TRN2", target_bir_lowering=False, num_devices=1)
    arrays = laid_out(inputs)
    io = {n: nc.dram_tensor(n, a.shape, mybir.dt.from_np(a.dtype), kind="ExternalInput").ap() for n, a in arrays.items()}
    io.update({n: nc.dram_tensor(n, s, F32, kind="ExternalOutput").ap() for n, s in OUTPUTS.items()})
    build(nc, io)
    r = run_bass_kernel_spmd(nc, [arrays], core_ids=[0]).results[0]
    y = r["y_out"]
    return (y[:SEQ].reshape(1, SEQ, D), y[SEQ:].reshape(NB, 1, D),
            r["k_out"].reshape(1, 1, SEQ, H, HD), r["v_out"].reshape(1, 1, SEQ, H, HD),
            np.ascontiguousarray(r["conv_p"].T).reshape(1, 1, TAPS - 1, CONV),
            np.ascontiguousarray(r["ssm_p"].reshape(NST, H, HD).transpose(1, 2, 0)).reshape(1, 1, H, HD, NST),
            r["ks_out"].reshape(1, NB, 1, H, HD), r["vs_out"].reshape(1, NB, 1, H, HD),
            r["conv_s"].reshape(1, NB, TAPS - 1, CONV), r["ssm_s"].reshape(1, NB, H, HD, NST))
```

```python
import math
from contextlib import ExitStack

import numpy as np
import concourse.bass as bass
from concourse import mybir

F32 = mybir.dt.float32
F32R = mybir.dt.float32r
ALU = mybir.AluOpType
ACTF = mybir.ActivationFunctionType
AX = mybir.AxisListType

P = 128
D = 1024
SEQ = 2048
NB = 8
TOK = SEQ + NB
TILES = SEQ // P
KT = D // P
H = 16
HD = 64
NST = 128
CONV = 1536
TAPS = 4
WIN = 2048
EPS = 1e-6
BUCKETS = 32
DILATIONS = (1, 4, 16)
MASKED = -1e30
Q0, K0, V0, Z0, G0, C0, DT0 = 0, D, 2 * D, 3 * D, 4 * D, 5 * D, 5 * D + CONV
NPROJ = DT0 + H
SLAB = 256
SHIFTS = 3 * P
BIAS_AT = ((0, 2 * P), (2 * P, 2 * P), (4 * P, P))
BIAS_W = 5 * P
RING = 4


def with_axes(ap, axes, offset=0):
    return bass.AP(tensor=ap.tensor, offset=ap.offset + offset, ap=[list(ap.ap[0])] + [list(a) for a in axes])


def spread(ap, n):
    return bass.AP(tensor=ap.tensor, offset=ap.offset, ap=[list(a) for a in ap.ap] + [[0, n]])


def repeat(ap, n):
    return bass.AP(tensor=ap.tensor, offset=ap.offset, ap=[list(ap.ap[0]), [0, n]] + [list(a) for a in ap.ap[1:]])


def rows_of(ap, n):
    return bass.AP(tensor=ap.tensor, offset=ap.offset, ap=[[0, n]] + [list(a) for a in ap.ap])


class Chain:

    def __init__(self, engine, done):
        self.engine, self.done, self.base, self.count = engine, done, 0, 0

    def __call__(self, instruction):
        self.count += 1
        instruction.then_inc(self.done, 1)
        self.engine.wait_ge(self.done, self.base + self.count)


def project(nc, io, scr):
    with ExitStack() as outer:
        def sb(ctx, name, shape, dt=F32):
            return ctx.enter_context(nc.sbuf_tensor(name, shape, dt))

        hT_hi = sb(outer, "hT_hi", [P, KT, TOK], F32R)
        hT_lo = sb(outer, "hT_lo", [P, KT, TOK], F32R)
        w_raw = sb(outer, "w_raw", [P, 2, KT, SLAB])
        w_hi = sb(outer, "w_hi", [P, 2, KT, SLAB], F32R)
        w_lo = sb(outer, "w_lo", [P, 2, KT, SLAB], F32R)
        w_loaded = [nc.alloc_semaphore(f"w_loaded{b}") for b in range(2)]
        w_cols = io["w_in"].rearrange("(k p) n -> p k n", p=P)

        def load_columns(pool, at, b, width=SLAB):
            pool.dma_start(w_raw[:, b, :, 0:width], w_cols[:, :, bass.ds(at, width)]).then_inc(w_loaded[b], 16)

        def product(pe, out, lhs_hi, lhs_lo, rhs_hi, rhs_lo):
            for k in range(KT):
                pe.matmul(out, lhs_hi(k), rhs_hi(k), start=k == 0, stop=False)
                pe.matmul(out, lhs_hi(k), rhs_lo(k), start=False, stop=False)
                last = pe.matmul(out, lhs_lo(k), rhs_hi(k), start=False, stop=k == KT - 1)
            return last

        with ExitStack() as ctx:
            xin = sb(ctx, "xin", [P, 2, D])
            hn = sb(ctx, "hn", [P, 2, D])
            norm_b = sb(ctx, "norm_b", [P, D])
            ident = sb(ctx, "ident_p", [P, P])
            ss = sb(ctx, "ss", [P, 2])
            ms = sb(ctx, "ms", [P, 2])
            rstd = sb(ctx, "rstd", [P, 2])
            mhalf = sb(ctx, "mhalf", [P, 1])
            v1_out = sb(ctx, "v1_out", [P, 2, 2 * SLAB])
            v1_bank = [ctx.enter_context(nc.psum_tensor(f"v1_bank{b}", [P, 2 * SLAB], F32)) for b in range(2)]
            hp = [ctx.enter_context(nc.psum_tensor(f"hp{b}", [P, KT, P], F32)) for b in range(2)]
            sem = lambda n: nc.alloc_semaphore(n)
            x_loaded = [sem(f"x_loaded{b}") for b in range(2)]
            const_loaded = sem("const_loaded")
            mhalf_set = sem("mhalf_set")
            squared, meaned, rooted, normed = sem("squared"), sem("meaned"), sem("rooted"), sem("normed")
            transposed, hi_done, lo_done = sem("transposed"), sem("hi_done"), sem("lo_done")
            v1_high, v1_split = sem("v1_high"), sem("v1_split")
            v1_done, v1_copied = sem("v1_done"), sem("v1_copied")
            v1_stored = [sem(f"v1_stored{b}") for b in range(2)]
            buffer_left = sem("buffer_left")
            first_high, first_split = sem("first_high"), sem("first_split")
            block = ctx.enter_context(nc.Block())

            @block.sync
            def _(sp):
                sp.dma_start(norm_b[:, :], rows_of(io["norm_w"], P)).then_inc(const_loaded, 16)
                sp.dma_start(ident[:, :], io["ident"]).then_inc(const_loaded, 16)
                for t in range(2):
                    sp.dma_start(xin[:, t, :], io["x_all"][t * P:(t + 1) * P, :]).then_inc(x_loaded[t], 16)

                def store_v1(n, b):
                    sp.wait_ge(v1_copied, n + 1)
                    sp.dma_start(io["v_out"][bass.ds(n * P, P), D - 2 * SLAB:D], v1_out[:, b, :]).then_inc(v1_stored[b], 16)

                for b in range(2):
                    sp.sem_inc(v1_stored[b], 16)
                for n in range(2, 4):
                    sp.wait_ge(normed, n - 1)
                    sp.dma_start(xin[:, n % 2, :], io["x_all"][n * P:(n + 1) * P, :]).then_inc(x_loaded[n % 2], 16)
                with sp.Fori(2, TILES // 2) as j:
                    for b in range(2):
                        sp.wait_ge(normed, 2 * j + b - 1)
                        sp.dma_start(xin[:, b, :], io["x_all"][bass.ds((2 * j + b) * P, P), :]).then_inc(x_loaded[b], 16)
                        store_v1(2 * j + b - 4, b)
                sp.wait_ge(normed, TILES - 1)
                sp.dma_start(xin[0:NB, 0, :], io["x_all"][SEQ:TOK, :]).then_inc(x_loaded[0], 16)
                for n in range(TILES - 4, TILES):
                    store_v1(n, n % 2)
                sp.wait_ge(v1_copied, TILES + 1)
                sp.dma_start(scr["proj_s"][:, Z0 - 2 * SLAB:Z0], v1_out[0:NB, 0, :]).then_inc(v1_stored[0], 16)
                sp.wait_ge(v1_stored[0], 16 * (TILES // 2 + 2))
                sp.wait_ge(v1_stored[1], 16 * (TILES // 2 + 1))

            @block.scalar
            def _(act):
                def square(n, j, b, rows=P, first=False):
                    act.wait_ge(x_loaded[b], 16 * (j + 1))
                    if not first:
                        act.wait_ge(transposed, n - 1)
                    act.activation(hn[0:rows, b, :], xin[0:rows, b, :], ACTF.Square,
                                   accum_out=ss[0:rows, b:b + 1]).then_inc(squared, 1)

                def take_hi(n, b, rows=P):
                    act.wait_ge(transposed, n + 1)
                    act.copy(hT_hi[:, :, bass.ds(n * P, rows)], hp[b][:, :, 0:rows]).then_inc(hi_done, 1)

                for b in range(2):
                    square(b, 0, b, first=True)

                def copy_v1(n, b, rows=P):
                    act.wait_ge(v1_done, n + 1)
                    act.wait_ge(v1_stored[b], 16 * (n // 2 + 1) if isinstance(n, int) else 8 * (n - b) + 16)
                    act.copy(v1_out[0:rows, b, :], v1_bank[b][0:rows, :]).then_inc(v1_copied, 1)

                take_hi(0, 0)
                for b in range(2):
                    act.wait_ge(w_loaded[b], 16)
                    act.copy(w_hi[:, b, :, :], w_raw[:, b, :, :]).then_inc(v1_high, 1)
                for n in range(2, 4):
                    square(n, 1, n % 2)
                    take_hi(n - 1, 1 - n % 2)
                with act.Fori(2, TILES // 2) as j:
                    for b in range(2):
                        n = 2 * j + b
                        square(n, j, b)
                        take_hi(n - 1, 1 - b)
                        act.wait_ge(v1_done, n - 3)
                        act.wait_ge(v1_stored[b], 16 * (j - 1))
                        act.copy(v1_out[:, b, :], v1_bank[b][:, :]).then_inc(v1_copied, 1)
                square(TILES, TILES // 2, 0, NB)
                take_hi(TILES - 1, 1)
                take_hi(TILES, 0, NB)
                for n in range(TILES - 4, TILES):
                    copy_v1(n, n % 2)
                act.wait_ge(w_loaded[0], 32)
                act.wait_ge(buffer_left, 1)
                act.copy(w_hi[:, 0, :, :], w_raw[:, 0, :, :]).then_inc(first_high, 1)
                copy_v1(TILES, 0, NB)

            @block.gpsimd
            def _(pool):
                pool.memset(mhalf[:, :], -0.5).then_inc(mhalf_set, 1)
                pool.wait_ge(mhalf_set, 1)
                for b in range(2):
                    load_columns(pool, NPROJ - 2 * SLAB + b * SLAB, b)

                def root(n, b, rows):
                    pool.wait_ge(meaned, n + 1)
                    pool.tensor_tensor(rstd[0:rows, b:b + 1], ms[0:rows, b:b + 1], mhalf[0:rows, :], ALU.pow).then_inc(rooted, 1)

                for b in range(2):
                    root(b, b, P)
                pool.wait_ge(v1_split, 2)
                for b in range(2):
                    load_columns(pool, b * SLAB, b)
                with pool.Fori(1, TILES // 2) as j:
                    for b in range(2):
                        root(2 * j + b, b, P)
                root(TILES, 0, NB)

            @block.vector
            def _(dve):
                def mean(n, b, rows=P):
                    dve.wait_ge(squared, n + 1)
                    dve.tensor_scalar(ms[0:rows, b:b + 1], ss[0:rows, b:b + 1], 1.0 / D, EPS, ALU.mult, ALU.add).then_inc(meaned, 1)

                def scale(n, b, rows=P):
                    dve.wait_ge(rooted, n + 1)
                    dve.scalar_tensor_tensor(out=hn[0:rows, b, :], in0=xin[0:rows, b, :], scalar=rstd[0:rows, b:b + 1],
                                             in1=norm_b[0:rows, :], op0=ALU.mult, op1=ALU.mult).then_inc(normed, 1)

                def take_lo(n, b, rows=P):
                    dve.wait_ge(hi_done, n + 1)
                    part = hT_hi[:, :, bass.ds(n * P, rows)]
                    dve.tensor_tensor(hT_lo[:, :, bass.ds(n * P, rows)], hp[b][:, :, 0:rows], part.bitcast(F32),
                                      ALU.subtract).then_inc(lo_done, 1)

                dve.wait_ge(const_loaded, 32)
                for b in range(2):
                    mean(b, b)
                    scale(b, b)
                for b in range(2):
                    dve.wait_ge(v1_high, b + 1)
                    dve.tensor_tensor(w_lo[:, b, :, :], w_raw[:, b, :, :], w_hi[:, b, :, :].bitcast(F32), ALU.subtract).then_inc(v1_split, 1)
                with dve.Fori(1, TILES // 2) as j:
                    for b in range(2):
                        n = 2 * j + b
                        mean(n, b)
                        take_lo(n - 2, b)
                        scale(n, b)
                mean(TILES, 0, NB)
                take_lo(TILES - 2, 0)
                scale(TILES, 0, NB)
                take_lo(TILES - 1, 1)
                take_lo(TILES, 0, NB)
                dve.wait_ge(first_high, 1)
                dve.tensor_tensor(w_lo[:, 0, :, :], w_raw[:, 0, :, :], w_hi[:, 0, :, :].bitcast(F32), ALU.subtract).then_inc(first_split, 1)

            @block.tensor
            def _(pe):
                def turn(n, b, rows, first):
                    pe.wait_ge(normed, n + 1)
                    if not first:
                        pe.wait_ge(lo_done, n - 1)
                    for k in range(KT):
                        last = pe.transpose(hp[b][:, k, 0:rows], hn[0:rows, b, k * P:(k + 1) * P], ident[0:rows, 0:rows])
                    last.then_inc(transposed, 1)

                def v1_products(n, rows=P):
                    pe.wait_ge(lo_done, n + 1)
                    if n == 0:
                        pe.wait_ge(v1_split, 2)
                    if n >= 2:
                        pe.wait_ge(v1_copied, n - 1)
                    tokens = slice(n * P, n * P + rows)
                    for b in range(2):
                        last = product(pe, v1_bank[n % 2][0:rows, b * SLAB:(b + 1) * SLAB],
                                       lambda k: hT_hi[:, k, tokens], lambda k: hT_lo[:, k, tokens],
                                       lambda k: w_hi[:, b, k, :], lambda k: w_lo[:, b, k, :])
                        if n == TILES and b == 0:
                            last.then_inc(buffer_left, 1)
                    last.then_inc(v1_done, 1)

                pe.wait_ge(const_loaded, 32)
                for n in range(TILES + 1):
                    turn(n, n % 2, P if n < TILES else NB, n < 2)
                    if n >= 2:
                        v1_products(n - 2)
                v1_products(TILES - 1)
                v1_products(TILES, NB)
                pe.wait_ge(first_split, 1)

        with ExitStack() as ctx:
            stage = sb(ctx, "stage", [P, RING, SLAB])
            stage_s = sb(ctx, "stage_s", [P, SLAB])
            squares = sb(ctx, "squares", [P, SLAB])
            scaled = sb(ctx, "scaled", [P, SLAB])
            ssq = sb(ctx, "ssq", [P, 4])
            msq = sb(ctx, "msq", [P, 4])
            rsq = sb(ctx, "rsq", [P, 4])
            mhalf = sb(ctx, "mhalf4", [P, 4])
            zero = sb(ctx, "zero", [P, 1])
            qkw = sb(ctx, "qkw", [P, 2, HD])
            banks = [ctx.enter_context(nc.psum_tensor(f"bank{r}", [P, 512], F32)) for r in range(RING)]
            bank_s = ctx.enter_context(nc.psum_tensor("bank_s", [P, SLAB], F32))
            tables = [ctx.enter_context(nc.psum_tensor(f"tab{p}", [P, 512], F32)) for p in range(3)]
            relb = sb(ctx, "relb", [BUCKETS + 1, H])
            xc_in = sb(ctx, "xc_in", [P, TAPS - 1 + SEQ])
            xc = sb(ctx, "xc", [P, SEQ])
            cw = sb(ctx, "cw", [P, CONV // P, TAPS])
            cb = sb(ctx, "cb", [P, CONV // P])
            sem = lambda n: nc.alloc_semaphore(n)
            small_loaded = sem("small_loaded")
            w_high = sem("w_high")
            w_split = sem("w_split")
            mm_done = sem("mm_done")
            norm_free = sem("norm_free")
            bank_free = sem("bank_free")
            s_done = sem("s_done")
            s_free = sem("s_free")
            s_staged = sem("s_staged")
            s_stored = sem("s_stored")
            q_sq, q_sum, q_root = sem("q_sq"), sem("q_sum"), sem("q_root")
            q_own = sem("q_own")
            staged = sem("staged")
            stored = [sem(f"stored{r}") for r in range(RING)]
            mhalf_set = sem("mhalf4_set")
            conv_step = sem("conv_step")
            conv_sum = sem("conv_sum")
            conv_act = sem("conv_act")
            raw_stored = sem("raw_stored")
            xc_stored = sem("xc_stored")
            pad_set = sem("pad_set")
            tab_loaded, tab_ones, tab_made, tab_copied, tab_stored, tab_spread = (
                sem("tab_loaded"), sem("tab_ones"), sem("tab_made"), sem("tab_copied"), sem("tab_stored"), sem("tab_spread"))
            bucket_of = xc[0:BUCKETS + 1, 0:3 * SHIFTS].rearrange("b (d u) -> b d u", d=3)
            bias_rows = xc_in[0:H, TAPS - 1:TAPS - 1 + 3 * SHIFTS].rearrange("h (d u) -> h d u", d=3)
            block = ctx.enter_context(nc.Block())

            TOK_SLABS = G0 // SLAB - 2
            CH_SLABS = (DT0 - G0) // SLAB
            PER = TILES
            GROUPS = SEQ // 512
            CPER = 2 * GROUPS
            ALL_TOK = TOK_SLABS * PER
            NORM = 2 * D // SLAB * PER
            G_TILES = D // P
            ALL = ALL_TOK + CH_SLABS * CPER
            N_SLABS = TOK_SLABS + CH_SLABS

            @block.gpsimd
            def _(pool):
                def load(s, b, width=SLAB):
                    load_columns(pool, s * SLAB, b, width)

                def split(s, b, width=SLAB, k=None):
                    ks, n = (slice(0, KT), KT) if k is None else (slice(k, k + 1), 1)
                    done = s * KT + (KT if k is None else k + 1)
                    pool.tensor_tensor(w_hi[:, b, ks, 0:width], w_raw[:, b, ks, 0:width], with_axes(zero[:, :], [[0, n], [0, width]]),
                                       ALU.add).then_inc(w_high, n)
                    pool.wait_ge(w_high, done)
                    pool.tensor_tensor(w_lo[:, b, ks, 0:width], w_raw[:, b, ks, 0:width], w_hi[:, b, ks, 0:width].bitcast(F32),
                                       ALU.subtract).then_inc(w_split, n)
                    pool.wait_ge(w_split, done)

                pool.memset(mhalf[:, :], -0.5).then_inc(mhalf_set, 1)
                pool.memset(zero[:, :], 0.0).then_inc(mhalf_set, 1)
                pool.wait_ge(mhalf_set, 2)
                pool.sem_inc(w_high, KT)
                pool.sem_inc(w_split, KT)
                load(2, 0)

                def root(n):
                    pool.wait_ge(q_sum, n + 1)
                    pool.tensor_tensor(rsq[:, :], msq[:, :], mhalf[:, :], ALU.pow).then_inc(q_root, 1)

                with pool.Fori(0, NORM // PER // 2) as j:
                    for b in range(2):
                        s = 2 * j + b
                        for k in range(KT):
                            root(s * PER + k)
                            if k == 0:
                                pool.wait_ge(w_loaded[1 - b], 16 * (j + b + 2))
                            split(s + 1, 1 - b, k=k)
                        load(s + 3, 1 - b)
                        with pool.Fori(KT, PER) as t:
                            root(s * PER + t)
                first = NORM // PER
                pool.wait_ge(s_done, first)
                pool.wait_ge(w_loaded[1], 16 * (first // 2 + 2))
                split(first + 1, 1)
                load(first + 3, 1)
                last = N_SLABS // 2 - 2
                with pool.Fori(first // 2, last) as j:
                    for b in range(2):
                        pool.wait_ge(s_done, 2 * j + b + 1)
                        pool.wait_ge(w_loaded[b], 16 * (j + 3))
                        split(2 * j + b + 2, b)
                        load(2 * j + b + 4, b)
                for b in range(2):
                    s = 2 * last + b
                    pool.wait_ge(s_done, s + 1)
                    pool.wait_ge(w_loaded[b], 16 * (last + 3))
                    split(s + 2, b)
                    if b == 0:
                        load(N_SLABS, 0, H)
                pool.wait_ge(s_done, N_SLABS - 1)
                pool.wait_ge(w_loaded[0], 16 * (N_SLABS // 2 + 2))
                split(N_SLABS, 0, H)

            @block.tensor
            def _(pe):
                def sample_rows(s, b, width=SLAB):
                    pe.wait_ge(s_free, s + 1)
                    return product(pe, bank_s[0:NB, 0:width],
                                   lambda k: hT_hi[:, k, SEQ:TOK], lambda k: hT_lo[:, k, SEQ:TOK],
                                   lambda k: w_hi[:, b, k, 0:width], lambda k: w_lo[:, b, k, 0:width])

                def token_slab(s, b, free, before):
                    pe.wait_ge(w_split, KT * (s + 1))
                    for t in range(TILES):
                        pe.wait_ge(free, s * PER + t + 1 - before)
                        product(pe, banks[t % RING][:, 0:SLAB],
                                lambda k: hT_hi[:, k, t * P:(t + 1) * P], lambda k: hT_lo[:, k, t * P:(t + 1) * P],
                                lambda k: w_hi[:, b, k, :], lambda k: w_lo[:, b, k, :]).then_inc(mm_done, 1)
                    sample_rows(s, b).then_inc(s_done, 1)

                with pe.Fori(0, NORM // PER // 2) as j:
                    for b in range(2):
                        token_slab(2 * j + b, b, norm_free, 0)
                pe.wait_ge(tab_loaded, 32)
                pe.wait_ge(tab_ones, 1)
                for p in range(3):
                    pe.matmul(tables[p][0:H, 0:SHIFTS], relb[:, :], bucket_of[:, p, :], start=True, stop=True).then_inc(tab_made, 1)
                pe.wait_ge(norm_free, RING + NORM)
                with pe.Fori(NORM // PER // 2, TOK_SLABS // 2) as j:
                    for b in range(2):
                        token_slab(2 * j + b, b, bank_free, NORM)
                with pe.Fori(0, CH_SLABS // 2) as j:
                    for b in range(2):
                        s = TOK_SLABS + 2 * j + b
                        pe.wait_ge(w_split, KT * (s + 1))
                        for m in range(CPER):
                            c, g = m // GROUPS, m % GROUPS
                            pe.wait_ge(bank_free, ALL_TOK - NORM + (2 * j + b) * CPER + m + 1)
                            product(pe, banks[m % RING][:, :],
                                    lambda k: w_hi[:, b, k, c * P:(c + 1) * P], lambda k: w_lo[:, b, k, c * P:(c + 1) * P],
                                    lambda k: hT_hi[:, k, g * 512:(g + 1) * 512],
                                    lambda k: hT_lo[:, k, g * 512:(g + 1) * 512]).then_inc(mm_done, 1)
                        sample_rows(s, b).then_inc(s_done, 1)
                pe.wait_ge(w_split, KT * (N_SLABS + 1))
                for g in range(GROUPS):
                    pe.wait_ge(bank_free, ALL - NORM + g + 1)
                    product(pe, banks[g % RING][0:H, :], lambda k: w_hi[:, 0, k, 0:H], lambda k: w_lo[:, 0, k, 0:H],
                            lambda k: hT_hi[:, k, g * 512:(g + 1) * 512],
                            lambda k: hT_lo[:, k, g * 512:(g + 1) * 512]).then_inc(mm_done, 1)
                sample_rows(N_SLABS, 0, H).then_inc(s_done, 1)

            @block.scalar
            def _(act):
                act.sem_inc(bank_free, RING)
                act.sem_inc(s_free, 1)

                def sample_out(s, width=SLAB):
                    act.wait_ge(s_done, s + 1)
                    act.wait_ge(s_stored, 16 * (s + 1))
                    act.copy(stage_s[0:NB, 0:width], bank_s[0:NB, 0:width]).then_inc(s_free, 1)

                with act.Fori(0, 8) as s:
                    with act.Fori(0, PER // RING) as u:
                        for r in range(RING):
                            n = s * PER + RING * u + r
                            act.wait_ge(mm_done, n + 1)
                            act.wait_ge(q_own, n + 1)
                            act.activation(squares[:, :], banks[r][:, 0:SLAB], ACTF.Square).then_inc(q_sq, 1)
                    sample_out(s)
                with act.Fori(8, 12) as s:
                    with act.Fori(0, PER // RING) as u:
                        for r in range(RING):
                            n = s * PER + RING * u + r
                            act.wait_ge(mm_done, n + 1)
                            act.wait_ge(stored[r], 16 * (s * (PER // RING) + u + 1))
                            act.activation(stage[:, r, :], banks[r][:, 0:SLAB], ACTF.Silu).then_inc(bank_free, 1)
                    sample_out(s)
                with act.Fori(12, 14) as s:
                    with act.Fori(0, PER // RING) as u:
                        for r in range(RING):
                            n = s * PER + RING * u + r
                            act.wait_ge(mm_done, n + 1)
                            act.wait_ge(stored[r], 16 * (s * (PER // RING) + u + 1))
                            act.copy(stage[:, r, :], banks[r][:, 0:SLAB]).then_inc(bank_free, 1)
                    sample_out(s)
                with act.Fori(0, D // SLAB) as s:
                    for c in range(2):
                        act.wait_ge(xc_stored, 16 * (2 * s + c + 1))
                        for g in range(GROUPS):
                            n = ALL_TOK + s * CPER + c * GROUPS + g
                            act.wait_ge(mm_done, n + 1)
                            act.activation(xc[:, g * 512:(g + 1) * 512], banks[g][:, :], ACTF.Silu).then_inc(bank_free, 1)
                    sample_out(TOK_SLABS + s)
                with act.Fori(0, CONV // SLAB) as s:
                    for c in range(2):
                        m = 2 * s + c
                        act.wait_ge(raw_stored, 16 * (m + 1))
                        act.wait_ge(conv_sum, m + 1)
                        for g in range(GROUPS):
                            n = ALL_TOK + G_TILES * GROUPS + m * GROUPS + g
                            act.wait_ge(mm_done, n + 1)
                            act.copy(xc_in[:, TAPS - 1 + g * 512:TAPS - 1 + (g + 1) * 512], banks[g][:, :]).then_inc(bank_free, 1)
                        act.wait_ge(conv_sum, m + 2)
                        act.activation(xc[:, :], xc[:, :], ACTF.Silu).then_inc(conv_act, 1)
                    sample_out(TOK_SLABS + D // SLAB + s)
                act.wait_ge(xc_stored, 16 * (G_TILES + CONV // P + 1))
                for g in range(GROUPS):
                    act.wait_ge(mm_done, ALL + g + 1)
                    act.copy(xc[0:H, g * 512:(g + 1) * 512], banks[g][0:H, :]).then_inc(bank_free, 1)
                sample_out(N_SLABS, H)

            @block.vector
            def _(dve):
                dve.sem_inc(norm_free, RING)
                dve.sem_inc(q_own, 1)
                dve.memset(relb[BUCKETS:BUCKETS + 1, :], 1.0).then_inc(tab_ones, 1)
                dve.memset(xc_in[:, 0:TAPS - 1], 0.0).then_inc(pad_set, 1)
                dve.wait_ge(pad_set, 1)
                dve.sem_inc(conv_sum, 1)
                dve.wait_ge(small_loaded, 64)
                dve.tensor_scalar(qkw[:, 0, :], qkw[:, 0, :], HD ** -0.5, None, ALU.mult).then_inc(pad_set, 1)
                dve.wait_ge(pad_set, 2)
                for kind in range(2):
                    with dve.Fori(4 * kind, 4 * kind + 4) as s:
                        with dve.Fori(0, PER // RING) as u:
                            for r in range(RING):
                                n = s * PER + RING * u + r
                                dve.wait_ge(q_sq, n + 1)
                                dve.tensor_reduce(ssq[:, :], squares[:, :].rearrange("p (h e) -> p h e", e=HD), AX.X,
                                                  ALU.add).then_inc(q_own, 1)
                                dve.wait_ge(q_own, n + 2)
                                dve.tensor_scalar(msq[:, :], ssq[:, :], 1.0 / HD, EPS, ALU.mult, ALU.add).then_inc(q_sum, 1)
                                dve.wait_ge(q_root, n + 1)
                                dve.tensor_tensor(scaled[:, :].rearrange("p (h e) -> p h e", e=HD),
                                                  banks[r][:, 0:SLAB].rearrange("p (h e) -> p h e", e=HD),
                                                  spread(rsq[:, :], HD), ALU.mult).then_inc(norm_free, 1)
                                dve.wait_ge(norm_free, RING + n + 1)
                                dve.wait_ge(stored[r], 16 * (s * (PER // RING) + u + 1))
                                dve.tensor_tensor(stage[:, r, :].rearrange("p (h e) -> p h e", e=HD),
                                                  scaled[:, :].rearrange("p (h e) -> p h e", e=HD),
                                                  repeat(qkw[:, kind, :], 4), ALU.mult).then_inc(staged, 1)
                for p in range(3):
                    dve.wait_ge(tab_made, p + 1)
                    dve.tensor_copy(bias_rows[:, p, :], tables[p][0:H, 0:SHIFTS]).then_inc(tab_copied, 1)
                with dve.Fori(0, CONV // P) as m:
                    dve.wait_ge(xc_stored, 16 * (G_TILES + m + 1))
                    dve.wait_ge(bank_free, RING + ALL_TOK - NORM + (G_TILES + m + 1) * GROUPS)
                    w = cw[:, bass.ds(m, 1), :].rearrange("p a t -> p (a t)")
                    dve.tensor_scalar(xc[:, :], xc_in[:, 0:SEQ], w[:, 0:1], cb[:, bass.ds(m, 1)], ALU.mult, ALU.add).then_inc(conv_step, 1)
                    for i in range(1, TAPS):
                        dve.wait_ge(conv_step, (TAPS - 1) * m + i)
                        dve.scalar_tensor_tensor(out=xc[:, :], in0=xc_in[:, i:i + SEQ], scalar=w[:, i:i + 1], in1=xc[:, :],
                                                 op0=ALU.mult, op1=ALU.add).then_inc(conv_step if i < TAPS - 1 else conv_sum, 1)

            @block.sync
            def _(sp):
                for r in range(RING):
                    sp.sem_inc(stored[r], 16)
                sp.sem_inc(s_stored, 16)
                sp.sem_inc(xc_stored, 16)
                sp.sem_inc(raw_stored, 16)
                sp.dma_start(qkw[:, 0, :], rows_of(io["q_norm_w"], P)).then_inc(small_loaded, 16)
                sp.dma_start(qkw[:, 1, :], rows_of(io["k_norm_w"], P)).then_inc(small_loaded, 16)
                sp.dma_start(cw[:, :, :], io["conv_w_t"].rearrange("(m p) t -> p m t", p=P)).then_inc(small_loaded, 16)
                sp.dma_start(cb[:, :], io["conv_b"].rearrange("(m p) -> p m", p=P),
                             allow_slow_non_contiguous=True).then_inc(small_loaded, 16)

                sp.dma_start(relb[0:BUCKETS, :], io["rel_bias"]).then_inc(tab_loaded, 16)
                sp.dma_start(bucket_of, io["onehot"].rearrange("b (d u) -> b d u", d=3)).then_inc(tab_loaded, 16)

                def store_tables():
                    sp.wait_ge(tab_copied, 3)
                    sp.dma_start(scr["rows"].rearrange("h (d u) -> h d u", d=3), bias_rows).then_inc(tab_stored, 16)
                    sp.wait_ge(tab_stored, 16)
                    for p, (at, wide) in enumerate(BIAS_AT):
                        first = p * SHIFTS + P - 1 + 2 * P - wide
                        src = bass.AP(tensor=scr["rows"].tensor, offset=first, ap=[[3 * SHIFTS, H], [-1, P], [1, wide]])
                        sp.dma_start(scr["bias"].rearrange("(h q) n -> h q n", q=P)[:, :, at:at + wide], src).then_inc(tab_spread, 16)

                def sample_store(s, ahead, width=SLAB):
                    sp.wait_ge(s_free, s + 2)
                    sp.dma_start(scr["proj_s"][:, bass.ds(s * SLAB + ahead, width)], stage_s[0:NB, 0:width]).then_inc(s_stored, 16)

                for kind, (dst, slabs, ahead) in enumerate((
                        (scr["q"], 4, 0), (io["k_out"], 4, 0), (scr["z"], 4, Z0 - 8 * SLAB), (io["v_out"], 2, V0 - 12 * SLAB))):
                    with sp.Fori(0, slabs) as s:
                        with sp.Fori(0, PER // RING) as u:
                            for r in range(RING):
                                n = (4 * kind + s) * PER + RING * u + r
                                if kind < 2:
                                    sp.wait_ge(staged, n + 1)
                                else:
                                    sp.wait_ge(bank_free, RING + n + 1 - NORM)
                                sp.dma_start(dst[bass.ds((RING * u + r) * P, P), bass.ds(s * SLAB, SLAB)],
                                             stage[:, r, :]).then_inc(stored[r], 16)
                        sample_store(4 * kind + s, ahead)
                    if kind == 1:
                        store_tables()
                with sp.Fori(0, D // SLAB) as s:
                    for c in range(2):
                        sp.wait_ge(bank_free, RING + ALL_TOK - NORM + (2 * s + c + 1) * GROUPS)
                        sp.dma_start(scr["gT"][bass.ds((2 * s + c) * P, P), :], xc[:, :]).then_inc(xc_stored, 16)
                    sample_store(TOK_SLABS + s, 2 * SLAB)
                with sp.Fori(0, CONV // SLAB) as s:
                    for c in range(2):
                        m = 2 * s + c
                        sp.wait_ge(bank_free, RING + ALL_TOK - NORM + (G_TILES + m + 1) * GROUPS)
                        sp.dma_start(io["conv_p"][bass.ds(m * P, P), :], xc_in[:, SEQ:SEQ + TAPS - 1],
                                     allow_slow_non_contiguous=True).then_inc(raw_stored, 16)
                        sp.wait_ge(conv_act, m + 1)
                        sp.dma_start(scr["xcT"][bass.ds(m * P, P), :], xc[:, :]).then_inc(xc_stored, 16)
                    sample_store(TOK_SLABS + D // SLAB + s, 2 * SLAB)
                sp.wait_ge(bank_free, RING + ALL - NORM + GROUPS)
                sp.dma_start(scr["dtT"], xc[0:H, :]).then_inc(xc_stored, 16)
                sample_store(N_SLABS, 2 * SLAB, H)
                for r in range(RING):
                    sp.wait_ge(stored[r], 16 * (TOK_SLABS * PER // RING + 1))
                sp.wait_ge(xc_stored, 16 * (G_TILES + CONV // P + 2))
                sp.wait_ge(raw_stored, 16 * (CONV // P + 1))
                sp.wait_ge(s_stored, 16 * (N_SLABS + 2))
                sp.wait_ge(tab_spread, 48)


def attention_plan():
    tiles, at = [], 0
    block = {}
    order = [(2, r, 0) for r in range(16)] + [(1, r, b) for b in range(4) for r in range(4)] + [(0, 0, t) for t in range(16)]
    for p, r, b in order:
        prev = p < 2 and b > 0
        tiles.append((p, r, b, at, prev))
        if prev:
            block[p, r, b, "prev"] = at
            at += P
        block[p, r, b, "own"] = at
        at += P
    tile_at = {(p, r, b): n for n, (p, r, b, _, _) in enumerate(tiles)}
    groups = []
    for g in range(4):
        rs = range(4 * g, 4 * g + 4)
        groups.append(dict(
            blocks=[block[2, r, 0, "own"] for r in rs], needs=tile_at[2, rs[-1], 0],
            products=[dict(v=(2, r), at=P * (r % 4), n=P, bank=g, col=P * (r % 4), start=r % 4 == 0) for r in rs]))
    for half in range(2):
        for r in range(4):
            blocks, products = [], []
            for kb in (2 * half, 2 * half + 1):
                n = 2 * P if kb < 3 else P
                products.append(dict(v=(1, 4 * kb + r), at=P * len(blocks), n=n, bank=r, col=P * kb, start=kb == 0))
                blocks.append(block[1, r, kb, "own"])
                if kb < 3:
                    blocks.append(block[1, r, kb + 1, "prev"])
            groups.append(dict(blocks=blocks, needs=tile_at[1, r, min(3, 2 * half + 2)], products=products))
    for u in range(8):
        blocks, products = [], []
        for kb in (2 * u, 2 * u + 1):
            at_own = P * len(blocks)
            blocks.append(block[0, 0, kb, "own"])
            if kb < 15:
                blocks.append(block[0, 0, kb + 1, "prev"])
            if kb % 4 < 3:
                products.append(dict(v=(0, kb), at=at_own, n=2 * P, bank=kb // 4, col=P * (kb % 4), start=kb == 0))
            else:
                products.append(dict(v=(0, kb), at=at_own, n=P, bank=kb // 4, col=3 * P, start=False))
                if kb < 15:
                    products.append(dict(v=(0, kb), at=at_own + P, n=P, bank=kb // 4 + 1, col=0, start=True))
        groups.append(dict(blocks=blocks, needs=tile_at[0, 0, min(15, 2 * u + 2)], products=products))
    return tiles, groups, at


def attend(nc, io, scr):
    tiles, groups, width = attention_plan()
    NG = len(groups)
    NT = len(tiles)
    UNITS = NT // 2
    FRONT = 8 + UNITS
    freed = []
    for n in range(UNITS):
        ends = tiles[2 * n + 2][3] if n < UNITS - 1 else width
        places = range(tiles[2 * n][3], ends, P)
        freed.append(1 + max(g for g, lot in enumerate(groups) if any(at in places for at in lot["blocks"])))
    FIRST = 8
    units_at = {g: (2 * (g - FIRST), 2 * (g - FIRST) + 1) for g in range(FIRST, NG)}
    units_at[NG] = tuple(range(2 * (NG - FIRST), UNITS))
    assert all(freed[n] <= g + 1 for g, ns in units_at.items() for n in ns)
    exps_at = {g: range(5 * (g - 10), min(5 * (g - 8), NT)) for g in range(10, 20, 2)}
    with ExitStack() as ctx:
        def sb(name, shape, dt=F32):
            return ctx.enter_context(nc.sbuf_tensor(name, shape, dt))

        ident = sb("ident_a", [P, P])
        q_in = sb("q_in", [P, TILES, P])
        k_in = sb("k_in", [P, TILES, P])
        q_st = sb("q_st", [P, SEQ], F32R)
        k_hi = sb("k_hi", [P, SEQ], F32R)
        k_lo = sb("k_lo", [P, SEQ], F32R)
        v_in = sb("v_in", [P, 3, TILES, 3 * HD])
        bias = sb("bias_sb", [P, 2, BIAS_W])
        score = sb("score", [P, 2, width])
        top = sb("top", [P, 2, NT])
        tick = sb("tick", [P, 2, NT // 2])
        tops = sb("tops_sb", [P, 3, TILES])
        top2 = sb("top2", [P, TILES])
        ntop = sb("ntop_sb", [P, 2, NT])
        turned_p = sb("turned_p", [P, 4, 512])
        acc = sb("acc", [P, 2, SEQ])
        recip = sb("recip", [P, SEQ])
        gate = sb("gate", [P, SEQ])
        den_in = sb("den_in", [P, 16])
        minus_one = sb("minus_one", [P, 16])
        front = [ctx.enter_context(nc.psum_tensor(f"front{b}", [P, 512], F32)) for b in range(2)]
        back = [ctx.enter_context(nc.psum_tensor(f"back{b}", [P, 512], F32)) for b in range(2)]
        obank = [ctx.enter_context(nc.psum_tensor(f"obank{b}", [P, 512], F32)) for b in range(4)]
        sem = lambda n: nc.alloc_semaphore(n)
        const_in = sem("const_in")
        qk_loaded = sem("qk_loaded")
        v_loaded = [sem(f"v_loaded{p}") for p in range(3)]
        ones_set = sem("ones_set")
        bias_loaded = [sem(f"bias_loaded{b}") for b in range(2)]
        gate_loaded = sem("gate_loaded")
        front_ready = sem("front_ready")
        front_free = sem("front_free")
        hi_taken = sem("hi_taken")
        top_written, top_read, top_maxed, ntop_made, ntop_written, ntop_loaded = (
            sem("top_written"), sem("top_read"), sem("top_maxed"), sem("ntop_made"), sem("ntop_written"), sem("ntop_loaded"))
        exp_done = sem("exp_done")
        back_ready = sem("back_ready")
        even_out, odd_out = sem("even_out"), sem("odd_out")
        mixed = sem("mixed")
        o_out = [sem("o1_out"), sem("o4_out"), sem("o16_out")]
        den_moved = sem("den_moved")
        recip_done = sem("recip_done")
        gated = sem("gated")
        finished = sem("finished")
        stored = sem("mix_stored")
        block = ctx.enter_context(nc.Block())

        def v_src(p, j):
            d = DILATIONS[p]
            cols = io["v_out"][:, bass.ds(j * P, P)]
            if p == 0:
                return cols.rearrange("(t i) c -> i t c", i=P)
            if p == 1:
                return cols.rearrange("(b i r) c -> i b r c", b=4, r=4)
            return cols.rearrange("(i r) c -> i r c", r=16)

        def load_v(eng, p, j):
            src = v_src(p, j)
            for side in range(2):
                at = 2 * HD * side
                dst = v_in[:, p, :, at:at + HD]
                if p == 1:
                    for b in range(4):
                        eng.dma_start(dst[:, 4 * b:4 * b + 4, :], src[:, b, :, side * HD:(side + 1) * HD]).then_inc(v_loaded[p], 16)
                else:
                    eng.dma_start(dst, src[:, :, side * HD:(side + 1) * HD]).then_inc(v_loaded[p], 16)

        V_LOADS = (2, 8, 2)

        def token_order(ap_of_row, p):
            t, o = ap_of_row.tensor, ap_of_row.offset
            if p == 0:
                return bass.AP(tensor=t, offset=o, ap=[[1, P], [P, TILES]])
            if p == 1:
                return bass.AP(tensor=t, offset=o, ap=[[4, P], [512, 4], [1, 4]])
            return bass.AP(tensor=t, offset=o, ap=[[16, P], [1, 16]])

        col_at = {0: 32, 1: 16, 2: 0}

        @block.sync
        def _(sp):
            def load_qk(h):
                for dst, src in ((q_in, scr["q"]), (k_in, io["k_out"])):
                    for twice in range(2):
                        sp.dma_start(dst[:, :, twice * HD:(twice + 1) * HD],
                                     src[:, bass.ds(h * HD, HD)].rearrange("(t i) c -> i t c", i=P)).then_inc(qk_loaded, 16)

            def load_bias(h, b):
                sp.dma_start(bias[:, b, :], scr["bias"][bass.ds(h * P, P), :]).then_inc(bias_loaded[b], 16)

            def load_gate(j):
                sp.dma_start(gate[:, :], scr["gT"][bass.ds(j * P, P), :]).then_inc(gate_loaded, 16)

            def tops_out(h, b):
                sp.wait_ge(front_free, 2 + FRONT * (h + 1))
                for p in range(3):
                    at = col_at[p]
                    sp.dma_start(token_order(scr["tops"][p:p + 1, :], p), top[:, b, at:at + 16],
                                 allow_slow_non_contiguous=True).then_inc(top_written, 16)

            def tops_back(h):
                sp.wait_ge(top_written, 48 * (h + 1))
                sp.dma_start(tops[:, :, :], scr["tops"].rearrange("d (i r) -> i d r", r=16)).then_inc(top_read, 16)

            def ntop_out(h, b):
                sp.wait_ge(ntop_made, h + 1)
                sp.dma_start(token_order(scr["ntop"], 2), ntop[:, b, 0:16]).then_inc(ntop_written, 16)

            def ntop_back(h, b):
                sp.wait_ge(ntop_written, 16 * (h + 1))
                for p in range(2):
                    at = col_at[p]
                    sp.dma_start(ntop[:, b, at:at + 16], token_order(scr["ntop"], p),
                                 allow_slow_non_contiguous=True).then_inc(ntop_loaded, 16)

            def den_out(h, b):
                den = HD * (1 - b)
                sp.wait_ge(o_out[0], 4 * h + 8)
                sp.dma_start(scr["den"][0:1, :], acc[den:den + 1, b, :]).then_inc(den_moved, 16)

            def den_back(h):
                sp.wait_ge(den_moved, 64 * h + 16)
                sp.dma_start(den_in[:, :], scr["den"][0, :].rearrange("(i r) -> i r", r=16)).then_inc(den_moved, 16)

            def recip_out(h):
                sp.wait_ge(recip_done, h + 1)
                sp.dma_start(scr["den"][1, :].rearrange("(i r) -> i r", r=16), den_in[:, :]).then_inc(den_moved, 16)

            def recip_back(h, b):
                sp.wait_ge(den_moved, 64 * h + 48)
                sp.dma_start(recip[HD * b:HD * b + HD, :], rows_of(scr["den"][1, :], HD)).then_inc(den_moved, 16)

            def store(h, b):
                sp.wait_ge(finished, h + 1)
                sp.dma_start(scr["mT"][bass.ds(h * HD, HD), :], acc[HD * b:HD * b + HD, b, :]).then_inc(stored, 16)

            def phase(m, b, pair, first=False, left=3):
                if left >= 2:
                    load_bias(m + 2, b)
                if left >= 1:
                    tops_out(m + 1, 1 - b)
                if not first:
                    den_out(m - 1, 1 - b)
                if left >= 1:
                    tops_back(m + 1)
                if b == 0 and not first:
                    sp.wait_ge(mixed, NG * m)
                    load_v(sp, 0, pair)
                if not first:
                    den_back(m - 1)
                if left >= 1:
                    ntop_out(m + 1, 1 - b)
                if left >= 1:
                    ntop_back(m + 1, 1 - b)
                if not first:
                    recip_out(m - 1)
                    recip_back(m - 1, 1 - b)
                if left >= 3:
                    sp.wait_ge(front_ready, FRONT * (m + 2) + 8)
                    load_qk(m + 3)
                if not first:
                    store(m - 1, 1 - b)
                if b == 0 and not first:
                    load_gate(pair)
                if left >= 1:
                    sp.wait_ge(ntop_loaded, 32 * (m + 2))
                if b == 1 and left >= 1:
                    for p, lots in ((2, 4), (1, 12)):
                        sp.wait_ge(mixed, NG * m + lots)
                        load_v(sp, p, pair + 1)

            sp.sem_inc(stored, 32)
            sp.dma_start(ident[:, :], io["ident"]).then_inc(const_in, 16)
            load_qk(0)
            load_bias(0, 0)
            sp.wait_ge(ones_set, 2)
            for p in (2, 1, 0):
                load_v(sp, p, 0)
            load_gate(0)
            sp.wait_ge(front_ready, 8)
            load_qk(1)
            load_bias(1, 1)
            tops_out(0, 0)
            tops_back(0)
            ntop_out(0, 0)
            ntop_back(0, 0)
            sp.wait_ge(front_ready, FRONT + 8)
            load_qk(2)
            sp.wait_ge(ntop_loaded, 32)
            phase(0, 0, 0, first=True)
            phase(1, 1, 0)
            with sp.Fori(1, H // 2 - 2) as i:
                phase(2 * i, 0, i)
                phase(2 * i + 1, 1, i)
            for m in range(H - 4, H):
                phase(m, m % 2, m // 2, left=H - 1 - m)
            m = H - 1
            den_out(m, 1)
            den_back(m)
            recip_out(m)
            recip_back(m, 1)
            store(m, 1)
            sp.wait_ge(stored, 16 * (H + 2))

        @block.gpsimd
        def _(pool):
            pool.memset(v_in[:, :, :, HD:2 * HD], 1.0).then_inc(ones_set, 1)
            pool.memset(minus_one[:, :], -1.0).then_inc(ones_set, 1)
            pool.wait_ge(ones_set, 2)

            def finish(h, b, pair):
                rows = slice(HD * b, HD * b + HD)
                pool.wait_ge(o_out[0], 4 * h + 8)
                pool.wait_ge(gate_loaded, 16 * (pair + 1))
                pool.tensor_tensor(acc[rows, b, :], acc[rows, b, :], gate[rows, :], ALU.mult).then_inc(gated, 1)
                pool.wait_ge(gated, h + 1)
                pool.wait_ge(den_moved, 64 * h + 32)
                pool.tensor_tensor(den_in[:, :], den_in[:, :], minus_one[:, :], ALU.pow).then_inc(recip_done, 1)
                pool.wait_ge(den_moved, 64 * h + 64)
                pool.tensor_tensor(acc[rows, b, :], acc[rows, b, :], recip[rows, :], ALU.mult).then_inc(finished, 1)
                pool.wait_ge(finished, h + 1)

            with pool.Fori(0, H // 2) as i:
                finish(2 * i, 0, i)
                finish(2 * i + 1, 1, i)

        @block.tensor
        def _(pe):
            def front_bank(n_before, b):
                pe.wait_ge(front_free, n_before + 1)
                return front[b]

            def turn(h, units=range(8)):
                if 0 in units:
                    pe.wait_ge(qk_loaded, 64 * (h + 1))
                for u in units:
                    c, src = u // 2, (q_in, k_in)[u % 2]
                    bank = front_bank(FRONT * h + u, u % 2)
                    for t in range(4):
                        last = pe.transpose(bank[:, t * P:(t + 1) * P],
                                            src[:, 4 * c + t, :], ident[:, :])
                    last.then_inc(front_ready, 1)

            def scores(h, units=range(UNITS)):
                if 0 in units:
                    pe.wait_ge(front_free, 2 + FRONT * h + 8)
                for u in units:
                    bank = front_bank(FRONT * h + 8 + u, u % 2)
                    for s in range(2):
                        p, r, blk, _, prev = tiles[2 * u + s]
                        d = DILATIONS[p]
                        lhs = with_axes(q_st[:, 0:1], [[d, P]], P * d * blk + r)
                        if p == 2:
                            axes, at = [[1, 2], [16, P]], r - r % 2
                        else:
                            axes, at = [[d, 2 * P]], P * d * max(blk - 1, 0) + r
                        out = bank[:, 2 * P * s:2 * P * (s + 1)]
                        pe.matmul(out, lhs, with_axes(k_hi[:, 0:1], axes, at), start=True, stop=False)
                        last = pe.matmul(out, lhs, with_axes(k_lo[:, 0:1], axes, at), start=False, stop=True)
                    last.then_inc(front_ready, 1)

            def mix(h, b, pair, more=True):
                vcols = slice(HD * b, HD * b + P)

                def turn_lot(g):
                    lot = groups[g]
                    pe.wait_ge(exp_done, NT * h + lot["needs"] + 1)
                    if g >= 2:
                        pe.wait_ge((even_out, odd_out)[g % 2], NG // 2 * h + g // 2)
                    for n, at in enumerate(lot["blocks"]):
                        last = pe.transpose(back[g % 2][:, n * P:(n + 1) * P], score[:, b, at:at + P], ident[:, :])
                    last.then_inc(back_ready, 1)

                def multiply(g):
                    pe.wait_ge((even_out, odd_out)[g % 2], NG // 2 * h + g // 2 + 1)
                    lot = groups[g]
                    if g in (0, 4, 12):
                        pe.wait_ge(v_loaded[{0: 2, 4: 1, 12: 0}[g]], 16 * V_LOADS[{0: 2, 4: 1, 12: 0}[g]] * (pair + 1))
                    for m in lot["products"]:
                        p = m["v"][0]
                        if m["start"]:
                            if p < 2:
                                pe.wait_ge(o_out[p + 1], 4 * h + m["bank"] + 1)
                            else:
                                pe.wait_ge(o_out[0], 4 * h + m["bank"] + 1)
                        last = pe.matmul(obank[m["bank"]][:, m["col"]:m["col"] + m["n"]], v_in[:, p, m["v"][1], vcols],
                                         turned_p[:, g % 4, m["at"]:m["at"] + m["n"]], start=m["start"], stop=True,
                                         skip_group_check=True)
                    last.then_inc(mixed, 1)

                for g in range(NG + 1):
                    if g < NG:
                        turn_lot(g)
                    if more and g < 8:
                        turn(h + 2, (g,))
                    if g >= 1:
                        multiply(g - 1)
                    if more:
                        scores(h + 2, units_at.get(g, ()))

            pe.wait_ge(const_in, 16)
            for h in range(2):
                turn(h)
                scores(h)
            with pe.Fori(0, H // 2 - 1) as i:
                mix(2 * i, 0, i)
                mix(2 * i + 1, 1, i)
            mix(H - 2, 0, H // 2 - 1, more=False)
            mix(H - 1, 1, H // 2 - 1, more=False)

        @block.vector
        def _(dve):
            dve.sem_inc(front_free, 2)
            dve.sem_inc(o_out[0], 4)

            def turn(h, units=range(8)):
                for u in units:
                    c, bank = u // 2, front[u % 2]
                    cols = slice(512 * c, 512 * (c + 1))
                    dve.wait_ge(hi_taken, 8 * h + u + 1)
                    if u % 2 == 0:
                        dve.tensor_tensor(q_st[HD:P, cols], bank[HD:P, :], q_st[HD:P, cols].bitcast(F32),
                                          ALU.subtract).then_inc(front_free, 1)
                    else:
                        dve.tensor_tensor(k_lo[:, cols], bank[:, :], k_hi[:, cols].bitcast(F32), ALU.subtract).then_inc(front_free, 1)

            def scores(h, b, pair_use, units=range(UNITS), beside=None):
                if 0 in units:
                    dve.wait_ge(bias_loaded[b], 16 * (pair_use + 1))
                for u in units:
                    if beside is not None:
                        dve.wait_ge(back_ready, NG * beside + freed[u])
                    dve.wait_ge(front_ready, FRONT * h + 8 + u + 1)
                    dve.memset(tick[:, b, u:u + 1], 0.0)
                    for s in range(2):
                        n = 2 * u + s
                        p, r, blk, at, prev = tiles[n]
                        b_at, b_w = BIAS_AT[p]
                        w = 2 * P if prev else P
                        skip = P if p == 2 and r % 2 else 0
                        last = dve.tensor_tensor_reduce(
                            out=score[:, b, at:at + w], in0=front[u % 2][:, 2 * P * s + skip:2 * P * s + skip + w],
                            in1=bias[:, b, b_at + b_w - w:b_at + b_w], scale=1.0, scalar=-3e38, op0=ALU.add, op1=ALU.max,
                            accum_out=top[:, b, n:n + 1])
                    last.then_inc(front_free, 1)

            def meet(h, b):
                dve.wait_ge(top_read, 16 * (h + 1))
                dve.tensor_reduce(top2[:, :], tops[:, :, :].rearrange("p d r -> p r d"), AX.X, ALU.max).then_inc(top_maxed, 1)
                dve.wait_ge(top_maxed, h + 1)
                dve.tensor_scalar(ntop[:, b, 0:16], top2[:, :], -1.0, None, ALU.mult).then_inc(ntop_made, 1)

            def mix(h, b, pair=0, more=True, meets=True):
                for g in range(NG + 1):
                    if g == 4 and meets:
                        meet(h + 1, 1 - b)
                    if g < NG and g % 2 == 0:
                        dve.wait_ge(back_ready, NG * h + g + 1)
                        if g >= 4:
                            dve.wait_ge(mixed, NG * h + g - 3)
                        n = P * len(groups[g]["blocks"])
                        dve.tensor_copy(turned_p[:, g % 4, 0:n], back[0][:, 0:n]).then_inc(even_out, 1)
                    if more and g < 8:
                        turn(h + 2, (g,))
                    if 10 <= g <= 13:
                        r = g - 10
                        dve.wait_ge(mixed, NG * h + 8 + r + 1)
                        dve.wait_ge(o_out[2], 4 * h + 4)
                        sl = acc[:, b, :].rearrange("p (i r) -> p i r", r=4)[:, :, r]
                        dve.tensor_tensor(sl, sl, obank[r][:, :], ALU.add).then_inc(o_out[1], 1)
                    if g in (15, 17, 19, 20):
                        r = {15: 0, 17: 1, 19: 2, 20: 3}[g]
                        dve.wait_ge(mixed, NG * h + 12 + 2 * r + 2)
                        if r == 0:
                            dve.wait_ge(o_out[1], 4 * h + 4)
                        cols = slice(512 * r, 512 * (r + 1))
                        dve.tensor_tensor(acc[:, b, cols], acc[:, b, cols], obank[r][:, :], ALU.add).then_inc(o_out[0], 1)
                    if more:
                        scores(h + 2, b, pair + 1, units_at.get(g, ()), beside=h)

            turn(0)
            scores(0, 0, 0)
            turn(1)
            scores(1, 1, 0, range(8))
            meet(0, 0)
            scores(1, 1, 0, range(8, UNITS))
            with dve.Fori(0, H // 2 - 1) as i:
                mix(2 * i, 0, i)
                mix(2 * i + 1, 1, i)
            mix(H - 2, 0, more=False)
            mix(H - 1, 1, more=False, meets=False)

        @block.scalar
        def _(act):
            def turn(h, units=range(8)):
                for u in units:
                    c, bank = u // 2, front[u % 2]
                    cols = slice(512 * c, 512 * (c + 1))
                    act.wait_ge(front_ready, FRONT * h + u + 1)
                    act.copy((q_st, k_hi)[u % 2][:, cols], bank[:, :]).then_inc(hi_taken, 1)

            def exps(h, b, which=range(NT)):
                if 0 in which:
                    act.wait_ge(ntop_loaded, 32 * (h + 1))
                    act.wait_ge(ntop_made, h + 1)
                for n in which:
                    p, r, blk, at, prev = tiles[n]
                    w = 2 * P if prev else P
                    act.activation(score[:, b, at:at + w], score[:, b, at:at + w], ACTF.Exp,
                                   bias=ntop[:, b, n:n + 1]).then_inc(exp_done, 1)

            def mix(h, b, more=True, next_exps=True):
                for g in range(NG + 1):
                    if next_exps:
                        exps(h + 1, 1 - b, exps_at.get(g, ()))
                    if g % 2 == 1:
                        act.wait_ge(back_ready, NG * h + g + 1)
                        if g >= 4:
                            act.wait_ge(mixed, NG * h + g - 3)
                        n = P * len(groups[g]["blocks"])
                        act.copy(turned_p[:, g % 4, 0:n], back[1][:, 0:n]).then_inc(odd_out, 1)
                    if more and g < 8:
                        turn(h + 2, (g,))
                    if 2 <= g <= 5:
                        r = g - 2
                        act.wait_ge(mixed, NG * h + r + 1)
                        if r == 0:
                            act.wait_ge(stored, 16 * (h + 1))
                        dst = acc[:, b, :].rearrange("p (i r) -> p r i", r=16)[:, 4 * r:4 * r + 4, :]
                        act.copy(dst, obank[r][:, :].rearrange("p (r i) -> p r i", r=4)).then_inc(o_out[2], 1)

            turn(0)
            turn(1)
            exps(0, 0)
            with act.Fori(0, H // 2 - 1) as i:
                mix(2 * i, 0)
                mix(2 * i + 1, 1)
            mix(H - 2, 0, more=False)
            mix(H - 1, 1, more=False, next_exps=False)



class Chunk:

    def __init__(self, q, r):
        self.q, self.r = q + r // 4, r % 4
        self.n = 4 * self.q + self.r
        self.b = self.r % 2
        self.pair = 2 * self.q + self.r // 2

    def plus(self, k):
        return Chunk(self.q, self.r + k)


def scan(nc, io, scr):
    NC = SEQ // P
    G = 2
    HG = H // G
    SPLIT = P // H
    with ExitStack() as ctx:
        def sb(name, shape, dt=F32):
            return ctx.enter_context(nc.sbuf_tensor(name, shape, dt))

        ident = sb("ident_s", [P, P])
        tri = sb("tri_sb", [P, P])
        dt_raw = sb("dt_raw", [P, 2 * P])
        step_h = sb("step_h", [P, 2 * P])
        cum_h = sb("cum_h", [P, 2 * P])
        work_a = sb("work_a", [P, 2 * P])
        work_b = sb("work_b", [P, 2 * P])
        h_small = sb("h_small", [P, 4])
        d_col = sb("d_col", [P, KT])
        d_diag = sb("d_diag", [P, KT, P])
        norm_b = sb("norm_b_s", [P, D])
        tok = sb("tok", [P, 2, NC, H])
        xc = sb("xc_chunk", [P, 4, CONV // P, P])
        zt = sb("zt", [P, 2, D])
        cum_all = sb("cum_all", [P, 2, H, P])
        x_tok = sb("x_tok", [P, 2, D])
        b_tok = sb("b_tok", [P, 2, G * P])
        masked = sb("masked", [P, G, P])
        decay = sb("decay", [P, 2, H, P])
        pre = sb("pre", [P, 2, 3, H])
        fac = sb("fac", [P, 2, 3, H])
        cum_now = sb("cum_now", [P, 2, H])
        zero = sb("zero_s", [P, 1])
        xdt = sb("xdt", [P, 2, D])
        xend = sb("xend", [P, 2, D])
        part = sb("part", [P, D])
        u = sb("u", [P, 2, D])
        state = sb("state", [P, D])
        sq = sb("sq_s", [P, D])
        small = sb("small_s", [P, 3])
        mhalf = sb("mhalf_s", [P, 1])
        out_t = sb("out_t", [P, 2, KT, P])
        XA = ctx.enter_context(nc.psum_tensor("XA", [P, D], F32))
        MX = ctx.enter_context(nc.psum_tensor("MX", [P, 512], F32))
        OFF = ctx.enter_context(nc.psum_tensor("OFF", [P, D], F32))
        DG = ctx.enter_context(nc.psum_tensor("DG", [P, D], F32))
        sem = lambda n: nc.alloc_semaphore(n)
        small_in, mhalf_set = sem("small_in_s"), sem("mhalf_set_s")
        pro_act, pro_dve, pro_pe, pro_ok, cum_out, diag_made = (
            sem("pro_act"), sem("pro_dve"), sem("pro_pe"), sem("pro_ok"), sem("cum_out"), sem("diag_made"))
        xc_in = [sem(f"xc_in_s{r}") for r in range(4)]
        z_in, cum_in = ([sem(f"{n}{b}") for b in range(2)] for n in ("z_in_s", "cum_in_s"))
        x_turned = sem("x_turned")
        mx_ready = sem("mx_ready")
        x_taken = sem("x_taken")
        b_taken = sem("b_taken")
        cb_masked = sem("cb_masked")
        now_ready = sem("now_ready")
        last_kept = sem("last_kept")
        seg_made = sem("seg_made")
        seg_ready = sem("seg_ready")
        seg_exp = sem("seg_exp")
        fac_ready, pre_ready = sem("fac_ready"), sem("pre_ready")
        dve_a = sem("dve_a")
        state_decayed = sem("state_decayed")
        decay_ready = sem("decay_ready")
        xdt_ready, xend_ready = sem("xdt_ready"), sem("xend_ready")
        off_ready, diag_ready, new_ready = sem("off_ready"), sem("diag_ready"), sem("new_ready")
        off_out = sem("off_out")
        diag_out = sem("diag_out")
        state_ready = sem("state_ready")
        gated, squared, meaned, rooted, normed = (
            sem("gated_s"), sem("squared_s"), sem("meaned_s"), sem("rooted_s"), sem("normed_s"))
        u_turned = sem("u_turned")
        u_taken = sem("u_taken")
        stored = [sem(f"stored_s{b}") for b in range(2)]
        ssm_stored = sem("ssm_stored")
        block = ctx.enter_context(nc.Block())

        heads = lambda ap: ap.rearrange("p (h e) -> p h e", e=HD)
        last_chunk = Chunk(NC // 4 - 1, 3)

        def run(engine, step):
            step(Chunk(0, 0), first=True)
            with engine.Fori(0, NC // 4 - 1) as q:
                for r in range(4):
                    step(Chunk(q, 1 + r))
            for r in (1, 2, 3):
                step(Chunk(NC // 4 - 1, r), last=r == 3)

        @block.sync
        def _(sp):
            def load_xc(c):
                sp.dma_start(xc[:, c.r, :, :], scr["xcT"].rearrange("(m p) t -> p m t", p=P)[:, :, bass.ds(c.n * P, P)]).then_inc(xc_in[c.r], 16)

            def load_z(c):
                sp.dma_start(zt[:, c.b, :], scr["z"][bass.ds(c.n * P, P), :]).then_inc(z_in[c.b], 16)

            def load_cum(c):
                row = scr["cum"][:, bass.ds(c.n * P, P)]
                sp.dma_start(cum_all[:, c.b, :, :], bass.AP(tensor=row.tensor, offset=row.offset, ap=[[0, P], [SEQ, H], [1, P]],
                                                            )).then_inc(cum_in[c.b], 16)

            def store(c):
                sp.wait_ge(u_taken, c.n + 2)
                sp.dma_start(scr["mT"][D:2 * D, :].rearrange("(m p) t -> p m t", p=P)[:, :, bass.ds(c.n * P, P)],
                             out_t[:, c.b, :, :]).then_inc(stored[c.b], 16)

            def per_head(vector):
                return bass.AP(tensor=vector.tensor, offset=0, ap=[[1, H], [0, SPLIT], [1, 1]])

            for b in range(2):
                sp.sem_inc(stored[b], 16)
            sp.dma_start(dt_raw[:, :], scr["dtT"].rearrange("h (g t) -> (h g) t", t=2 * P)).then_inc(small_in, 16)
            sp.dma_start(h_small[:, 0:1], per_head(io["dt_bias"])).then_inc(small_in, 16)
            sp.dma_start(h_small[:, 1:2], per_head(io["a_log"])).then_inc(small_in, 16)
            sp.dma_start(ident[:, :], io["ident"]).then_inc(small_in, 16)
            sp.dma_start(tri[:, :], io["tri"]).then_inc(small_in, 16)
            for half in range(2):
                sp.dma_start(d_col[half * HD:(half + 1) * HD, :],
                             bass.AP(tensor=io["d_skip"].tensor, offset=half, ap=[[0, HD], [2, KT], [1, 1]]),
                             allow_slow_non_contiguous=True).then_inc(small_in, 16)
            sp.dma_start(norm_b[:, :], rows_of(io["ssd_norm_w"], P)).then_inc(small_in, 16)
            load_xc(Chunk(0, 0))
            sp.wait_ge(pro_ok, 1)
            sp.dma_start(scr["cum"].rearrange("h (g t) -> (h g) t", t=2 * P), cum_h[:, :]).then_inc(cum_out, 16)
            sp.wait_ge(cum_out, 16)
            load_cum(Chunk(0, 0))
            load_xc(Chunk(0, 1))
            load_cum(Chunk(0, 1))
            for n in range(2):
                load_z(Chunk(0, n))
                load_xc(Chunk(0, n + 2))

            def next_cum(c):
                sp.wait_ge(decay_ready, c.n - 1)
                load_cum(c)

            def step(c, cum_too=True, xc_too=True, store_too=True, z_too=True):
                if cum_too:
                    next_cum(c.plus(3))
                if xc_too:
                    sp.wait_ge(diag_ready, c.n + 1)
                    load_xc(c.plus(4))
                if store_too:
                    store(c.plus(-1))
                if z_too:
                    sp.wait_ge(gated, c.n + 1)
                    load_z(c.plus(2))

            next_cum(Chunk(0, 2))
            step(Chunk(0, 0), store_too=False)
            with sp.Fori(0, NC // 4 - 2) as q:
                for r in range(4):
                    step(Chunk(q, 1 + r))
            for r in range(1, 8):
                step(Chunk(NC // 4 - 2, r), cum_too=r < 5, xc_too=r < 4, z_too=r < 6)
            store(last_chunk)
            sp.wait_ge(state_ready, NC + 1)
            sp.dma_start(io["ssm_p"], state[:, :]).then_inc(ssm_stored, 16)
            sp.wait_ge(ssm_stored, 16)
            for b in range(2):
                sp.wait_ge(stored[b], 16 * (NC // 2 + 1))

        @block.scalar
        def _(act):
            act.wait_ge(small_in, 16 * 8)
            act.activation(h_small[:, 2:3], h_small[:, 1:2], ACTF.Exp).then_inc(pro_act, 1)
            act.wait_ge(pro_dve, 2)
            act.activation(work_b[:, :], work_b[:, :], ACTF.Exp, scale=-1.0).then_inc(pro_act, 1)
            act.wait_ge(pro_dve, 3)
            act.activation(step_h[:, :], work_a[:, :], ACTF.Ln).then_inc(pro_act, 1)
            act.sem_inc(u_taken, 1)

            def prepare(c):
                act.wait_ge(x_turned, c.n + 1)
                act.copy(x_tok[:, c.b, :], XA[:, :]).then_inc(x_taken, 1)
                act.wait_ge(mx_ready, c.n + 1)
                act.copy(b_tok[:, c.b, :], MX[:, 0:G * P]).then_inc(b_taken, 1)
                act.wait_ge(pre_ready, c.n + 1)
                act.activation(fac[:, c.b, :, :], pre[:, c.b, :, :], ACTF.Exp).then_inc(fac_ready, 1)
                act.wait_ge(seg_ready, c.n + 1)
                act.activation(cum_all[:, c.b, :, :], cum_all[:, c.b, :, :], ACTF.Exp).then_inc(seg_exp, 1)

            def finish(c):
                act.wait_ge(gated, c.n + 1)
                act.activation(sq[:, :], u[:, c.b, :], ACTF.Square, accum_out=small[:, 0:1]).then_inc(squared, 1)
                act.wait_ge(u_turned, c.n + 3)
                act.wait_ge(stored[c.b], 16 * (c.pair + 1))
                act.copy(out_t[:, c.b, :, :], OFF[:, :].rearrange("p (m t) -> p m t", t=P)).then_inc(u_taken, 1)

            def step(c, first=False, last=False):
                if not last:
                    prepare(c.plus(1))
                if not first:
                    finish(c.plus(-1))

            prepare(Chunk(0, 0))
            run(act, step)
            finish(last_chunk)

        @block.gpsimd
        def _(pool):
            pool.memset(mhalf[:, :], -0.5).then_inc(mhalf_set, 1)
            pool.memset(state[:, :], 0.0).then_inc(mhalf_set, 1)
            pool.memset(zero[:, :], 0.0).then_inc(mhalf_set, 1)
            pool.wait_ge(mhalf_set, 3)

            def differences(c):
                pool.wait_ge(cum_in[c.b], 16 * (c.pair + 1))
                last = cum_all[:, c.b, :, P - 1:P].rearrange("p h o -> p (h o)")
                pool.tensor_tensor(pre[:, c.b, 2, :], last, with_axes(zero[:, :], [[0, H]]), ALU.add).then_inc(last_kept, 1)
                pool.wait_ge(last_kept, c.n + 1)
                pool.wait_ge(now_ready, c.n + 1)
                pool.tensor_tensor(cum_all[:, c.b, :, :], cum_all[:, c.b, :, :], spread(cum_now[:, c.b, :], P), ALU.subtract).then_inc(seg_made, 1)
                pool.wait_ge(seg_made, c.n + 1)

            def prepare(c):
                pool.wait_ge(xdt_ready, c.n + 1)
                pool.wait_ge(fac_ready, c.n + 1)
                pool.tensor_tensor(heads(xend[:, c.b, :]), heads(xdt[:, c.b, :]), spread(fac[:, c.b, 0, :], HD), ALU.mult).then_inc(xend_ready, 1)
                pool.wait_ge(xend_ready, c.n + 1)

            def gate(c):
                pool.wait_ge(diag_out, c.n + 1)
                pool.wait_ge(z_in[c.b], 16 * (c.pair + 1))
                pool.wait_ge(u_turned, c.n + 1)
                pool.tensor_tensor(u[:, c.b, :], part[:, :], zt[:, c.b, :], ALU.mult).then_inc(gated, 1)
                pool.wait_ge(gated, c.n + 1)

            def decay_state(c):
                pool.wait_ge(off_ready, c.n + 1)
                pool.wait_ge(fac_ready, c.n + 1)
                pool.tensor_tensor(heads(state[:, :]), heads(state[:, :]), spread(fac[:, c.b, 2, :], HD), ALU.mult).then_inc(state_decayed, 1)
                pool.wait_ge(state_decayed, c.n + 1)

            def root(c):
                pool.wait_ge(meaned, c.n + 1)
                pool.tensor_tensor(small[:, 2:3], small[:, 1:2], mhalf[:, :], ALU.pow).then_inc(rooted, 1)
                pool.wait_ge(rooted, c.n + 1)

            def step(c, first=False, last=False):
                if not first:
                    gate(c.plus(-1))
                decay_state(c)
                if not last:
                    prepare(c.plus(1))
                if not first:
                    root(c.plus(-1))
                if not isinstance(c.n, int) or c.n + 2 < NC:
                    differences(c.plus(2))

            for n in range(2):
                differences(Chunk(0, n))
            prepare(Chunk(0, 0))
            run(pool, step)
            gate(last_chunk)
            root(last_chunk)

        @block.vector
        def _(dve):
            chain = Chain(dve, pro_dve)
            dve.wait_ge(small_in, 16 * 8)
            chain(dve.tensor_scalar(dt_raw[:, :], dt_raw[:, :], h_small[:, 0:1], None, ALU.add))
            chain(dve.scalar_tensor_tensor(out=work_b[:, :], in0=dt_raw[:, :], scalar=-1.0, in1=dt_raw[:, :],
                                           op0=ALU.mult, op1=ALU.max))
            dve.wait_ge(pro_act, 2)
            chain(dve.tensor_scalar(work_a[:, :], work_b[:, :], 1.0, None, ALU.add))
            dve.wait_ge(pro_act, 3)
            chain(dve.tensor_tensor(step_h[:, :], step_h[:, :], work_b[:, :], ALU.mult))
            chain(dve.tensor_scalar(work_a[:, :], work_a[:, :], -1.0, None, ALU.add))
            chain(dve.scalar_tensor_tensor(out=cum_h[:, :], in0=work_a[:, :], scalar=0.0, in1=work_b[:, :],
                                           op0=ALU.is_equal, op1=ALU.mult))
            chain(dve.tensor_scalar(work_a[:, :], work_a[:, :], 1e-30, None, ALU.max))
            chain(dve.reciprocal(work_a[:, :], work_a[:, :]))
            chain(dve.tensor_tensor(step_h[:, :], step_h[:, :], work_a[:, :], ALU.mult))
            chain(dve.tensor_tensor(step_h[:, :], step_h[:, :], cum_h[:, :], ALU.add))
            chain(dve.scalar_tensor_tensor(out=step_h[:, :], in0=dt_raw[:, :], scalar=0.0, in1=step_h[:, :],
                                           op0=ALU.max, op1=ALU.add))
            chain(dve.tensor_scalar(h_small[:, 2:3], h_small[:, 2:3], -1.0, None, ALU.mult))
            chain(dve.tensor_scalar(work_b[:, :], step_h[:, :], h_small[:, 2:3], None, ALU.mult))
            chain(dve.memset(work_a[:, :], 1.0))
            chain(dve.memset(work_a[:, :].rearrange("h (c l) -> h c l", l=P)[:, :, 0:1], 0.0))
            dve.tensor_tensor_scan(cum_h[:, :], work_a[:, :], work_b[:, :], 0.0, ALU.mult, ALU.add).then_inc(pro_ok, 1)
            dve.tensor_tensor(d_diag[:, :, :], spread(d_col[:, :], P), repeat(ident[:, :], KT), ALU.mult).then_inc(diag_made, 1)
            dve.wait_ge(pro_pe, 1)
            turned = MX[:, :].rearrange("p (a i h g) -> p a i g h", a=2, i=2, h=H)
            for a in range(2):
                for i in range(2):
                    dve.tensor_copy(tok[:, a, :, :].rearrange("p (g i) h -> p i g h", i=2)[:, i], turned[:, a, i]).then_inc(pro_ok, 1)
            dve.wait_ge(pro_ok, 5)
            dve.wait_ge(mhalf_set, 3)
            dve.sem_inc(state_ready, 1)

            def copy_now(c):
                dve.tensor_scalar(cum_now[:, c.b, :], tok[:, 1, bass.ds(c.n, 1), :].rearrange("p o h -> p (o h)"), 1.0, None,
                                  ALU.mult).then_inc(now_ready, 1)
                dve.wait_ge(now_ready, c.n + 1)

            def prepare(c):
                b = c.b
                step = tok[:, 0, bass.ds(c.n, 1), :].rearrange("p o h -> p (o h)")
                if not isinstance(c.n, int) or c.n + 1 < NC:
                    copy_now(c.plus(1))
                dve.wait_ge(seg_made, c.n + 1)
                a = Chain(dve, dve_a)
                a.base = 3 * c.n
                a(dve.tensor_scalar(pre[:, b, 0, :], cum_all[:, b, :, P - 1:P].rearrange("p h o -> p (h o)"), 1.0, None, ALU.mult))
                a(dve.tensor_scalar(pre[:, b, 1, :], cum_now[:, b, :], 1.0, None, ALU.mult))
                dve.sem_inc(pre_ready, 1)
                dve.tensor_scalar(cum_all[:, b, :, :], cum_all[:, b, :, :], 0.0, None, ALU.min).then_inc(seg_ready, 1)
                dve.wait_ge(x_taken, c.n + 1)
                dve.tensor_tensor(heads(xdt[:, b, :]), heads(x_tok[:, b, :]), spread(step, HD), ALU.mult).then_inc(xdt_ready, 1)
                dve.wait_ge(b_taken, c.n + 1)
                dve.tensor_tensor(masked[:, :, :], MX[:, G * P:].rearrange("p (g l) -> p g l", g=G), repeat(tri[:, :], G),
                                  ALU.mult).then_inc(cb_masked, 1)
                dve.wait_ge(cb_masked, c.n + 1)
                dve.wait_ge(seg_exp, c.n + 1)
                for g in range(G):
                    hs = slice(HG * g, HG * (g + 1))
                    ins = dve.tensor_tensor(decay[:, b, hs, :], cum_all[:, b, hs, :], repeat(masked[:, g, :], HG), ALU.mult)
                    if g == 0:
                        a(ins)
                    else:
                        ins.then_inc(decay_ready, 1)
                dve.wait_ge(decay_ready, c.n + 1)
                assert a.count == 3

            def apply(c, first=False):
                b = c.b
                dve.wait_ge(fac_ready, c.n + 1)
                dve.wait_ge(off_ready, c.n + 1)
                if not first:
                    dve.wait_ge(gated, c.n)
                dve.tensor_tensor(heads(part[:, :]), heads(OFF[:, :]), spread(fac[:, b, 1, :], HD), ALU.mult).then_inc(off_out, 1)
                dve.wait_ge(state_decayed, c.n + 1)
                dve.wait_ge(new_ready, c.n + 1)
                dve.tensor_tensor(state[:, :], XA[:, :], state[:, :], ALU.add).then_inc(state_ready, 1)
                dve.wait_ge(off_out, c.n + 1)
                dve.wait_ge(diag_ready, c.n + 1)
                dve.tensor_tensor(part[:, :], DG[:, :], part[:, :], ALU.add).then_inc(diag_out, 1)

            def finish(c):
                dve.wait_ge(squared, c.n + 1)
                dve.tensor_scalar(small[:, 1:2], small[:, 0:1], 1.0 / D, EPS, ALU.mult, ALU.add).then_inc(meaned, 1)
                dve.wait_ge(rooted, c.n + 1)
                dve.scalar_tensor_tensor(out=u[:, c.b, :], in0=u[:, c.b, :], scalar=small[:, 2:3], in1=norm_b[:, :],
                                         op0=ALU.mult, op1=ALU.mult).then_inc(normed, 1)

            def step(c, first=False, last=False):
                if not last:
                    prepare(c.plus(1))
                if not first:
                    finish(c.plus(-1))
                apply(c, first)

            copy_now(Chunk(0, 0))
            prepare(Chunk(0, 0))
            run(dve, step)
            finish(last_chunk)

        @block.tensor
        def _(pe):
            pe.wait_ge(small_in, 16 * 8)
            pe.wait_ge(pro_ok, 1)
            for a, src in enumerate((step_h, cum_h)):
                for i in range(2):
                    at = (2 * a + i) * P
                    last = pe.transpose(MX[:, at:at + P], src[:, i * P:(i + 1) * P], ident[:, :])
            last.then_inc(pro_pe, 1)
            pe.sem_inc(u_turned, 2)
            pe.wait_ge(pro_ok, 5)
            pe.wait_ge(diag_made, 1)

            def prepare(c, first=False):
                pe.wait_ge(xc_in[c.r], 16 * (c.q + 1))
                if not first:
                    pe.wait_ge(x_taken, c.n)
                    pe.wait_ge(state_ready, c.n)
                for m in range(KT):
                    last = pe.transpose(XA[:, m * P:(m + 1) * P], xc[:, c.r, m, :], ident[:, :])
                last.then_inc(x_turned, 1)
                if not first:
                    pe.wait_ge(cb_masked, c.n)
                for g in range(G):
                    pe.transpose(MX[:, g * P:(g + 1) * P], xc[:, c.r, KT + g, :], ident[:, :])
                for g in range(G):
                    last = pe.matmul(MX[:, (G + g) * P:(G + g + 1) * P], xc[:, c.r, KT + g, :], xc[:, c.r, KT + G + g, :],
                                     start=True, stop=True)
                last.then_inc(mx_ready, 1)

            def apply(c, first=False, last=False):
                b = c.b
                pe.wait_ge(state_ready, c.n + 1)
                if not first:
                    pe.wait_ge(off_out, c.n)
                    pe.wait_ge(u_taken, c.n)
                for g in range(G):
                    done = pe.matmul(OFF[:, g * 512:(g + 1) * 512], xc[:, c.r, KT + G + g, :], state[:, g * 512:(g + 1) * 512],
                                     start=True, stop=True)
                done.then_inc(off_ready, 1)
                pe.wait_ge(x_taken, NC if last else c.n + 2)
                pe.wait_ge(b_taken, c.n + 1)
                pe.wait_ge(xend_ready, c.n + 1)
                for g in range(G):
                    done = pe.matmul(XA[:, g * 512:(g + 1) * 512], b_tok[:, b, g * P:(g + 1) * P], xend[:, b, g * 512:(g + 1) * 512],
                                     start=True, stop=True)
                done.then_inc(new_ready, 1)
                if not first:
                    pe.wait_ge(diag_out, c.n)
                pe.wait_ge(decay_ready, c.n + 1)
                for m in range(KT):
                    pe.matmul(DG[:, m * P:(m + 1) * P], xc[:, c.r, m, :], d_diag[:, m, :], start=m % 4 == 0, stop=False,
                              skip_group_check=True)
                    for h in (2 * m, 2 * m + 1):
                        done = pe.matmul(DG[:, h * HD:(h + 1) * HD], decay[:, b, h, :], xdt[:, b, h * HD:(h + 1) * HD],
                                         start=False, stop=True, skip_group_check=True)
                done.then_inc(diag_ready, 1)

            def finish(c):
                pe.wait_ge(off_out, NC if isinstance(c.n, int) and c.n == NC - 1 else c.n + 2)
                pe.wait_ge(normed, c.n + 1)
                for m in range(KT):
                    done = pe.transpose(OFF[:, m * P:(m + 1) * P], u[:, c.b, m * P:(m + 1) * P], ident[:, :])
                done.then_inc(u_turned, 1)

            def step(c, first=False, last=False):
                if not last:
                    prepare(c.plus(1))
                apply(c, first, last)
                if not first:
                    finish(c.plus(-1))

            prepare(Chunk(0, 0), first=True)
            run(pe, step)
            pe.wait_ge(u_taken, NC)
            finish(last_chunk)


def decode(nc, io, scr):
    V_BUFS = 4
    BH = NB * H
    NP = len(DILATIONS)
    with ExitStack() as ctx:
        def sb(name, shape, dt=F32):
            return ctx.enter_context(nc.sbuf_tensor(name, shape, dt))

        qk = sb("qk_d", [BH, 2, HD])
        qk_w = sb("qk_w_d", [BH, 2, HD])
        v_new = sb("v_new", [BH, HD])
        g_t = sb("g_d", [BH, HD])
        z_t = sb("z_d", [BH, HD])
        norm_h = sb("norm_h", [BH, HD])
        col = sb("col_d", [BH, 4])
        window = sb("window", [BH, TAPS, CONV // H])
        taps = sb("taps", [BH, TAPS, CONV // H])
        conv_bias = sb("conv_bias_d", [BH, CONV // H])
        ident = sb("ident_d", [P, P])
        pick_sb = sb("pick_sb", [BH, 4])
        same_sb = sb("same_sb", [BH, BH])
        seq_sb = sb("seq_sb", [NB, BH])
        near_sb = sb("near_sb", [BUCKETS, NP * P + 1])
        rel_rep = sb("rel_rep", [BUCKETS, NB, H])
        sums = sb("sums_d", [BH, 2])
        rs = sb("rs_d", [BH, 2])
        half = sb("half_d", [BH, 2])
        prod = sb("prod_d", [BH, HD])
        s0 = sb("s0", [BH, 1])
        q_all = sb("q_all", [P, 2, D])
        kt = sb("kt_d", [P, 2, NP, D])
        vt = sb("vt_d", [P, V_BUFS, NP, D])
        S = sb("S_d", [P, NP, BH])
        biased = sb("biased", [BH, NP * P + 1])
        prob = sb("prob_d", [BH, NP, P])
        probT = sb("probT", [P, NP, NB, BH])
        head_sb = sb("head_sb", [BH, H])
        blocks = sb("blocks", [BH, H, HD])
        top = sb("top_d", [BH, 4])
        p0 = sb("p0_d", [BH, 1])
        den = sb("den_d", [BH, 2])
        att = sb("att_d", [BH, HD])
        half_a = sb("half_a", [BH, HD])
        raw_d, abs_d, one_d, ln_d, tiny_d, rate_d = (sb(f"soft{i}", [BH, 1]) for i in range(6))
        scal = sb("scal_d", [BH, 3])
        state = sb("state_d", [BH, HD, NST])
        outer = sb("outer_d", [BH, HD, NST])
        bc4 = sb("bc4", [NB, 4 * NST])
        bc = sb("bc_d", [BH, 2, NST])
        bc_half = sb("bc_half", [BH, 2, NST])
        x_h = sb("x_h", [BH, HD])
        xdt = sb("xdt_d", [BH, HD])
        y_h = sb("y_h", [BH, HD])
        us = sb("us_d", [BH, 3])
        ps = lambda name, shape: ctx.enter_context(nc.psum_tensor(name, shape, F32))
        near_ps = ps("near_ps", [BH, 512])
        turn_ps = ps("turn_ps", [P, 512])
        back_ps = ps("back_ps", [P, 512])
        pv_ps = ps("pv_ps", [BH, D])
        bc_ps = ps("bc_ps", [BH, 512])
        rms_ps = ps("rms_ps", [BH, 512])
        sem = lambda n: nc.alloc_semaphore("d_" + n)
        loaded, xc_in, state_in = sem("loaded"), sem("xc_in"), sem("state_in")
        half_set, squared, meaned, rooted, qk_ready = sem("half_set"), sem("squared"), sem("meaned"), sem("rooted"), sem("qk_ready")
        q_stored, xc_stored, stored = sem("q_stored"), sem("xc_stored"), sem("stored")
        conv_sum, conv_act = sem("conv_sum"), sem("conv_act")
        silu = sem("silu")
        dv = sem("vector_order")
        k_in, q_in = ([sem(f"{n}{b}") for b in range(2)] for n in ("k_in", "q_in"))
        v_in = [sem(f"v_in{b}") for b in range(V_BUFS)]
        k_used = sem("k_used")
        v_used = sem("v_used")
        near_ready, turned, bc_ready = sem("near_ready"), sem("turned"), sem("bc_ready")
        near_out = sem("near_out")
        top_ready, exped, p0_ready, backed, prob_out, zeroed = (
            sem("top_ready"), sem("exped"), sem("p0_ready"), sem("backed"), sem("prob_out"), sem("zeroed"))
        also_loaded = sem("also_loaded")
        a_exp, abs_ready, e_ready, w_ready, ln_ready, rate_ready, decay_ready = (
            sem("a_exp"), sem("abs_ready"), sem("e_ready"), sem("w_ready"), sem("ln_ready"), sem("rate_ready"), sem("decay_ready"))
        xb_ready, outer_ready, hc_ready = sem("xb_ready"), sem("outer_ready"), sem("hc_ready")
        state_ready, u_ready, u_sq, u_sum, u_mean, u_root, u_norm, att_ready = (
            sem("state_ready"), sem("u_ready"), sem("u_sq"), sem("u_sum"), sem("u_mean"), sem("u_root"), sem("u_norm"), sem("att_ready"))
        block = ctx.enter_context(nc.Block())

        proj = scr["proj_s"]
        CW = CONV // H
        N_LOADS = 5 + 2 + 4 + 5
        N_ALSO = 2 * TAPS + 4

        def pairs(vector, width):
            return bass.AP(tensor=vector.tensor, offset=vector.offset, ap=[[0, NB], [width, H], [1, width]])

        def load_cache(eng, out, src, n, b, signal):
            for p, d in enumerate(DILATIONS):
                row = src[bass.ds(n, 1), WIN - P * d, :]
                eng.dma_start(out[:, b, p, :], bass.AP(tensor=row.tensor, offset=row.offset, ap=[[d * D, P], [1, D]])).then_inc(signal[b], 16)

        def part_of(first, width=HD):
            return bass.AP(tensor=proj.tensor, offset=first, ap=[[NPROJ, NB], [width, H], [1, width]])

        @block.sync
        def _(sp):
            def load(out, src):
                sp.dma_start(out, src).then_inc(loaded, 16)

            def load_q(j, b):
                row = scr["q_s"][bass.ds((2 * j + b) * H, H), :]
                sp.dma_start(q_all[:, b, :], bass.AP(tensor=row.tensor, offset=row.offset, ap=[[0, P], [1, D]])).then_inc(q_in[b], 16)

            load(qk[:, 0, :], part_of(Q0))
            load(qk[:, 1, :], part_of(K0))
            load(qk_w[:, 0, :], rows_of(io["q_norm_w"], BH))
            load(qk_w[:, 1, :], rows_of(io["k_norm_w"], BH))
            load(v_new[:, :], part_of(V0))
            load(g_t[:, :], part_of(G0))
            load(z_t[:, :], part_of(Z0))
            load(col[:, 0:1], part_of(DT0, 1))
            for i, name in enumerate(("dt_bias", "a_log", "d_skip")):
                load(col[:, 1 + i:2 + i], pairs(io[name], 1))
            load(ident[:, :], io["ident"])
            load(pick_sb[:, :], io["pick"])
            load(head_sb[:, :], io["of_head"])
            load(near_sb[:, :], io["near"])
            load(rel_rep[:, :, :], bass.AP(tensor=io["rel_bias"].tensor, offset=0, ap=[[H, BUCKETS], [0, NB], [1, H]]))
            sp.wait_ge(qk_ready, 2)
            sp.dma_start(scr["q_s"], qk[:, 0, :]).then_inc(q_stored, 16)
            sp.dma_start(io["ks_out"], qk[:, 1, :]).then_inc(stored, 16)
            sp.dma_start(io["vs_out"], v_new[:, :]).then_inc(stored, 16)
            sp.wait_ge(q_stored, 16)
            for b in range(2):
                load_q(0, b)
                load_cache(sp, kt, io["cache_k"], b, b, k_in)
            sp.wait_ge(conv_act, 1)
            sp.dma_start(bass.AP(tensor=scr["xc_s"].tensor, offset=0, ap=[[CONV, NB], [CW, H], [1, CW]]), taps[:, 0, :]).then_inc(xc_stored, 16)
            sp.wait_ge(xc_stored, 16)
            sp.dma_start(x_h[:, :], bass.AP(tensor=scr["xc_s"].tensor, offset=0, ap=[[CONV, NB], [HD, H], [1, HD]])).then_inc(xc_in, 16)
            sp.dma_start(bc4[:, :], scr["xc_s"][:, D:CONV]).then_inc(xc_in, 16)
            sp.dma_start(state[:, :, :], io["state_ssm"].rearrange("a (p n) -> a p n", n=NST)).then_inc(state_in, 16)
            sp.dma_start(io["conv_s"][:, 0:TAPS - 2, :], io["state_conv"][:, 1:TAPS - 1, :]).then_inc(stored, 16)
            sp.dma_start(io["conv_s"][:, TAPS - 2, :], proj[:, C0:DT0]).then_inc(stored, 16)
            with sp.Fori(1, NB // 2) as j:
                for b in range(2):
                    sp.wait_ge(k_used, 2 * j + b - 1)
                    load_q(j, b)
                    load_cache(sp, kt, io["cache_k"], 2 * j + b, b, k_in)
            sp.wait_ge(state_ready, 1)
            sp.dma_start(io["ssm_s"].rearrange("a (p n) -> a p n", n=NST), state[:, :, :]).then_inc(stored, 16)
            mixed = scr["mixed_s"]
            sp.wait_ge(u_norm, 1)
            sp.dma_start(bass.AP(tensor=mixed.tensor, offset=D, ap=[[2 * D, NB], [HD, H], [1, HD]]), y_h[:, :]).then_inc(stored, 16)
            sp.wait_ge(att_ready, 1)
            sp.dma_start(bass.AP(tensor=mixed.tensor, offset=0, ap=[[2 * D, NB], [HD, H], [1, HD]]), att[:, :]).then_inc(stored, 16)
            sp.wait_ge(stored, 16 * 7)

        @block.scalar
        def _(act):
            def load(out, src):
                act.dma_start(out, src).then_inc(also_loaded, 16)

            for i in range(TAPS):
                if i < TAPS - 1:
                    src = bass.AP(tensor=io["state_conv"].tensor, offset=i * CONV, ap=[[(TAPS - 1) * CONV, NB], [CW, H], [1, CW]])
                else:
                    src = part_of(C0, CW)
                load(window[:, i, :], src)
                load(taps[:, i, :], pairs(io["conv_w"][i, :], CW))
            load(conv_bias[:, :], pairs(io["conv_b"], CW))
            load(norm_h[:, :], pairs(io["ssd_norm_w"], HD))
            load(same_sb[:, :], io["same_seq"])
            load(seq_sb[:, :], io["of_seq"])
            act.wait_ge(loaded, 16 * N_LOADS)
            for i in range(2):
                act.activation(outer[:, i, 0:HD], qk[:, i, :], ACTF.Square, accum_out=sums[:, i:i + 1]).then_inc(squared, 1)
            act.activation(rate_d[:, :], col[:, 2:3], ACTF.Exp).then_inc(a_exp, 1)
            act.wait_ge(abs_ready, 1)
            act.activation(abs_d[:, :], abs_d[:, :], ACTF.Exp, scale=-1.0).then_inc(e_ready, 1)
            act.wait_ge(w_ready, 1)
            act.activation(ln_d[:, :], one_d[:, :], ACTF.Ln).then_inc(ln_ready, 1)
            act.wait_ge(rate_ready, 1)
            act.activation(scal[:, 2:3], scal[:, 1:2], ACTF.Exp).then_inc(decay_ready, 1)
            act.wait_ge(conv_sum, 1)
            act.activation(taps[:, 0, :], window[:, 0, :], ACTF.Silu).then_inc(conv_act, 1)
            act.activation(g_t[:, :], g_t[:, :], ACTF.Silu).then_inc(silu, 1)
            act.activation(z_t[:, :], z_t[:, :], ACTF.Silu).then_inc(silu, 1)
            act.wait_ge(u_ready, 1)
            act.activation(xdt[:, :], y_h[:, :], ACTF.Square, accum_out=us[:, 0:1]).then_inc(u_sq, 1)
            act.wait_ge(near_ready, 1)
            act.copy(biased[:, :], near_ps[:, 0:NP * P + 1]).then_inc(near_out, 1)
            act.wait_ge(top_ready, 1)
            act.activation(prob[:, :, :], biased[:, 0:NP * P].rearrange("a (d j) -> a d j", j=P), ACTF.Exp, bias=top[:, 2:3],
                           accum_out=den[:, 0:1]).then_inc(exped, 1)
            act.activation(p0[:, :], s0[:, :], ACTF.Exp, bias=top[:, 2:3]).then_inc(p0_ready, 1)
            act.wait_ge(backed, 1)
            act.wait_ge(zeroed, 1)
            own_columns = with_axes(probT[:, 0, 0, 0:1], [[NB * BH, NP], [BH + H, NB], [1, H]])
            act.copy(own_columns, back_ps[:, 0:NP * P].rearrange("j (d s h) -> j d s h", s=NB, h=H)).then_inc(prob_out, 1)

        @block.gpsimd
        def _(pool):
            pool.memset(half[:, :], -0.5).then_inc(half_set, 1)
            pool.wait_ge(half_set, 1)
            pool.memset(probT[:, :, :, :], 0.0).then_inc(zeroed, 1)
            pool.wait_ge(zeroed, 1)
            pool.wait_ge(meaned, 1)
            pool.tensor_tensor(rs[:, :], sums[:, :], half[:, :], ALU.pow).then_inc(rooted, 1)
            pool.wait_ge(rooted, 1)
            pool.wait_ge(xb_ready, 1)
            pool.tensor_tensor(outer[:, :, :], spread(xdt[:, :], NST), repeat(bc[:, 0, :], HD), ALU.mult).then_inc(outer_ready, 1)
            pool.wait_ge(outer_ready, 1)
            for n in range(V_BUFS):
                load_cache(pool, vt, io["cache_v"], n, n, v_in)
            pool.wait_ge(state_ready, 1)
            pool.tensor_tensor(outer[:, :, :], state[:, :, :], repeat(bc[:, 1, :], HD), ALU.mult).then_inc(hc_ready, 1)
            pool.wait_ge(hc_ready, 1)
            pool.wait_ge(u_mean, 1)
            pool.tensor_tensor(us[:, 2:3], us[:, 1:2], half[:, 0:1], ALU.pow).then_inc(u_root, 1)
            for n in range(V_BUFS, NB):
                pool.wait_ge(v_used, n - V_BUFS + 1)
                load_cache(pool, vt, io["cache_v"], n, n % V_BUFS, v_in)

        @block.vector
        def _(dve):
            own = Chain(dve, dv)
            dve.wait_ge(loaded, 16 * N_LOADS)
            dve.wait_ge(squared, 2)
            dve.tensor_scalar(sums[:, :], sums[:, :], 1.0 / HD, EPS, ALU.mult, ALU.add).then_inc(meaned, 1)
            dve.wait_ge(rooted, 1)
            own(dve.tensor_scalar(rs[:, 0:1], rs[:, 0:1], HD ** -0.5, None, ALU.mult))
            for i in range(2):
                dve.scalar_tensor_tensor(out=qk[:, i, :], in0=qk[:, i, :], scalar=rs[:, i:i + 1], in1=qk_w[:, i, :],
                                         op0=ALU.mult, op1=ALU.mult).then_inc(qk_ready, 1)
            dve.wait_ge(also_loaded, 16 * N_ALSO)
            own(dve.tensor_tensor(window[:, :, :], window[:, :, :], taps[:, :, :], ALU.mult))
            own(dve.tensor_tensor(window[:, 0:2, :], window[:, 0:2, :], window[:, 2:4, :], ALU.add))
            own(dve.tensor_tensor(window[:, 0, :], window[:, 0, :], window[:, 1, :], ALU.add))
            dve.tensor_tensor(window[:, 0, :], window[:, 0, :], conv_bias[:, :], ALU.add).then_inc(conv_sum, 1)
            own(dve.tensor_tensor(raw_d[:, :], col[:, 0:1], col[:, 1:2], ALU.add))
            dve.scalar_tensor_tensor(out=abs_d[:, :], in0=raw_d[:, :], scalar=-1.0, in1=raw_d[:, :],
                                     op0=ALU.mult, op1=ALU.max).then_inc(abs_ready, 1)
            dve.wait_ge(e_ready, 1)
            dve.tensor_scalar(one_d[:, :], abs_d[:, :], 1.0, None, ALU.add).then_inc(w_ready, 1)
            dve.wait_ge(ln_ready, 1)
            own(dve.tensor_tensor(ln_d[:, :], ln_d[:, :], abs_d[:, :], ALU.mult))
            own(dve.tensor_scalar(one_d[:, :], one_d[:, :], -1.0, None, ALU.add))
            own(dve.scalar_tensor_tensor(out=tiny_d[:, :], in0=one_d[:, :], scalar=0.0, in1=abs_d[:, :],
                                         op0=ALU.is_equal, op1=ALU.mult))
            own(dve.tensor_scalar(one_d[:, :], one_d[:, :], 1e-30, None, ALU.max))
            own(dve.reciprocal(one_d[:, :], one_d[:, :]))
            own(dve.tensor_tensor(ln_d[:, :], ln_d[:, :], one_d[:, :], ALU.mult))
            own(dve.tensor_tensor(ln_d[:, :], ln_d[:, :], tiny_d[:, :], ALU.add))
            own(dve.scalar_tensor_tensor(out=scal[:, 0:1], in0=raw_d[:, :], scalar=0.0, in1=ln_d[:, :],
                                         op0=ALU.max, op1=ALU.add))
            dve.wait_ge(a_exp, 1)
            dve.scalar_tensor_tensor(out=scal[:, 1:2], in0=rate_d[:, :], scalar=-1.0, in1=scal[:, 0:1],
                                     op0=ALU.mult, op1=ALU.mult).then_inc(rate_ready, 1)
            dve.wait_ge(qk_ready, 2)
            own(dve.tensor_tensor(prod[:, :], qk[:, 0, :], qk[:, 1, :], ALU.mult))
            own(dve.tensor_reduce(s0[:, :], prod[:, :], axis=AX.X, op=ALU.add))

            def cached(seqs):
                for n in seqs:
                    b = n % 2
                    dve.wait_ge(k_in[b], 16 * NP * (n // 2 + 1))
                    dve.wait_ge(q_in[b], 16 * (n // 2 + 1))
                    own(dve.tensor_tensor(kt[:, b, :, :], kt[:, b, :, :], repeat(q_all[:, b, :], NP), ALU.mult))
                    dve.tensor_reduce(S[:, :, n * H:(n + 1) * H], kt[:, b, :, :].rearrange("p d (h e) -> p d h e", e=HD),
                                      axis=AX.X, op=ALU.add).then_inc(k_used, 1)

            cached((0, 1))

            dve.wait_ge(bc_ready, 1)
            bcg = bc_ps[:, :].rearrange("a (i g n) -> a i g n", i=2, g=2)
            own(dve.tensor_scalar(bc_half[:, :, :], bcg[:, :, 1, :], pick_sb[:, 3:4], None, ALU.mult))
            own(dve.scalar_tensor_tensor(out=bc[:, :, :], in0=bcg[:, :, 0, :], scalar=pick_sb[:, 2:3], in1=bc_half[:, :, :],
                                         op0=ALU.mult, op1=ALU.add))
            dve.wait_ge(xc_in, 32)
            dve.tensor_scalar(xdt[:, :], x_h[:, :], scal[:, 0:1], None, ALU.mult).then_inc(xb_ready, 1)
            cached((2, 3, 4))
            dve.wait_ge(outer_ready, 1)
            dve.wait_ge(decay_ready, 1)
            dve.wait_ge(state_in, 16)
            dve.scalar_tensor_tensor(out=state[:, :, :], in0=state[:, :, :], scalar=scal[:, 2:3], in1=outer[:, :, :],
                                     op0=ALU.mult, op1=ALU.add).then_inc(state_ready, 1)
            cached((5, 6))
            dve.wait_ge(hc_ready, 1)
            own(dve.tensor_reduce(y_h[:, :], outer[:, :, :], axis=AX.X, op=ALU.add))
            own(dve.scalar_tensor_tensor(out=y_h[:, :], in0=x_h[:, :], scalar=col[:, 3:4], in1=y_h[:, :],
                                         op0=ALU.mult, op1=ALU.add))
            dve.wait_ge(silu, 2)
            dve.tensor_tensor(y_h[:, :], y_h[:, :], z_t[:, :], ALU.mult).then_inc(u_ready, 1)
            dve.wait_ge(u_sum, 1)
            dve.tensor_scalar(us[:, 1:2], rms_ps[:, 0:1], 1.0 / D, EPS, ALU.mult, ALU.add).then_inc(u_mean, 1)

            cached((7,))

            dve.wait_ge(u_root, 1)
            dve.scalar_tensor_tensor(out=y_h[:, :], in0=y_h[:, :], scalar=us[:, 2:3], in1=norm_h[:, :],
                                     op0=ALU.mult, op1=ALU.mult).then_inc(u_norm, 1)

            dve.wait_ge(turned, 1)
            dve.wait_ge(near_out, 1)
            own(dve.tensor_tensor(biased[:, 0:NP * P], turn_ps[:, 0:NP * P], biased[:, 0:NP * P], ALU.add))
            own(dve.tensor_tensor(s0[:, :], s0[:, :], biased[:, NP * P:], ALU.add))
            own(dve.tensor_reduce(top[:, 0:1], biased[:, 0:NP * P], axis=AX.X, op=ALU.max))
            own(dve.tensor_tensor(top[:, 1:2], top[:, 0:1], s0[:, :], ALU.max))
            dve.tensor_scalar(top[:, 2:3], top[:, 1:2], -1.0, None, ALU.mult).then_inc(top_ready, 1)

            dve.wait_ge(p0_ready, 1)
            dve.wait_ge(exped, 1)
            own(dve.tensor_scalar(p0[:, :], p0[:, :], float(NP), None, ALU.mult))
            own(dve.tensor_tensor(den[:, 0:1], den[:, 0:1], p0[:, :], ALU.add))
            own(dve.reciprocal(den[:, 1:2], den[:, 0:1]))
            own(dve.tensor_scalar(half_a[:, :], v_new[:, :], p0[:, 0:1], None, ALU.mult))
            dve.wait_ge(v_used, NB)
            own(dve.tensor_tensor(blocks[:, :, :], pv_ps[:, :].rearrange("a (h e) -> a h e", e=HD), spread(head_sb[:, :], HD), ALU.mult))
            own(dve.tensor_reduce(prod[:, :], blocks[:, :, :].rearrange("a h e -> a e h"), axis=AX.X, op=ALU.add))
            own(dve.tensor_tensor(half_a[:, :], half_a[:, :], prod[:, :], ALU.add))
            dve.scalar_tensor_tensor(out=att[:, :], in0=half_a[:, :], scalar=den[:, 1:2], in1=g_t[:, :],
                                     op0=ALU.mult, op1=ALU.mult).then_inc(att_ready, 1)

        @block.tensor
        def _(pe):
            pe.wait_ge(loaded, 16 * N_LOADS)
            pe.matmul(near_ps[:, 0:NP * P + 1], rel_rep[:, :, :].rearrange("b s h -> b (s h)"), near_sb[:, :], start=True, stop=True).then_inc(near_ready, 1)
            pe.wait_ge(also_loaded, 16 * N_ALSO)
            pe.wait_ge(xc_in, 32)
            pe.matmul(bc_ps[:, :], seq_sb[:, :], bc4[:, :], start=True, stop=True).then_inc(bc_ready, 1)
            pe.wait_ge(u_sq, 1)
            pe.matmul(rms_ps[:, 0:1], same_sb[:, :], us[:, 0:1], start=True, stop=True).then_inc(u_sum, 1)
            pe.wait_ge(k_used, NB)
            for p in range(NP):
                last = pe.transpose(turn_ps[:, p * P:(p + 1) * P], S[:, p, :], ident[:, :])
            last.then_inc(turned, 1)
            pe.wait_ge(exped, 1)
            for p in range(NP):
                last = pe.transpose(back_ps[:, p * P:(p + 1) * P], prob[:, p, :], ident[:, :])
            last.then_inc(backed, 1)
            pe.wait_ge(prob_out, 1)
            for n in range(NB):
                pe.wait_ge(v_in[n % V_BUFS], 16 * NP * (n // V_BUFS + 1))
                for p in range(NP):
                    for half_cols in (slice(0, 512), slice(512, D)):
                        last = pe.matmul(pv_ps[:, half_cols], probT[:, p, n, :], vt[:, n % V_BUFS, p, half_cols],
                                         start=n == 0 and p == 0, stop=n == NB - 1 and p == NP - 1)
                last.then_inc(v_used, 1)


def output(nc, io, scr):
    MK = 2 * D // P
    SLABS = 3
    with ExitStack() as ctx:
        def sb(name, shape, dt=F32):
            return ctx.enter_context(nc.sbuf_tensor(name, shape, dt))

        w_hi = sb("wo_hi", [P, MK, D], F32R)
        w_lo = sb("wo_lo", [P, MK, D], F32R)
        slab = sb("slab", [P, SLABS, D])
        m_raw = sb("m_raw", [P, 2, MK, P])
        m_hi = sb("m_hi", [P, 2, MK, P], F32R)
        m_lo = sb("m_lo", [P, 2, MK, P], F32R)
        x_t = sb("x_o", [P, 2, D])
        x_s = slab[0:NB, 0, :]
        s_hi = sb("s_hi", [P, MK, NB], F32R)
        s_lo = sb("s_lo", [P, MK, NB], F32R)
        ident = sb("ident_o", [NB, NB])
        acc = [ctx.enter_context(nc.psum_tensor(f"acc{b}", [P, D], F32)) for b in range(2)]
        acc_s = ctx.enter_context(nc.psum_tensor("acc_s", [P, D], F32))
        ms_ps = ctx.enter_context(nc.psum_tensor("ms_ps", [P, MK, NB], F32))
        sem = lambda n: nc.alloc_semaphore("o_" + n)
        w_in_ = [sem(f"w_in{b}") for b in range(SLABS)]
        w_high, w_split = sem("w_high"), sem("w_split")
        m_in, x_in, y_stored = ([sem(f"{n}{b}") for b in range(2)] for n in ("m_in", "x_in", "y_stored"))
        m_high, m_split, done, added = sem("m_high"), sem("m_split"), sem("done"), sem("added")
        s_in, s_turned, s_high, s_split, xs_in, s_done, s_added, s_stored = (
            sem("s_in"), sem("s_turned"), sem("s_high"), sem("s_split"), sem("xs_in"), sem("s_done"), sem("s_added"), sem("s_stored"))
        block = ctx.enter_context(nc.Block())
        mixed_s = x_t[0:NB, :, :].rearrange("p a n -> p (a n)")

        @block.sync
        def _(sp):
            def load_w(k):
                if k >= SLABS:
                    sp.wait_ge(w_split, k - SLABS + 1)
                sp.dma_start(slab[:, k % SLABS, :], io["w_out"][k * P:(k + 1) * P, :]).then_inc(w_in_[k % SLABS], 16)

            def load_m(t, b):
                sp.dma_start(m_raw[:, b, :, :], scr["mT"].rearrange("(m p) t -> p m t", p=P)[:, :, bass.ds(t * P, P)]).then_inc(m_in[b], 16)

            def load_x(t, b):
                sp.dma_start(x_t[:, b, :], io["x_all"][bass.ds(t * P, P), :]).then_inc(x_in[b], 16)

            def store(t, b):
                sp.wait_ge(added, t + 1)
                sp.dma_start(io["y_out"][bass.ds(t * P, P), :], x_t[:, b, :]).then_inc(y_stored[b], 16)

            load_w(0)
            load_m(0, 0)
            load_m(1, 1)
            sp.dma_start(ident[:, :], io["ident"][0:NB, 0:NB]).then_inc(s_in, 16)
            sp.dma_start(mixed_s, scr["mixed_s"]).then_inc(s_in, 16)
            for k in range(1, MK):
                load_w(k)
            sp.wait_ge(s_turned, 1)
            load_x(0, 0)
            load_x(1, 1)
            sp.wait_ge(w_split, MK)
            sp.dma_start(x_s, io["x_all"][SEQ:TOK, :]).then_inc(xs_in, 16)
            with sp.Fori(0, TILES // 2 - 1) as j:
                for b in range(2):
                    sp.wait_ge(m_split, 2 * j + b + 1)
                    load_m(2 * j + b + 2, b)
                for b in range(2):
                    store(2 * j + b, b)
                    sp.wait_ge(y_stored[b], 16 * (j + 1))
                    load_x(2 * j + b + 2, b)
            sp.wait_ge(s_added, 1)
            sp.dma_start(io["y_out"][SEQ:TOK, :], x_s).then_inc(s_stored, 16)
            store(TILES - 2, 0)
            store(TILES - 1, 1)
            sp.wait_ge(s_stored, 16)
            for b in range(2):
                sp.wait_ge(y_stored[b], 16 * (TILES // 2))

        @block.scalar
        def _(act):
            def high(t, b, j):
                act.wait_ge(m_in[b], 16 * (j + 1))
                if not isinstance(t, int) or t >= 2:
                    act.wait_ge(done, t - 1)
                act.copy(m_hi[:, b, :, :], m_raw[:, b, :, :]).then_inc(m_high, 1)

            def high_w(k):
                act.wait_ge(w_in_[k % SLABS], 16 * (k // SLABS + 1))
                act.copy(w_hi[:, k, :], slab[:, k % SLABS, :]).then_inc(w_high, 1)

            high_w(0)
            for b in range(2):
                high(b, b, 0)
            for k in range(1, MK):
                high_w(k)
            act.wait_ge(s_turned, 1)
            act.copy(s_hi[:, :, :], ms_ps[:, :, :]).then_inc(s_high, 1)
            with act.Fori(1, TILES // 2) as j:
                for b in range(2):
                    high(2 * j + b, b, j)

        @block.vector
        def _(dve):
            def low(t, b):
                dve.wait_ge(m_high, t + 1)
                dve.tensor_tensor(m_lo[:, b, :, :], m_raw[:, b, :, :], m_hi[:, b, :, :].bitcast(F32), ALU.subtract).then_inc(m_split, 1)

            def low_w(k):
                dve.wait_ge(w_high, k + 1)
                dve.tensor_tensor(w_lo[:, k, :], slab[:, k % SLABS, :], w_hi[:, k, :].bitcast(F32), ALU.subtract).then_inc(w_split, 1)

            def add(t, b, j):
                dve.wait_ge(done, t + 1)
                dve.wait_ge(x_in[b], 16 * (j + 1))
                dve.tensor_tensor(x_t[:, b, :], acc[b][:, :], x_t[:, b, :], ALU.add).then_inc(added, 1)

            low_w(0)
            for b in range(2):
                low(b, b)
            for k in range(1, MK):
                low_w(k)
            dve.wait_ge(s_high, 1)
            dve.tensor_tensor(s_lo[:, :, :], ms_ps[:, :, :], s_hi[:, :, :].bitcast(F32), ALU.subtract).then_inc(s_split, 1)

            with dve.Fori(0, TILES // 2 - 1) as j:
                for b in range(2):
                    add(2 * j + b, b, j)
                    low(2 * j + b + 2, b)
            dve.wait_ge(s_done, 1)
            dve.wait_ge(xs_in, 16)
            dve.tensor_tensor(x_s, acc_s[0:NB, :], x_s, ALU.add).then_inc(s_added, 1)
            for b in range(2):
                add(TILES - 2 + b, b, TILES // 2 - 1)

        @block.tensor
        def _(pe):
            def products(out, hi, lo, k, n):
                cols = slice(n * 512, (n + 1) * 512)
                pe.matmul(out[:, cols], hi, w_hi[:, k, cols], start=k == 0, stop=False)
                pe.matmul(out[:, cols], hi, w_lo[:, k, cols], start=False, stop=False)
                return pe.matmul(out[:, cols], lo, w_hi[:, k, cols], start=False, stop=k == MK - 1)

            def tile(t, b):
                pe.wait_ge(m_split, t + 1)
                pe.wait_ge(added, t - 1)
                for n in range(D // 512):
                    for k in range(MK):
                        last = products(acc[b], m_hi[:, b, k, :], m_lo[:, b, k, :], k, n)
                last.then_inc(done, 1)

            pe.wait_ge(s_in, 32)
            for k in range(MK):
                last = pe.transpose(ms_ps[:, k, :], mixed_s[:, k * P:(k + 1) * P], ident[:, :])
            last.then_inc(s_turned, 1)
            pe.wait_ge(m_split, 2)
            for k in range(MK):
                pe.wait_ge(w_split, k + 1)
                for b in range(2):
                    for n in range(D // 512):
                        last = products(acc[b], m_hi[:, b, k, :], m_lo[:, b, k, :], k, n)
                    if k == MK - 1:
                        last.then_inc(done, 1)
            pe.wait_ge(s_split, 1)
            for n in range(D // 512):
                for k in range(MK):
                    last = products(acc_s[0:NB, :], s_hi[:, k, :], s_lo[:, k, :], k, n)
            last.then_inc(s_done, 1)
            with pe.Fori(1, TILES // 2) as j:
                for b in range(2):
                    tile(2 * j + b, b)


def build(nc, io):
    scr = {name: nc.dram_tensor(name, shape, F32).ap() for name, shape in SCRATCH.items()}
    for stage in STAGES:
        with nc.cleanup_on_exit():
            stage(nc, io, scr)
            nc.all_engine_barrier()
    return scr


SCRATCH = {
    "q": (SEQ, D),
    "z": (SEQ, D),
    "gT": (D, SEQ),
    "xcT": (CONV, SEQ),
    "dtT": (H, SEQ),
    "proj_s": (NB, NPROJ),
    "rows": (H, 3 * SHIFTS),
    "bias": (H * P, BIAS_W),
    "tops": (3, SEQ),
    "ntop": (1, SEQ),
    "den": (2, SEQ),
    "cum": (H, SEQ),
    "q_s": (NB * H, HD),
    "xc_s": (NB, CONV),
    "mixed_s": (NB, 2 * D),
    "mT": (2 * D, SEQ),
}
STAGES = [project, attend, scan, decode, output]
OUTPUTS = {
    "y_out": (TOK, D),
    "k_out": (SEQ, D),
    "v_out": (SEQ, D),
    "conv_p": (CONV, TAPS - 1),
    "ssm_p": (P, D),
    "ks_out": (NB * H, HD),
    "vs_out": (NB * H, HD),
    "conv_s": (NB, TAPS - 1, CONV),
    "ssm_s": (NB * H, HD * NST),
}


def t5_bucket(dist):
    exact = BUCKETS // 2
    far = np.maximum(dist, 1).astype(np.float32)
    large = exact + (np.log(far / np.float32(exact)) / np.float32(math.log(WIN / exact))
                     * np.float32(BUCKETS - exact)).astype(np.int32)
    return np.where(dist < exact, dist, np.minimum(large, BUCKETS - 1))


def constants():
    dist = 2 * P - 1 - np.arange(SHIFTS)
    inside = (dist >= 0) & (dist <= P)
    onehot = np.zeros((BUCKETS + 1, 3, SHIFTS), np.float32)
    for p, d in enumerate(DILATIONS):
        for u in np.flatnonzero(inside):
            onehot[t5_bucket(dist[u] * d), p, u] = 1.0
    onehot[BUCKETS, :, ~inside] = MASKED
    tri = np.triu(np.ones((P, P), np.float32))
    pair = np.arange(NB * H)
    pick = np.stack([pair % 2 == 0, pair % 2 == 1, pair % H < H // 2, pair % H >= H // 2], axis=1).astype(np.float32)
    same = (pair[:, None] // H == pair[None, :] // H).astype(np.float32)
    of_seq = (np.arange(NB)[:, None] == pair[None, :] // H).astype(np.float32)
    of_head = (pair[:, None] % H == np.arange(H)[None, :]).astype(np.float32)
    near = np.zeros((BUCKETS, len(DILATIONS) * P + 1), np.float32)
    for p, d in enumerate(DILATIONS):
        for j in range(P):
            near[t5_bucket((P - j) * d), p * P + j] = 1.0
    near[t5_bucket(0), -1] = 1.0
    return {"pick": pick, "same_seq": same, "of_seq": of_seq, "of_head": of_head, "near": near, "tri": tri, "ident": np.eye(P, dtype=np.float32), "onehot": onehot.reshape(BUCKETS + 1, 3 * SHIFTS)}


def laid_out(inputs):
    a = {k: np.asarray(v) for k, v in inputs.items()}
    w = a["w_in"][0]
    cuts = np.split(w, [D, 2 * D, 3 * D, 4 * D, 5 * D, 5 * D + CONV], axis=1)
    q, k, v, g, z, xbc, dt = cuts
    out = {
        "x_all": np.concatenate([a["x_prompt"][0], a["x_sample"][:, 0]], axis=0),
        "w_in": np.concatenate([q, k, z, v[:, :D - 2 * SLAB], g, xbc, dt, v[:, D - 2 * SLAB:]], axis=1),
        "norm_w": a["norm_w"][0], "q_norm_w": a["q_norm_w"][0], "k_norm_w": a["k_norm_w"][0],
        "conv_w_t": a["conv_w"][0].T, "conv_b": a["conv_b"][0],
        "conv_w": a["conv_w"][0],
        "cache_k": a["cache_win_k"][0].reshape(NB, WIN, D), "cache_v": a["cache_win_v"][0].reshape(NB, WIN, D),
        "state_conv": a["state_conv"][0], "state_ssm": a["state_ssm"][0].reshape(NB * H, HD * NST),
        "rel_bias": a["rel_bias"], "dt_bias": a["dt_bias"][0], "a_log": a["a_log"][0], "d_skip": a["d_skip"][0],
        "ssd_norm_w": a["ssd_norm_w"][0], "w_out": a["w_out"][0],
    }
    return {k: np.ascontiguousarray(v) for k, v in {**out, **constants()}.items()}


def kernel(**inputs):
    import concourse.bacc as bacc
    from concourse.bass_utils import run_bass_kernel_spmd

    nc = bacc.Bacc("TRN2", target_bir_lowering=False, num_devices=1)
    arrays = laid_out(inputs)
    io = {n: nc.dram_tensor(n, a.shape, mybir.dt.from_np(a.dtype), kind="ExternalInput").ap() for n, a in arrays.items()}
    io.update({n: nc.dram_tensor(n, s, F32, kind="ExternalOutput").ap() for n, s in OUTPUTS.items()})
    build(nc, io)
    r = run_bass_kernel_spmd(nc, [arrays], core_ids=[0]).results[0]
    y = r["y_out"]
    return (y[:SEQ].reshape(1, SEQ, D), y[SEQ:].reshape(NB, 1, D),
            r["k_out"].reshape(1, 1, SEQ, H, HD), r["v_out"].reshape(1, 1, SEQ, H, HD),
            np.ascontiguousarray(r["conv_p"].T).reshape(1, 1, TAPS - 1, CONV),
            np.ascontiguousarray(r["ssm_p"].reshape(NST, H, HD).transpose(1, 2, 0)).reshape(1, 1, H, HD, NST),
            r["ks_out"].reshape(1, NB, 1, H, HD), r["vs_out"].reshape(1, NB, 1, H, HD),
            r["conv_s"].reshape(1, NB, TAPS - 1, CONV), r["ssm_s"].reshape(1, NB, H, HD, NST))
```
